# Optimizing a Trainium2 kernel written in Bass

```python
import math
import jax, jax.numpy as jnp
from jax import lax
import numpy as np

D_MODEL = 1024
BATCH = 1
SEQ = 2048
DEPTH = 1
DEC_BATCH = 8
DEC_SEQ = 1
PAST_LEN = 16384
PAGE_SIZE = 128

D_A = D_MODEL // 2
D_B = D_MODEL // 2
D_MIX = D_A + D_B
N_POOL = 4
POOL_WINDOWS = (2, 4, 8, 16)
POOL_GC = D_A // N_POOL
POOL_BUF = max(POOL_WINDOWS) - 1
HEAD_DIM = 128
N_HEADS_B = D_B // HEAD_DIM
D_QKV = 3 * D_B
CONV_K = 4
GDN_CHUNK = 64
D_IN = 2 * D_A + D_QKV + D_B + 2 * N_HEADS_B
EPS = 1e-6

kernel_name = 'hybrid_pool_gdn_decoder_step'

def rms_norm(x, w):
    xf = x.astype(jnp.float32)
    y = xf * lax.rsqrt(jnp.mean(xf * xf, axis=-1, keepdims=True) + EPS)
    return (y * w.astype(jnp.float32)).astype(x.dtype)

def l2_normalize(x):
    return x * lax.rsqrt(jnp.sum(x * x, axis=-1, keepdims=True) + EPS)

def causal_conv(u, buf, w):
    T = u.shape[1]
    xx = jnp.concatenate([buf.astype(u.dtype), u], axis=1)
    out = sum(xx[:, j:j + T] * w[j] for j in range(CONV_K))
    return jax.nn.silu(out), xx[:, -(CONV_K - 1):]

def pool_mix(u, buf, start_pos, w_pool, scale):
    B, T, _ = u.shape
    xx = jnp.concatenate([buf.astype(u.dtype), u], axis=1)
    xf = xx.astype(jnp.float32)
    cs = jnp.concatenate([jnp.zeros((B, 1, D_A), jnp.float32), jnp.cumsum(xf, axis=1)], axis=1)
    pos = start_pos + jnp.arange(T)
    outs = []
    for gi, w in enumerate(POOL_WINDOWS):
        sl = slice(gi * POOL_GC, (gi + 1) * POOL_GC)
        win = cs[:, POOL_BUF + 1:POOL_BUF + 1 + T, sl] - cs[:, POOL_BUF + 1 - w:POOL_BUF + 1 - w + T, sl]
        cnt = jnp.minimum(pos + 1, w).astype(jnp.float32)
        outs.append(win / cnt[None, :, None])
    pooled = jnp.concatenate(outs, axis=-1) - u.astype(jnp.float32)
    pooled = pooled.reshape(B, T, N_POOL, POOL_GC)
    y = jnp.einsum('btgc,gcd->btgd', pooled, w_pool.astype(jnp.float32)).reshape(B, T, D_A)
    y = y * scale.astype(jnp.float32)
    return y.astype(u.dtype), xx[:, -POOL_BUF:]

def gdn_chunked(q, k, v, g, beta, S0):
    B, T, H, DK = q.shape
    DV = v.shape[-1]
    C = GDN_CHUNK
    n = -(-T // C)
    pad = n * C - T

    def to_chunks(a):
        a = jnp.pad(a, [(0, 0), (0, pad)] + [(0, 0)] * (a.ndim - 2))
        a = a.reshape((B, n, C) + a.shape[2:])
        return jnp.moveaxis(a, (1, 3), (0, 2))

    qc, kc, vc, gc, bc = (to_chunks(a) for a in (q, k, v, g, beta))
    gc = jnp.cumsum(gc, axis=-1)
    idx = jnp.arange(C)
    causal = idx[:, None] >= idx[None, :]
    strict = idx[:, None] > idx[None, :]
    decay = jnp.exp(jnp.where(causal, gc[..., :, None] - gc[..., None, :], -jnp.inf))
    kb = kc * bc[..., None]
    vb = vc * bc[..., None]
    Lm = jnp.where(strict, jnp.einsum('nbhid,nbhjd->nbhij', kb, kc) * decay, 0.0)
    A = Lm + jnp.eye(C, dtype=Lm.dtype)
    rhs = jnp.concatenate([vb, kb * jnp.exp(gc)[..., None]], axis=-1)
    sol = lax.linalg.triangular_solve(A, rhs, left_side=True, lower=True, unit_diagonal=True)
    uc, wc = sol[..., :DV], sol[..., DV:]
    qk = jnp.einsum('nbhid,nbhjd->nbhij', qc, kc) * decay
    qg = qc * jnp.exp(gc)[..., None]
    kg = kc * jnp.exp(gc[..., -1:] - gc)[..., None]
    g_last = jnp.exp(gc[..., -1])

    def step(S, xs):
        qg_i, kg_i, u_i, w_i, qk_i, gl_i = xs
        v_new = u_i - jnp.einsum('bhcd,bhde->bhce', w_i, S)
        o = jnp.einsum('bhcd,bhde->bhce', qg_i, S) + jnp.einsum('bhij,bhje->bhie', qk_i, v_new)
        S = S * gl_i[..., None, None] + jnp.einsum('bhcd,bhce->bhde', kg_i, v_new)
        return S, o

    S, o = lax.scan(step, S0, (qg, kg, uc, wc, qk, g_last))
    o = jnp.moveaxis(o, (0, 2), (1, 3)).reshape(B, n * C, H, DV)[:, :T]
    return o, S

def gdn_recurrent(q, k, v, g, beta, S0):
    xs = tuple(jnp.moveaxis(a, 1, 0) for a in (q, k, v, g, beta))

    def step(S, xt):
        q_t, k_t, v_t, g_t, b_t = xt
        S = S * jnp.exp(g_t)[..., None, None]
        kv = jnp.einsum('bhd,bhde->bhe', k_t, S)
        delta = (v_t - kv) * b_t[..., None]
        S = S + jnp.einsum('bhd,bhe->bhde', k_t, delta)
        o = jnp.einsum('bhd,bhde->bhe', q_t, S)
        return S, o

    S, o = lax.scan(step, S0, xs)
    return jnp.moveaxis(o, 0, 1), S

def mixer_layer(x, c, start_pos, pool_buf, conv_buf, S0, chunked,
                w_ada, b_ada, pre_norm_w, post_norm_w, w_in, conv_w, pool_w, pool_scale,
                a_log, dt_bias, o_norm_w, w_out):
    B, T, _ = x.shape
    mod = jax.nn.silu(c) @ w_ada + b_ada
    shift, scale, gate = jnp.split(mod, 3, axis=-1)
    h = rms_norm(x, pre_norm_w) * (1.0 + scale[:, None]) + shift[:, None]
    proj = h @ w_in
    cuts = np.cumsum([D_A, D_A, D_QKV, D_B, N_HEADS_B]).tolist()
    u_a, z_a, qkv, z_b, b_raw, a_raw = jnp.split(proj, cuts, axis=-1)

    y_a, new_pool = pool_mix(u_a, pool_buf, start_pos, pool_w, pool_scale)
    y_a = y_a * jax.nn.silu(z_a)

    qkv_c, new_conv = causal_conv(qkv, conv_buf, conv_w)
    qkv_c = qkv_c.astype(jnp.float32)
    q, k, v = (a.reshape(B, T, N_HEADS_B, HEAD_DIM) for a in jnp.split(qkv_c, 3, axis=-1))
    q = l2_normalize(q) * (HEAD_DIM ** -0.5)
    k = l2_normalize(k)
    beta = jax.nn.sigmoid(b_raw.astype(jnp.float32))
    g = -jnp.exp(a_log.astype(jnp.float32)) * jax.nn.softplus(a_raw.astype(jnp.float32) + dt_bias.astype(jnp.float32))
    S0f = S0.astype(jnp.float32)
    if chunked:
        o, S = gdn_chunked(q, k, v, g, beta, S0f)
    else:
        o, S = gdn_recurrent(q, k, v, g, beta, S0f)
    o = rms_norm(o, o_norm_w) * jax.nn.silu(z_b.astype(jnp.float32)).reshape(B, T, N_HEADS_B, HEAD_DIM)
    y_b = o.reshape(B, T, D_B).astype(x.dtype)

    y = jnp.concatenate([y_a, y_b], axis=-1) @ w_out
    x = x + gate[:, None] * rms_norm(y, post_norm_w)
    return x, new_pool, new_conv, S.astype(S0.dtype)

def setup_inputs(seed: int = 0) -> dict:
    key = jax.random.key(seed)
    ks = jax.random.split(key, 20)

    def nrm(k, shape, s):
        return jax.random.normal(k, shape, jnp.float32) * s

    dt = jnp.exp(jax.random.uniform(ks[16], (DEPTH, N_HEADS_B), jnp.float32, math.log(1e-3), math.log(1e-1)))
    return {
        'x_prompt': nrm(ks[0], (BATCH, SEQ, D_MODEL), 1.0),
        'x_sample': nrm(ks[1], (DEC_BATCH, DEC_SEQ, D_MODEL), 1.0),
        'c_prompt': nrm(ks[2], (BATCH, D_MODEL), 1.0),
        'c_sample': nrm(ks[3], (DEC_BATCH, D_MODEL), 1.0),
        'state_pool': nrm(ks[4], (DEPTH, DEC_BATCH, POOL_BUF, D_A), 1.0),
        'state_conv': nrm(ks[5], (DEPTH, DEC_BATCH, CONV_K - 1, D_QKV), 1.0),
        'state_ssm': nrm(ks[6], (DEPTH, DEC_BATCH, N_HEADS_B, HEAD_DIM, HEAD_DIM), 0.05),
        'w_ada': nrm(ks[7], (DEPTH, D_MODEL, 3 * D_MODEL), 0.1 * D_MODEL ** -0.5),
        'b_ada': nrm(ks[8], (DEPTH, 3 * D_MODEL), 0.01),
        'pre_norm_w': 1.0 + nrm(ks[9], (DEPTH, D_MODEL), 0.05),
        'post_norm_w': 1.0 + nrm(ks[10], (DEPTH, D_MODEL), 0.05),
        'w_in': nrm(ks[11], (DEPTH, D_MODEL, D_IN), D_MODEL ** -0.5),
        'conv_w': nrm(ks[12], (DEPTH, CONV_K, D_QKV), CONV_K ** -0.5),
        'pool_w': nrm(ks[13], (DEPTH, N_POOL, POOL_GC, POOL_GC), POOL_GC ** -0.5),
        'pool_scale': 1.0 + nrm(ks[14], (DEPTH, D_A), 0.05),
        'a_log': jnp.log(jax.random.uniform(ks[15], (DEPTH, N_HEADS_B), jnp.float32, 1.0, 16.0)),
        'dt_bias': dt + jnp.log(-jnp.expm1(-dt)),
        'o_norm_w': 1.0 + nrm(ks[17], (DEPTH, HEAD_DIM), 0.05),
        'w_out': nrm(ks[18], (DEPTH, D_MIX, D_MODEL), D_MIX ** -0.5),
    }

def reference(x_prompt, x_sample, c_prompt, c_sample, state_pool, state_conv, state_ssm,
              w_ada, b_ada, pre_norm_w, post_norm_w, w_in, conv_w, pool_w, pool_scale,
              a_log, dt_bias, o_norm_w, w_out):
    bp = x_prompt.shape[0]
    yp, ys = x_prompt, x_sample
    pp, cp, sp, ps, cs, ss = [], [], [], [], [], []
    for l in range(DEPTH):
        params = (w_ada[l], b_ada[l], pre_norm_w[l], post_norm_w[l], w_in[l], conv_w[l],
                  pool_w[l], pool_scale[l], a_log[l], dt_bias[l], o_norm_w[l], w_out[l])
        zero_pool = jnp.zeros((bp, POOL_BUF, D_A), x_prompt.dtype)
        zero_conv = jnp.zeros((bp, CONV_K - 1, D_QKV), x_prompt.dtype)
        zero_ssm = jnp.zeros((bp, N_HEADS_B, HEAD_DIM, HEAD_DIM), state_ssm.dtype)
        yp, a1, a2, a3 = mixer_layer(yp, c_prompt, 0, zero_pool, zero_conv, zero_ssm, True, *params)
        ys, b1, b2, b3 = mixer_layer(ys, c_sample, PAST_LEN, state_pool[l], state_conv[l], state_ssm[l], False, *params)
        pp.append(a1); cp.append(a2); sp.append(a3)
        ps.append(b1); cs.append(b2); ss.append(b3)
    return (yp, ys, jnp.stack(pp), jnp.stack(cp), jnp.stack(sp), jnp.stack(ps), jnp.stack(cs), jnp.stack(ss))


_drawn_inputs = setup_inputs


def setup_inputs(seed=0):
    import zlib

    import numpy as np

    out = dict(_drawn_inputs(seed))
    spreads = {}
    factors = {'post_norm_w': 8.0, 'pool_scale': 8.0, 'o_norm_w': 8.0}
    for name, (base, spread) in spreads.items():
        noise = np.random.default_rng([zlib.crc32(name.encode()), seed]).standard_normal(out[name].shape)
        drawn = base * np.exp(spread * noise) if base else spread * noise
        out[name] = __import__('jax').numpy.asarray(drawn.astype(out[name].dtype))
    for name, factor in factors.items():
        out[name] = (out[name] * factor).astype(out[name].dtype)
    return out
```

```python
from contextlib import ExitStack

import concourse.bass as bass
from concourse import mybir

F32 = mybir.dt.float32
F32R = mybir.dt.float32r
BF16 = mybir.dt.bfloat16
ALU = mybir.AluOpType
ACT = mybir.ActivationFunctionType
AX = mybir.AxisListType

P = 128
DM = 1024
KT = DM // P
SEQ = 2048
BT = 512
NB = SEQ // BT
C = 128
NC = BT // C
H = 4
NQ = 12
NG = 4
CK = 4
PB = 15
NS = 8
NW = 32
ZB, ZA, UA, OUT = 12, 16, 20, 24
EPS = 1e-6
LEVELS = (2, 4, 8, 16, 32, 64)
NL = len(LEVELS)
NPREP = 3 + 2 * NL
SLOTS = (NC + 1) * NPREP
THIRDS = 42
BANKS = 6


class Event:

    def __init__(self, sem, per, step=1, credit=None, at=0, turns=1):
        self.sem, self.per, self.step = sem, per, step
        self.credit = per if credit is None else credit
        self.at, self.turns = at, turns

    def rank(self, n):
        return n * self.turns + self.at

    def __call__(self, it, n):
        return self.sem, (it * (self.per * self.turns * self.step)
                          + (self.credit * self.turns + self.rank(n) + 1) * self.step)


def scan_step(p):
    at = [1 + i * ((NPREP - 2) // 4) for i in range(4)]
    return at.index(p) if p in at else None


def slot_plan():
    out, n = [], 0
    for k in range(SLOTS):
        r, p = divmod(k, NPREP)
        q = scan_step(p)
        upto = min(THIRDS, (k + 1) * THIRDS // (SLOTS - NPREP) + 1)
        out.append((r if r < NC else None, p, r - 1 if r > 0 and q is not None else None, q,
                    list(range(n, upto))))
        n = upto
    return out


PLAN = slot_plan()


def pool_after(n):
    g, rest = divmod(n - 3 * (UA - 12) - 8, 3)
    return g if rest == 0 and 0 <= g < NG else None


def psum_jobs():
    jobs = []
    for t in range(NQ):
        if t == 1:
            jobs.append(("gates", 0))
        if t == 2:
            jobs.append(("gt", 0))
        if t == 5:
            jobs.append(("gc", 0))
        if t >= 2 and t - 2 < 8:
            jobs.append(("ss", t - 2))
    for c, p, sc, q, thirds in PLAN:
        for n in thirds:
            if pool_after(n) is not None:
                jobs.append(("pool", pool_after(n)))
        if c is not None:
            if p == 0:
                jobs += [("kt", c), ("vt", c), ("gb", c)]
            elif p == 1:
                jobs += [("kk", c), ("qk", c)]
            elif p == 2:
                jobs.append(("xt", c))
            elif p % 2:
                jobs.append(("w", c * NL + (p - 3) // 2))
            else:
                lv = (p - 4) // 2
                if lv < NL - 1:
                    jobs.append(("xx", c * (NL - 1) + lv))
                jobs.append(("yy", c * NL + lv))
        if sc is not None:
            jobs += {0: [("ks", sc), ("qs", sc)], 1: [("u", sc)], 2: [("su", sc), ("mv", sc)],
                     3: [("ot", sc)]}[q]
    for m in range(8):
        if m >= 1:
            jobs.append(("yt", m - 1))
        jobs.append(("xf", m))
    jobs.append(("yt", 7))
    return jobs


JOBS = psum_jobs()
JOB_AT = {job: n for n, job in enumerate(JOBS)}


def layer_kernel(nc, a):
    ctx = ExitStack()
    with ctx:
        def sb(name, shape, dt=F32):
            return ctx.enter_context(nc.sbuf_tensor(name, shape, dt))

        def over(name, base, offset, shape, dt=F32):
            return nc.alloc_sbuf_tensor_at(name, shape, dt, offset=base + offset)

        def region(name, nbytes):
            sb(name, [P, nbytes // 4])
            return nc.sbuf_base - nbytes

        def event(name, per, step=1, credit=None):
            return Event(ctx.enter_context(nc.semaphore(name)), per, step, credit)

        def chain(name, per, *steps):
            shared = ctx.enter_context(nc.semaphore(name))
            return [Event(shared, per, at=i, turns=len(steps)) for i in range(len(steps))]

        def sem(name):
            return ctx.enter_context(nc.semaphore(name))

        KB = 1024
        ra = region("region_a", 32 * KB)
        cq = over("cq", ra, 0, [P, NQ, BT])
        mtb = over("mtb", ra, 24 * KB, [P, 2, H, C])
        yv = over("yv", ra, 28 * KB, [P, 2, H, C])
        yhi = over("yhi", ra, 0, [P, KT, BT], F32R)
        ylo = over("ylo", ra, 16 * KB, [P, KT, BT], F32R)
        rb = region("region_b", 16 * KB)
        ktok = over("ktok", rb, 0, [P, 2, H, C])
        rv = over("rv", rb, 4 * KB, [P, 2, H, C])
        ub = over("ub", rb, 8 * KB, [P, H, C])
        ve = over("ve", rb, 10 * KB, [P, H, C])
        ao = over("ao", rb, 12 * KB, [P, H, C])
        tks = over("tks", rb, 14 * KB, [P, H, C])
        xres = over("xres", rb, 0, [P, 4, DM])
        rc = region("region_c", 16 * KB)
        y32 = over("y32", rc, 0, [P, KT, BT])
        ytok = over("ytok", rc, 0, [P, 4, DM])
        rd = region("region_d", 32 * KB)
        hhi = over("hhi", rd, 0, [P, KT, BT], F32R)
        hlo = over("hlo", rd, 16 * KB, [P, KT, BT], F32R)
        wada = over("wada", rd, 0, [P, 8, KT, P])
        re_ = region("region_e", 40 * KB)
        wraw = over("wraw", re_, 0, [P, 2, KT, P])
        whi = over("whi", re_, 8 * KB, [P, 2, KT, P], F32R)
        wlo = over("wlo", re_, 16 * KB, [P, 2, KT, P], F32R)
        xb = over("xb", re_, 24 * KB, [P, 4, DM])

        tmpa = sb("tmpa", [P, 2, BT])
        ytt = sb("ytt", [P, 2, BT])
        htmp = sb("htmp", [P, 2, BT])
        raw = sb("raw", [P, 2, BT + CK - 1])
        cacc = sb("cacc", [P, 2, BT])
        ubuf = sb("ubuf", [P, 2, BT + PB])
        win = sb("win", [P, 2, BT + PB])
        pooled = sb("pooled", [P, 2, BT])
        dcy = sb("dcy", [P, H, C])
        lt = sb("lt", [P, H, C])
        gsb = sb("gsb", [8, BT])
        xv = sb("xv", [P, H, C])
        wb = sb("wb", [P, H, C])
        st = sb("st", [P, H, C])
        sdec = sb("sdec", [P, H, C])
        gb4 = sb("gb4", [P, H, C])
        junk = sb("junk", [P, DM], BF16)
        hist = sb("hist", [P, NQ, CK - 1])
        uhist = sb("uhist", [P, NG, PB])
        ident = sb("ident", [P, P])
        upper = sb("upper", [P, P])
        ones = sb("ones", [P, P])
        dmask = sb("dmask", [P, P])
        lmask = sb("lmask", [P, NL + 1, P])
        gpw = sb("gpw", [P, DM])
        poolw = sb("poolw", [P, NG, P])
        wgr = sb("wgr", [P, KT, 8])
        wgh = sb("wgh", [P, KT, 8], F32R)
        wgl = sb("wgl", [P, KT, 8], F32R)
        cw = sb("cw", [P, NQ, CK])
        vec = sb("vec", [P, 64])
        bada = sb("bada", [P, 24])
        ftab = sb("ftab", [P, NG, 16])
        cin = sb("cin", [P, KT, 1 + NS])
        mod = sb("mod", [P, 24, 1 + NS])
        amul = sb("amul", [P, KT, 1 + NS])
        grow = over("grow", ra, 0, [1, DM])
        pwr = over("pwr", ra, 4 * KB, [1, DM])
        ssx = sb("ssx", [P, 4]); rx0 = sb("rx0", [P, 4]); rx = sb("rx", [P, 4])
        ssy = sb("ssy", [P, 4]); ry0 = sb("ry0", [P, 4]); ry = sb("ry", [P, 4])
        half = sb("half", [P, 16]); mhalf = sb("mhalf", [P, 16])
        ga = sb("ga", [P, NC, H]); gab = sb("gab", [P, NC, H]); gl1 = sb("gl1", [P, NC, H])
        gsp = sb("gsp", [P, NC, H]); gg = sb("gg", [P, NC, H])
        btt = sb("btt", [P, NC, H]); beta = sb("beta", [P, NC, H])
        gcs = sb("gcs", [P, 2, NC, H]); eg = sb("eg", [P, 2, NC, H])
        gd = sb("gd", [P, NC, H]); ekg = sb("ekg", [P, NC, H])
        ssb = sb("ssb", [P, 8, NC])
        kk1 = sb("kk1", [P, NC, H]); kk2 = sb("kk2", [P, NC, H]); bb = sb("bb", [P, NC, H]); bke = sb("bke", [P, NC, H])
        sk0 = sb("sk0", [P, NC, H]); sk = sb("sk", [P, NC, H]); odb = sb("odb", [P, NC, H])
        oss = sb("oss", [P, H]); on0 = sb("on0", [P, H]); on = sb("on", [P, H])

        xs, pw8, gr8, ys = (over(n, rb, 4 * KB * j, [NS, DM]) for j, n in enumerate(("xs", "pw8", "gr8", "ys")))
        wring = over("wring", ra, 0, [P, 8, KT, P])
        ssm = over("ssm", rd, 0, [P, NS, H, P])
        krow = over("krow", rd, 16 * KB, [NS * H, NS * H, P])
        cbuf, cnew = over("cbuf", rc, 0, [P, NQ, NS, CK - 1]), over("cnew", rc, 2 * KB, [P, NQ, NS, CK - 1])
        pbuf, pnew = over("pbuf", rc, 4 * KB, [P, NG, NS, PB]), over("pnew", rc, 6 * KB, [P, NG, NS, PB])
        hs, pj = over("hs", rc, 8 * KB, [P, KT, NS]), over("pj", rc, 8 * KB + 512, [P, 24, NS])
        cs = over("cs", rc, 10 * KB, [P, NQ, NS])
        ct = over("ct", rc, 10 * KB + 512, [P, NQ, NS])
        sqs = over("sqs", rc, 11 * KB, [P, NQ, NS])
        kq = over("kq", rc, 11 * KB + 512, [P, NS, H, 2])
        zs = over("zs", rc, 12 * KB, [P, 8, NS])
        ym = over("ym", rc, 12 * KB + 512, [P, 8, NS])
        pls = over("pls", rc, 13 * KB, [P, NG, NS])
        sst = over("sst", rc, 13 * KB + 512, [P, NQ, NS])
        rk = over("rk", rc, 14 * KB, [P, 2, H, NS])
        dl = over("dl", rc, 14 * KB + 256, [P, 4, H, NS])
        gvb = over("gvb", rc, 15 * KB, [P, NS, 2, H])
        g8 = over("g8", rc, 15 * KB + 256, [NS, 8, H])
        gdg = over("gdg", rc, 15 * KB + 512, [NS, NS, 2 * H])
        s8 = over("s8", rc, 15 * KB + 768, [NS, 8])
        drow = over("drow", re_, 0, [NS * H, 2, P])
        spw = over("spw", re_, 2 * KB, [P, 2, NS * H])

        PREW, PSC, ONW, NEA, DTB = 0, 8, 12, 13, 17

        acc = [ctx.enter_context(nc.psum_tensor(f"acc{i}", [P, BT], F32)) for i in range(2)]
        ring = [ctx.enter_context(nc.psum_tensor(f"ring{i}", [P, BT], F32)) for i in range(BANKS)]

        def bank(kind, n=0):
            return ring[JOB_AT[kind, n] % BANKS]

        def heads(t):
            return t[:, :].rearrange("p (h c) -> p h c", h=H)

        def bc(col, n=C):
            return col.unsqueeze(2).to_broadcast([P, H, n])

        def packed(t, s):
            return t[:, 0:H * C // 2].rearrange("p (b s) -> p b s", s=s)

        def half_blocks(t, s, odd):
            return t.rearrange("p h (b two s) -> p (h b) two s", two=2, s=s)[:, :, odd]

        def head_blocks(t, s, odd):
            return t.rearrange("p (b two s) -> p b two s", two=2, s=s)[:, :, odd]

        def level_mask(lv):
            return mbc(lmask[:, 1 + lv])

        def mbc(m):
            return m.unsqueeze(1).to_broadcast([P, H, C])

        x_in = event("x_in", 1, 16)
        xres_in = event("xres_in", 1, 16)
        w_in0, w_in1 = event("w_in0", NW // 2, 16), event("w_in1", NW // 2, 16)
        w_in = [w_in0, w_in1]
        y_out = event("y_out", 4, 16, 1)
        w_hi, w_lo = event("w_hi", NW), event("w_lo", NW)
        proj = event("proj", NW)
        raw_f, hist_in, hist_out = event("raw_f", NQ), event("hist_in", NQ), event("hist_out", NQ)
        conv_a, conv, silu = event("conv_a", 3 * NQ), event("conv", NQ), event("silu", NQ)
        sq = event("sq", 8)
        ss_ev = event("ss_ev", 8)
        g_c, g_y, g_b, g_sp, g_g, gc_f, g_d, k_1, k_2, b_f, bke_f = chain(
            "dve_factors", 1, "g_c", "g_y", "g_b", "g_sp", "g_g", "gc_f", "g_d", "k_1", "k_2", "b_f", "bke_f")
        g_t, g_ab, g_e, g_l, g_eg, g_ekg = chain("act_factors", 1, "g_t", "g_ab", "g_e", "g_l", "g_eg", "g_ekg")
        sk_0, sk_f, odb_0, ry_0, ry_f, ftab_f = chain(
            "pool_factors", 1, "sk_0", "sk_f", "odb_0", "ry_0", "ry_f", "ftab_f")
        tanh_f, z_f = event("tanh_f", 8), event("z_f", 8)
        u_f, u_in, u_out, u_add, win_f = (event("u_f", 4), event("u_in", 4), event("u_out", 4),
                                          event("u_add", 10), event("win_f", 4))
        pooled_f, ya_f = event("pooled_f", 4), event("ya_f", 4)
        kt_f, gb_in, d_e, x_0 = (event(n, NC) for n in ("kt_f", "gb_in", "d_e", "x_0"))
        rv_f, d_1, d_2, d_b, lt_f, mt_f, y_0, y_1 = chain(
            "dve_prep", NC, "rv_f", "d_1", "d_2", "d_b", "lt_f", "mt_f", "y_0", "y_1")
        w_f, y_l, x_l = event("w_f", NC * NL), event("y_l", NC * NL), event("x_l", NC * (NL - 1))
        ks_t, r_f, ao_f, ve_f, s_f, o_f, yb_f = chain(
            "dve_scan", NC, "ks_t", "r_f", "ao_f", "ve_f", "s_f", "o_f", "yb_f")
        o_n0, o_n, o_sq, o_s = chain("pool_norm", NC, "o_n0", "o_n", "o_sq", "o_s")
        sdec_f, u_c = event("sdec_f", NC), event("u_c", NC)
        o_sq4 = event("o_sq4", 4 * NC)
        yhi_f, ylo_f, ytt_f, ytok_f = (event(n, 8) for n in ("yhi_f", "ylo_f", "ytt_f", "ytok_f"))
        ysq, yn_f, yr_f = event("ysq", 4), event("yn_f", 4), event("yr_f", 4)
        xsq, rx_0, rx_f, xn = event("xsq", 4), event("rx_0", 1), event("rx_f", 1), event("xn", 4)
        h_f, h_hi, h_lo = event("h_f", 8), event("h_hi", 8), event("h_lo", 8)
        per_job = {"gates": 1, "gt": 1, "gc": 1, "ss": 8, "pool": 4, "w": NC * NL, "xx": NC * (NL - 1), "yy": NC * NL,
                   "yt": 8, "xf": 8}
        job = {kind: event("job_" + kind, per_job.get(kind, NC)) for kind in dict.fromkeys(k for k, _ in JOBS)}
        reader = {"gates": [g_c], "gt": [g_y, g_t], "gc": [gc_f], "ss": [ss_ev], "pool": [ya_f], "kt": [kt_f], "vt": [rv_f],
                  "gb": [d_1], "kk": [lt_f], "qk": [mt_f], "xt": [x_0], "w": [w_f], "xx": [x_l], "yy": [y_l],
                  "ks": [ks_t], "qs": [ao_f], "u": [u_c], "su": [s_f], "mv": [o_f], "ot": [yb_f],
                  "yt": [ytok_f], "xf": [h_f]}
        one = {"gates", "gc"}

        s_const, s_prm, s_prm2, s_pre, s_end = (sem(n) for n in ("s_const", "s_prm", "s_prm2", "s_pre", "s_end"))
        s_cact, s_mod, s_modc, s_tr, s_trc, s_row, s_rowc = (sem(n) for n in (
            "s_cact", "s_mod", "s_modc", "s_tr", "s_trc", "s_row", "s_rowc"))
        ada_in = [sem(f"ada_in{i}") for i in range(8)]
        out_sem = sem("out_sem")
        pool_held, pe_held = sem("pool_held"), sem("pe_held")
        sm_x, sm_st, sm_ssm, sm_tile, sm_new, sm_snew, sm_y = (sem(n) for n in (
            "sm_x", "sm_st", "sm_ssm", "sm_tile", "sm_new", "sm_snew", "sm_y"))
        sm_w = ada_in
        sm_sq, sm_r, sm_xn, sm_xt, sm_h, sm_gp, sm_g, sm_gd, sm_gb, sm_gr = (sem(n) for n in (
            "sm_sq", "sm_r", "sm_xn", "sm_xt", "sm_h", "sm_gp", "sm_g", "sm_gd", "sm_gb", "sm_gr"))
        sm_pj, sm_cv, sm_z, sm_pl, sm_plp, sm_s2, sm_s2p, sm_kv, sm_d, sm_dt, sm_op, sm_rk, sm_o, sm_op2, sm_ym = (
            sem(n) for n in ("sm_pj", "sm_cv", "sm_z", "sm_pl", "sm_plp", "sm_s2", "sm_s2p", "sm_kv", "sm_d", "sm_dt",
                             "sm_op", "sm_rk", "sm_o", "sm_op2", "sm_ym"))
        sm_ot, sm_yt, sm_on, sm_oe, sm_gt = (sem(n) for n in ("sm_ot", "sm_yt", "sm_on", "sm_oe", "sm_gt"))

        def bank_free(eng, it, kind, n=0, *needs):
            j = JOB_AT[kind, n]
            before = j - BANKS
            late = before < 0
            if late:
                before = max(i for i in range(len(JOBS)) if i % BANKS == j % BANKS)
            needs = list(needs)
            if not (late and it is PROLOGUE):
                pk, pn = JOBS[before]
                needs += [(ev, pn - ev.per if late else pn) for ev in reader[pk]]
            latest = {}
            for ev, m in needs:
                if ev.sem not in latest or ev.rank(m) > latest[ev.sem][0]:
                    latest[ev.sem] = ev.rank(m), ev, m
            for _, ev, m in latest.values():
                eng.wait_ge(*ev(it, m))

        PROLOGUE = -1

        def prep_of(k):
            return PLAN[k]

        def tile_reader(eng, it, t):
            t = t - 2
            if t < 0:
                eng.wait_ge(*ytt_f(it, t))
            elif t < NQ:
                eng.wait_ge(*raw_f(it, t))
            elif t < UA:
                eng.wait_ge(*z_f(it, t - ZB))
            elif t < OUT:
                eng.wait_ge(*u_f(it, t - UA))
            else:
                eng.wait_ge(*ytt_f(it, t - OUT))

        block = ctx.enter_context(nc.Block())

        @block.sync
        def _(sp):
            for ev in (xres_in, w_in0, w_in1):
                sp.nop().then_inc(ev.sem, ev.per * ev.step)
            for dst, src in ((ident, a["ident"]), (upper, a["upper"]), (dmask, a["dmask"]), (lmask, a["lmask"])):
                sp.dma_start(dst[:], src).then_inc(s_const, 16)
            for dst, src in ((cin, a["c_all"]), (bada, a["b_ada"]), (vec[:, PREW:PREW + 8], a["pre_w"])):
                sp.dma_start(dst[:], src).then_inc(s_prm, 16)
            for n in range(8):
                sp.dma_start(wada[:, n], a["w_ada"][n]).then_inc(ada_in[n], 16)
            sp.dma_start(xb[:], a["x"][0]).then_inc(x_in.sem, 16)
            for dst, src in ((vec[:, PSC:PSC + 4], a["pool_scale"]), (vec[:, ONW:ONW + 1], a["o_norm"]),
                             (vec[:, NEA:NEA + 4], a["a_log"].to_broadcast([P, H])),
                             (vec[:, DTB:DTB + 4], a["dt_bias"].to_broadcast([P, H])),
                             (cw, a["conv_w"]), (wgr, a["w_gate"]), (ftab, a["ftab"]),
                             (pwr, a["post_w"])):
                sp.dma_start(dst[:], src).then_inc(s_prm2, 16)
            for n in range(8, 24):
                sp.wait_ge(s_mod, n - 7)
                sp.dma_start(wada[:, n % 8], a["w_ada"][n]).then_inc(ada_in[n % 8], 16)
            for t in range(2):
                sp.dma_start(wraw[:, t], a["w"][t]).then_inc(w_in[t].sem, 16)
            with sp.Fori(0, NB) as it:
                sp.wait_ge(*job["xf"](it, -1))
                sp.dma_start(xb[:], a["x"][it + 1]).then_inc(x_in.sem, 16)
                for t in range(NW):
                    sp.wait_ge(*w_lo(it, t))
                    sp.dma_start(wraw[:, t % 2], a["w"][(t + 2) % NW]).then_inc(w_in[t % 2].sem, 16)
                    if t == OUT:
                        sp.wait_ge(*job["su"](it, NC - 1))
                        sp.wait_ge(*job["mv"](it, NC - 1))
                        sp.wait_ge(*job["ot"](it, NC - 1))
                        sp.dma_start(xres[:], a["x"][it]).then_inc(xres_in.sem, 16)
            sp.wait_ge(s_end, 1)
            sp.dma_start(a["o_ssm"], st[:]).then_inc(out_sem, 16)
            sp.dma_start(a["o_conv"], hist[:]).then_inc(out_sem, 16)
            sp.dma_start(a["o_pool"], uhist[:]).then_inc(out_sem, 16)
            sp.wait_ge(*x_in(NB - 1, 0))
            sp.wait_ge(*w_in0(NB, 0))
            sp.wait_ge(*w_in1(NB, 0))
            sp.wait_ge(*yr_f(NB - 1, 3))
            sp.wait_ge(*y_out(NB - 1, 3))
            sp.dma_start(xs[:], a["xs"]).then_inc(sm_x, 16)
            for dst, src in ((cbuf, a["s_conv"]), (pbuf, a["s_pool"]), (pw8, a["post_w"].to_broadcast([NS, DM]))):
                sp.dma_start(dst[:], src).then_inc(sm_st, 16)
            for n in range(NW):
                if n >= 8:
                    sp.wait_ge(sm_tile, n - 7)
                sp.dma_start(wring[:, n % 8], a["w"][n]).then_inc(sm_w[n % 8], 16)
                if n == 8:
                    sp.wait_ge(*h_lo(NB - 1, 7))
                    sp.wait_ge(*h_hi(NB - 1, 7))
                    sp.dma_start(ssm[:], a["s_ssm"]).then_inc(sm_ssm, 16)
            sp.wait_ge(sm_new, 2)
            sp.dma_start(a["o_sconv"], cnew[:]).then_inc(out_sem, 16)
            sp.dma_start(a["o_spool"], pnew[:]).then_inc(out_sem, 16)
            for r in range(NS):
                sp.wait_ge(sm_snew, r + 1)
                sp.dma_start(a["o_sssm"][:, r], ssm[:, r]).then_inc(out_sem, 16)
            sp.wait_ge(sm_y, 5)
            sp.dma_start(a["ys"], ys[:]).then_inc(out_sem, 16)
            sp.wait_ge(out_sem, 16 * (6 + NS))

        def front_act(act, it):
            act.wait_ge(*x_in(it, 0))
            for t in range(4):
                if it is not PROLOGUE or t > 0:
                    act.wait_ge(*xsq(it, t - 1))
                if t == 0 and it is not PROLOGUE:
                    act.wait_ge(*rx_0(it, -1))
                    act.wait_ge(*ysq(it, -1))
                nc.scalar.activation(junk[:, :], xb[:, t, :], ACT.Square,
                                     accum_out=ssx[:, t:t + 1]).then_inc(xsq.sem, 1)

        def front_h(act, it, m):
            act.wait_ge(*job["xf"](it, m))
            if m >= 2 or it is not PROLOGUE:
                act.wait_ge(*h_lo(it, m - 2))
            nc.scalar.activation(htmp[:, m % 2], bank("xf", m)[:], ACT.Identity, bias=mod[:, m, 0:1],
                                 scale=amul[:, m, 0:1]).then_inc(h_f.sem, 1)

        @block.scalar
        def _(act):
            for ev in (w_hi, raw_f, silu, sq, g_ab, g_e, g_l, g_t, g_eg, g_ekg, tanh_f, u_f, kt_f, d_e, x_0,
                       u_c, o_sq4, yhi_f, ytt_f, ysq):
                act.nop().then_inc(ev.sem, ev.per)
            act.wait_ge(s_prm, 48)
            nc.scalar.activation(cin[:], cin[:], ACT.Silu).then_inc(s_cact, 1)
            front_act(act, PROLOGUE)
            act.wait_ge(s_prm2, 128)
            nc.scalar.activation(vec[:, NEA:NEA + 4], vec[:, NEA:NEA + 4], ACT.Exp).then_inc(s_cact, 1)
            act.wait_ge(s_pre, 5)
            for m in range(8):
                front_h(act, PROLOGUE, m)
            for t in range(2):
                act.wait_ge(*w_in[t](0, 0))
                nc.scalar.activation(whi[:, t], wraw[:, t], ACT.Copy).then_inc(w_hi.sem, 1)

            def split_hi(it, t):
                act.wait_ge(*w_in[(t + 1) % 2](it + (t + 1) // NW, (t + 1) % NW // 2))
                act.wait_ge(*proj(it, t - 1))
                nc.scalar.activation(whi[:, (t + 1) % 2], wraw[:, (t + 1) % 2], ACT.Copy).then_inc(w_hi.sem, 1)

            def tile(it, t):
                act.wait_ge(*proj(it, t))
                if t < NQ:
                    act.wait_ge(*conv(it, t - 2))
                    act.wait_ge(*hist_out(it, t - 2))
                    nc.scalar.activation(raw[:, t % 2, CK - 1:], acc[t % 2][:], ACT.Copy).then_inc(raw_f.sem, 1)
                elif t < UA:
                    z = t - ZB
                    if z == 0:
                        act.wait_ge(*job["ss"](it, 7))
                        act.wait_ge(*job["ss"](it, 6))
                    act.wait_ge(*z_f(it, z - 2))
                    nc.scalar.activation(tmpa[:, t % 2], acc[t % 2][:], ACT.Tanh, scale=0.5).then_inc(tanh_f.sem, 1)
                elif t < OUT:
                    g = t - UA
                    act.wait_ge(*pooled_f(it, g - 2))
                    act.wait_ge(*u_out(it, g - 2))
                    nc.scalar.activation(ubuf[:, g % 2, PB:], acc[t % 2][:], ACT.Copy).then_inc(u_f.sem, 1)
                else:
                    m = t - OUT
                    act.wait_ge(*job["yt"](it, m - 2))
                    nc.scalar.activation(ytt[:, m % 2], acc[t % 2][:], ACT.Copy).then_inc(ytt_f.sem, 1)

            def silu_sq(it, t):
                act.wait_ge(*conv(it, t))
                if t == 0:
                    act.wait_ge(*proj(it, -1))
                nc.scalar.activation(cq[:, t], cacc[:, t % 2], ACT.Silu).then_inc(silu.sem, 1)
                if t < 8:
                    act.wait_ge(*silu(it, t))
                    if t < 2:
                        act.wait_ge(*z_f(it, -1 - t % 2))
                        act.wait_ge(*z_f(it, -1))
                    else:
                        act.wait_ge(*job["ss"](it, t - 2))
                    nc.scalar.activation(tmpa[:, t % 2], cq[:, t], ACT.Square).then_inc(sq.sem, 1)

            with act.Fori(0, NB) as it:
                for t in range(NQ):
                    if t:
                        split_hi(it, t)
                    if t == 2:
                        act.wait_ge(*job["gt"](it, 0))
                        act.wait_ge(*g_b(it, -1))
                        nc.scalar.activation(btt[:], bank("gt")[:, 0:32].rearrange("p (c e) -> p c e", c=NC)[:, :, 0:4],
                                             ACT.Tanh, scale=0.5).then_inc(g_t.sem, 1)
                        act.wait_ge(*g_y(it, 0))
                        nc.scalar.activation(gab[:], ga[:], ACT.Abs).then_inc(g_ab.sem, 1)
                        act.wait_ge(*g_ab(it, 0))
                        act.wait_ge(*g_sp(it, -1))
                        nc.scalar.activation(gl1[:], gab[:], ACT.Exp, scale=-1.0).then_inc(g_e.sem, 1)
                        act.wait_ge(*g_e(it, 0))
                        nc.scalar.activation(gl1[:], gl1[:], ACT.Ln, bias=1.0).then_inc(g_l.sem, 1)
                    tile(it, t)
                    if t >= 1:
                        silu_sq(it, t - 1)
                silu_sq(it, NQ - 1)
                act.wait_ge(*gc_f(it, 0))
                act.wait_ge(*yb_f(it, -1))
                nc.scalar.activation(eg[:], gcs[:], ACT.Exp).then_inc(g_eg.sem, 1)
                act.wait_ge(*g_d(it, 0))
                nc.scalar.activation(ekg[:], gd[:], ACT.Exp).then_inc(g_ekg.sem, 1)
                for c, p, sc, q, thirds in PLAN:
                    for n in thirds:
                        if n < 36 and n % 3 == 0:
                            split_hi(it, 12 + n // 3)
                        if n < 36 and n % 3 == 2:
                            tile(it, 12 + n // 3)
                    if c is not None and p == 0:
                        act.wait_ge(*job["kt"](it, c))
                        act.wait_ge(*job["su"](it, c - 2)) if c >= 2 else act.wait_ge(*yr_f(it, -1))
                        nc.scalar.activation(ktok[:, c % 2], heads(bank("kt", c)), ACT.Copy).then_inc(kt_f.sem, 1)
                        act.wait_ge(*d_2(it, c))
                        nc.scalar.activation(dcy[:], dcy[:], ACT.Exp).then_inc(d_e.sem, 1)
                    elif c is not None and p == 2:
                        act.wait_ge(*job["xt"](it, c))
                        act.wait_ge(*job["w"](it, c * NL - 1))
                        nc.scalar.activation(xv[:], heads(bank("xt", c)), ACT.Copy).then_inc(x_0.sem, 1)
                    if q == 1 and sc is not None:
                        act.wait_ge(*job["u"](it, sc))
                        act.wait_ge(*ve_f(it, sc - 1))
                        act.wait_ge(*job["mv"](it, sc - 1)) if sc else act.wait_ge(*yr_f(it, -1))
                        nc.scalar.activation(ub[:], heads(bank("u", sc)), ACT.Copy).then_inc(u_c.sem, 1)
                    if q == 2 and sc is not None:
                        act.wait_ge(*o_f(it, sc))
                        act.wait_ge(*o_n0(it, sc - 1))
                        for h in range(H):
                            act.wait_ge(*o_sq4(it, 4 * sc + h - 1))
                            if h == 0 and sc == 0:
                                act.wait_ge(*xsq(it, -1))
                                act.wait_ge(*ysq(it, -1))
                            nc.scalar.activation(junk[:, 0:C], ao[:, h], ACT.Square,
                                                 accum_out=oss[:, h:h + 1]).then_inc(o_sq4.sem, 1)
                for m in range(8):
                    act.wait_ge(*yb_f(it, NC - 1))
                    act.wait_ge(*job["ot"](it, NC - 1))
                    act.wait_ge(*ya_f(it, NG - 1))
                    nc.scalar.activation(yhi[:, m], y32[:, m], ACT.Copy).then_inc(yhi_f.sem, 1)
                act.wait_ge(*o_sq4(it, 4 * NC - 1))
                front_act(act, it)
                for m in range(8):
                    split_hi(it, OUT + m)
                    tile(it, OUT + m)
                    front_h(act, it, m)
                split_hi(it, NW)
                for t in range(4):
                    act.wait_ge(*ytok_f(it, 7))
                    act.wait_ge(*ry_0(it, -1))
                    act.wait_ge(*ysq(it, t - 1))
                    act.wait_ge(*xsq(it, 3))
                    nc.scalar.activation(junk[:, :], ytok[:, t], ACT.Square, accum_out=ssy[:, t:t + 1]).then_inc(ysq.sem, 1)

            act.wait_ge(sm_x, 16)
            act.wait_ge(*ysq(NB - 1, 3))
            nc.scalar.activation(junk[0:NS, :], xs[:], ACT.Square, accum_out=s8[:, 0:1]).then_inc(sm_sq, 1)
            act.wait_ge(sm_gp, 1)
            nc.scalar.activation(g8[:, 0], ring[1][0:NS, 0:4], ACT.Tanh, scale=0.5).then_inc(sm_g, 1)
            act.wait_ge(sm_g, 2)
            nc.scalar.activation(g8[:, 2], g8[:, 1], ACT.Abs).then_inc(sm_g, 1)
            act.wait_ge(sm_g, 3)
            nc.scalar.activation(g8[:, 2], g8[:, 2], ACT.Exp, scale=-1.0).then_inc(sm_g, 1)
            act.wait_ge(sm_g, 4)
            nc.scalar.activation(g8[:, 2], g8[:, 2], ACT.Ln, bias=1.0).then_inc(sm_g, 1)
            act.wait_ge(sm_g, 8)
            nc.scalar.activation(g8[:, 5], g8[:, 4], ACT.Exp).then_inc(sm_g, 1)
            act.wait_ge(sm_pj, 1)
            nc.scalar.activation(zs[:], pj[:, 12:20], ACT.Tanh, scale=0.5).then_inc(sm_z, 1)
            act.wait_ge(sm_cv, 7)
            nc.scalar.activation(cs[:], ct[:], ACT.Silu).then_inc(sm_cv, 1)
            act.wait_ge(sm_y, 1)
            act.wait_ge(sm_sq, 1)
            nc.scalar.activation(junk[0:NS, :], ys[:], ACT.Square, accum_out=s8[:, 4:5]).then_inc(sm_y, 1)

        def front_xn(dve, it):
            dve.wait_ge(*rx_f(it, 0))
            for t in range(4):
                nc.vector.tensor_scalar(xb[:, t], xb[:, t], rx[:, t:t + 1], None, ALU.mult).then_inc(xn.sem, 1)

        def front_lo(dve, it, m):
            dve.wait_ge(*h_hi(it, m))
            nc.vector.tensor_tensor(hlo[:, m], htmp[:, m % 2], hhi[:, m].bitcast(F32), ALU.subtract).then_inc(h_lo.sem, 1)

        @block.vector
        def _(dve):
            for ev in (conv_a, conv, ss_ev, g_c, g_y, g_sp, g_g, g_b, gc_f, g_d, k_1, k_2, b_f, bke_f, z_f, pooled_f, ya_f,
                       rv_f, d_1, d_2, d_b, lt_f, mt_f, y_0, y_1, y_l, x_l, w_f, ks_t, r_f, ao_f, ve_f, s_f, o_f, yb_f,
                       ylo_f, ytok_f, yn_f, yr_f):
                dve.nop().then_inc(ev.sem, ev.per)
            nc.vector.memset(st[:], 0.0)
            nc.vector.memset(ones[:], 1.0)
            nc.vector.memset(hist[:], 0.0)
            nc.vector.memset(uhist[:], 0.0).then_inc(s_pre, 1)
            dve.wait_ge(s_mod, 24)
            dve.wait_ge(s_prm, 48)
            nc.vector.tensor_tensor(mod[:], ring[0][:, 0:216].rearrange("p (m s) -> p m s", m=24),
                                    bada[:].unsqueeze(2).to_broadcast([P, 24, 1 + NS]), ALU.add).then_inc(s_pre, 1)
            dve.wait_ge(s_pre, 2)
            nc.vector.tensor_scalar(amul[:], mod[:, 8:16], 1.0, None, ALU.add).then_inc(s_pre, 1)
            dve.wait_ge(s_pre, 3)
            nc.vector.tensor_tensor(amul[:], amul[:], vec[:, PREW:PREW + 8].unsqueeze(2).to_broadcast([P, 8, 1 + NS]),
                                    ALU.mult).then_inc(s_pre, 1)
            dve.wait_ge(s_cact, 2)
            dve.wait_ge(s_prm2, 128)
            nc.vector.tensor_scalar(vec[:, NEA:NEA + 4], vec[:, NEA:NEA + 4], -1.0, None, ALU.mult)
            nc.vector.tensor_scalar(vec[:, PSC:PSC + 5], vec[:, PSC:PSC + 5], 0.5, None, ALU.mult)
            nc.vector.tensor_copy(wgh[:], wgr[:]).then_inc(s_pre, 1)
            dve.wait_ge(s_pre, 5)
            nc.vector.tensor_tensor(wgl[:], wgr[:], wgh[:].bitcast(F32), ALU.subtract).then_inc(s_pre, 1)
            for m in range(2):
                dve.wait_ge(s_tr, m + 1)
                nc.vector.tensor_tensor(grow[:, m * 512:(m + 1) * 512], ring[1 + m][0:1, :],
                                        pwr[:, m * 512:(m + 1) * 512], ALU.mult).then_inc(s_trc, 1)
            for m in range(2):
                dve.wait_ge(s_row, m + 1)
                nc.vector.tensor_copy(gpw[:, m * 512:(m + 1) * 512], ring[3 + m][:]).then_inc(s_rowc, 1)
            front_xn(dve, PROLOGUE)
            for m in range(8):
                front_lo(dve, PROLOGUE, m)

            def convolve(it, t):
                r = raw[:, t % 2]
                dve.wait_ge(*raw_f(it, t))
                dve.wait_ge(*hist_in(it, t))
                dve.wait_ge(*silu(it, t - 2))
                nc.vector.tensor_scalar(cacc[:, t % 2], r[:, 0:BT], cw[:, t, 0:1], None, ALU.mult).then_inc(conv_a.sem, 1)
                for j in range(1, CK):
                    dve.wait_ge(*conv_a(it, 3 * t + j - 1))
                    nc.vector.scalar_tensor_tensor(out=cacc[:, t % 2], in0=r[:, j:j + BT], scalar=cw[:, t, j:j + 1],
                                                   in1=cacc[:, t % 2], op0=ALU.mult, op1=ALU.add
                                                   ).then_inc((conv_a if j < CK - 1 else conv).sem, 1)

            def stat(it, t):
                dve.wait_ge(*job["ss"](it, t))
                if t == 0:
                    dve.wait_ge(*k_1(it, -1))
                    dve.wait_ge(*odb_0(it, -1))
                nc.vector.tensor_copy(ssb[:, t], bank("ss", t)[:, 0:NC]).then_inc(ss_ev.sem, 1)

            def zmul(it, t):
                z = t - ZB
                yk = y32[:, (z + 4) % 8]
                dve.wait_ge(*tanh_f(it, z))
                if z == 0:
                    dve.wait_ge(*y_out(it, -1))
                nc.vector.scalar_tensor_tensor(out=yk, in0=tmpa[:, t % 2], scalar=1.0, in1=acc[t % 2][:],
                                               op0=ALU.add, op1=ALU.mult).then_inc(z_f.sem, 1)

            with dve.Fori(0, NB) as it:
                for t in range(NQ):
                    if t == 1:
                        dve.wait_ge(*job["gates"](it, 0))
                        dve.wait_ge(*job["gt"](it, -1))
                        nc.vector.tensor_copy(gsb[:], bank("gates")[0:8, :]).then_inc(g_c.sem, 1)
                    if t == 2:
                        dve.wait_ge(*job["gt"](it, 0))
                        dve.wait_ge(*g_t(it, 0))
                        dve.wait_ge(*g_sp(it, -1))
                        nc.vector.tensor_tensor(ga[:], bank("gt")[:, 0:32].rearrange("p (c e) -> p c e", c=NC)[:, :, 4:8],
                                                vec[:, DTB:DTB + 4].unsqueeze(1).to_broadcast([P, NC, H]), ALU.add
                                                ).then_inc(g_y.sem, 1)
                        dve.wait_ge(*g_t(it, 0))
                        dve.wait_ge(*b_f(it, -1))
                        nc.vector.tensor_scalar(beta[:], btt[:], 0.5, 0.5, ALU.mult, ALU.add).then_inc(g_b.sem, 1)
                    convolve(it, t)
                    if t == 2:
                        dve.wait_ge(*g_l(it, 0))
                        dve.wait_ge(*g_y(it, 0))
                        nc.vector.scalar_tensor_tensor(out=gsp[:], in0=ga[:], scalar=0.0, in1=gl1[:], op0=ALU.max,
                                                       op1=ALU.add).then_inc(g_sp.sem, 1)
                        dve.wait_ge(*g_sp(it, 0))
                        dve.wait_ge(*job["gc"](it, -1))
                        dve.wait_ge(*gb_in(it, -1))
                        nc.vector.tensor_tensor(gg[:], gsp[:], vec[:, NEA:NEA + 4].unsqueeze(1).to_broadcast([P, NC, H]),
                                                ALU.mult).then_inc(g_g.sem, 1)
                    if t == 5:
                        dve.wait_ge(*job["gc"](it, 0))
                        dve.wait_ge(*g_eg(it, -1))
                        dve.wait_ge(*d_1(it, -1))
                        nc.vector.tensor_copy(gcs[:].rearrange("p a c h -> p (a c h)"), bank("gc")[:, 0:32]).then_inc(gc_f.sem, 1)
                        dve.wait_ge(*gc_f(it, 0))
                        dve.wait_ge(*g_ekg(it, -1))
                        nc.vector.tensor_tensor(gd[:], gcs[:, 1], gcs[:, 0], ALU.subtract).then_inc(g_d.sem, 1)
                    if 2 <= t < 10:
                        stat(it, t - 2)
                dve.wait_ge(*ss_ev(it, 7))
                nc.vector.tensor_scalar(kk1[:], ssb[:, 0:4].rearrange("p h c -> p c h"), EPS, None, ALU.add).then_inc(k_1.sem, 1)
                dve.wait_ge(*k_1(it, 0))
                nc.vector.reciprocal(kk2[:], kk1[:]).then_inc(k_2.sem, 1)
                dve.wait_ge(*k_2(it, 0))
                nc.vector.tensor_tensor(bb[:], beta[:], kk2[:], ALU.mult).then_inc(b_f.sem, 1)
                dve.wait_ge(*b_f(it, 0))
                dve.wait_ge(*g_ekg(it, 0))
                nc.vector.tensor_tensor(bke[:], bb[:], ekg[:], ALU.mult).then_inc(bke_f.sem, 1)

                for c, p, sc, q, thirds in PLAN:
                    for n in thirds:
                        t = 12 + n // 3
                        if n % 3 == 2 and t < UA:
                            zmul(it, t)
                        if n % 3 == 2 and UA <= t - 1 < OUT:
                            g = t - 1 - UA
                            dve.wait_ge(*win_f(it, g))
                            dve.wait_ge(*job["pool"](it, g - 2))
                            nc.vector.scalar_tensor_tensor(out=pooled[:, g % 2], in0=win[:, g % 2, PB:],
                                                           scalar=1.0 / (2 << g), in1=ubuf[:, g % 2, PB:],
                                                           op0=ALU.mult, op1=ALU.subtract).then_inc(pooled_f.sem, 1)
                        g = pool_after(n)
                        if g is not None:
                            dve.wait_ge(*job["pool"](it, g))
                            dve.wait_ge(*z_f(it, 4 + g))
                            nc.vector.scalar_tensor_tensor(out=y32[:, g], in0=bank("pool", g)[:], scalar=vec[:, PSC + g:PSC + g + 1],
                                                           in1=y32[:, g], op0=ALU.mult, op1=ALU.mult).then_inc(ya_f.sem, 1)
                    if c is not None and p == 0:
                        dve.wait_ge(*job["vt"](it, c))
                        dve.wait_ge(*sk_f(it, 0))
                        dve.wait_ge(*job["u"](it, c - 2)) if c >= 2 else dve.wait_ge(*yr_f(it, -1))
                        nc.vector.tensor_tensor(rv[:, c % 2], heads(bank("vt", c)), bc(sk[:, c]), ALU.mult).then_inc(rv_f.sem, 1)
                        dve.wait_ge(*job["gb"](it, c))
                        dve.wait_ge(*mt_f(it, c - 1))
                        nc.vector.tensor_tensor(dcy[:], heads(bank("gb", c)), bc(gcs[:, 0, c]), ALU.subtract).then_inc(d_1.sem, 1)
                        dve.wait_ge(*d_1(it, c))
                        nc.vector.tensor_tensor(dcy[:], dcy[:], mbc(dmask[:]), ALU.min).then_inc(d_2.sem, 1)
                        dve.wait_ge(*d_e(it, c))
                        nc.vector.tensor_tensor(dcy[:], dcy[:], bc(bb[:, c]), ALU.mult).then_inc(d_b.sem, 1)
                    elif c is not None and p == 1:
                        dve.wait_ge(*d_b(it, c))
                        dve.wait_ge(*job["kk"](it, c))
                        dve.wait_ge(*job["w"](it, c * NL - 1))
                        nc.vector.tensor_tensor(lt[:], heads(bank("kk", c)), dcy[:], ALU.mult).then_inc(lt_f.sem, 1)
                        dve.wait_ge(*job["qk"](it, c))
                        if c >= 2:
                            dve.wait_ge(*job["mv"](it, c - 2))
                        elif c == 0:
                            dve.wait_ge(*proj(it, -1))
                        nc.vector.tensor_tensor(mtb[:, c % 2], heads(bank("qk", c)), dcy[:], ALU.mult).then_inc(mt_f.sem, 1)
                        dve.wait_ge(*lt_f(it, c))
                        if c >= 2:
                            dve.wait_ge(*job["u"](it, c - 2))
                        nc.vector.tensor_tensor(yv[:, c % 2], lt[:], mbc(lmask[:, 0]), ALU.mult).then_inc(y_0.sem, 1)
                        dve.wait_ge(*y_0(it, c))
                        nc.vector.tensor_tensor(yv[:, c % 2], mbc(ident[:]), yv[:, c % 2], ALU.subtract).then_inc(y_1.sem, 1)
                    elif c is not None and p >= 3 and p % 2:
                        lv = (p - 3) // 2
                        i = c * NL + lv
                        dve.wait_ge(*job["w"](it, i))
                        dve.wait_ge(*job["yy"](it, i - 1))
                        sz = LEVELS[lv]
                        nc.vector.tensor_tensor(
                            wb[:].rearrange("p h (b two s) -> p (h b) two s", two=2, s=sz),
                            packed(bank("w", i), sz).unsqueeze(2).to_broadcast([P, H * C // (2 * sz), 2, sz]),
                            level_mask(lv), ALU.mult).then_inc(w_f.sem, 1)
                    elif c is not None and p >= 4:
                        lv = (p - 4) // 2
                        sz = LEVELS[lv]
                        if lv < NL - 1:
                            i = c * (NL - 1) + lv
                            dve.wait_ge(*job["xx"](it, i))
                            if lv == 0:
                                dve.wait_ge(*x_0(it, c))
                            else:
                                dve.wait_ge(*x_l(it, i - 1))
                            xe = half_blocks(xv[:], sz, 0)
                            nc.vector.tensor_tensor(xe, xe, packed(bank("xx", i), sz), ALU.subtract).then_inc(x_l.sem, 1)
                        i = c * NL + lv
                        dve.wait_ge(*job["yy"](it, i))
                        if lv == 0:
                            dve.wait_ge(*y_1(it, c))
                        else:
                            dve.wait_ge(*y_l(it, i - 1))
                        yo = half_blocks(yv[:, c % 2], sz, 1)
                        nc.vector.tensor_tensor(yo, yo, packed(bank("yy", i), sz), ALU.subtract).then_inc(y_l.sem, 1)
                    if sc is not None and q == 0:
                        dve.wait_ge(*job["ks"](it, sc))
                        dve.wait_ge(*g_eg(it, 0))
                        dve.wait_ge(*r_f(it, sc - 1))
                        if sc == 0:
                            dve.wait_ge(*yr_f(it, -1))
                        nc.vector.tensor_tensor(tks[:], heads(bank("ks", sc)), bc(eg[:, 0, sc]), ALU.mult).then_inc(ks_t.sem, 1)
                        dve.wait_ge(*ks_t(it, sc))
                        dve.wait_ge(*rv_f(it, sc))
                        nc.vector.tensor_tensor(rv[:, sc % 2], rv[:, sc % 2], tks[:], ALU.subtract).then_inc(r_f.sem, 1)
                        dve.wait_ge(*job["qs"](it, sc))
                        dve.wait_ge(*job["ot"](it, sc - 1))
                        nc.vector.tensor_tensor(ao[:], heads(bank("qs", sc)), bc(eg[:, 0, sc]), ALU.mult).then_inc(ao_f.sem, 1)
                    if sc is not None and q == 1:
                        dve.wait_ge(*u_c(it, sc))
                        dve.wait_ge(*job["su"](it, sc - 1))
                        dve.wait_ge(*bke_f(it, 0))
                        if sc == 0:
                            dve.wait_ge(*yr_f(it, -1))
                        nc.vector.tensor_tensor(ve[:], ub[:], bc(bke[:, sc]), ALU.mult).then_inc(ve_f.sem, 1)
                    if sc is not None and q == 2:
                        dve.wait_ge(*job["su"](it, sc))
                        dve.wait_ge(*sdec_f(it, sc))
                        nc.vector.tensor_tensor(st[:], sdec[:], heads(bank("su", sc)), ALU.add).then_inc(s_f.sem, 1)
                        dve.wait_ge(*job["mv"](it, sc))
                        dve.wait_ge(*ao_f(it, sc))
                        nc.vector.tensor_tensor(ao[:], ao[:], heads(bank("mv", sc)), ALU.add).then_inc(o_f.sem, 1)
                    if sc is not None and q == 3:
                        dve.wait_ge(*job["ot"](it, sc))
                        dve.wait_ge(*z_f(it, 3))
                        yo = y32[:, 4:8, sc * C:(sc + 1) * C]
                        nc.vector.scalar_tensor_tensor(out=yo, in0=heads(bank("ot", sc)), scalar=vec[:, ONW:ONW + 1], in1=yo,
                                                       op0=ALU.mult, op1=ALU.mult).then_inc(yb_f.sem, 1)
                for m in range(8):
                    dve.wait_ge(*yhi_f(it, m))
                    if m == 0:
                        dve.wait_ge(*job["mv"](it, NC - 1))
                        dve.wait_ge(*ya_f(it, NG - 1))
                        dve.wait_ge(*yb_f(it, NC - 1))
                    nc.vector.tensor_tensor(ylo[:, m], y32[:, m], yhi[:, m].bitcast(F32), ALU.subtract).then_inc(ylo_f.sem, 1)
                front_xn(dve, it)
                for m in range(8):
                    if m >= 1:
                        dve.wait_ge(*job["yt"](it, m - 1))
                        dve.wait_ge(*ylo_f(it, 7))
                        nc.vector.tensor_copy(ytok[:, :, (m - 1) * P:m * P], heads(bank("yt", m - 1))).then_inc(ytok_f.sem, 1)
                    front_lo(dve, it, m)
                dve.wait_ge(*job["yt"](it, 7))
                nc.vector.tensor_copy(ytok[:, :, 7 * P:8 * P], heads(bank("yt", 7))).then_inc(ytok_f.sem, 1)
                dve.wait_ge(*ry_f(it, 0))
                dve.wait_ge(*ytok_f(it, 7))
                for t in range(4):
                    nc.vector.scalar_tensor_tensor(out=ytok[:, t], in0=ytok[:, t], scalar=ry[:, t:t + 1], in1=gpw[:],
                                                   op0=ALU.mult, op1=ALU.mult).then_inc(yn_f.sem, 1)
                dve.wait_ge(*xres_in(it, 0))
                for t in range(4):
                    dve.wait_ge(*yn_f(it, t))
                    nc.vector.tensor_tensor(ytok[:, t], ytok[:, t], xres[:, t], ALU.add).then_inc(yr_f.sem, 1)
            dve.wait_ge(*s_f(NB - 1, NC - 1))
            dve.wait_ge(*hist_out(NB - 1, NQ - 1))
            dve.wait_ge(*u_out(NB - 1, NG - 1))
            dve.nop().then_inc(s_end, 1)

            dve.wait_ge(sm_r, 2)
            nc.vector.tensor_scalar(ys[:], xs[:], s8[:, 2:3], None, ALU.mult).then_inc(sm_xn, 1)
            dve.wait_ge(sm_xt, 1)
            nc.vector.tensor_tensor(hs[:], ring[0][:, 0:64].rearrange("p (k s) -> p k s", k=KT), amul[:, :, 1:1 + NS],
                                    ALU.mult).then_inc(sm_h, 1)
            dve.wait_ge(sm_h, 1)
            nc.vector.tensor_tensor(hs[:], hs[:], mod[:, 0:8, 1:1 + NS], ALU.add).then_inc(sm_h, 1)
            dve.wait_ge(sm_st, 48)
            for m in range(2):
                dve.wait_ge(sm_gt, m + 1)
                nc.vector.tensor_tensor(gr8[:, m * 512:(m + 1) * 512], ring[4 + m][0:NS, :], pw8[:, m * 512:(m + 1) * 512],
                                        ALU.mult).then_inc(sm_gr, 1)
            dve.wait_ge(sm_g, 1)
            nc.vector.tensor_tensor(g8[:, 1], ring[1][0:NS, 4:8], vec[0:NS, DTB:DTB + 4], ALU.add).then_inc(sm_g, 1)
            dve.wait_ge(sm_g, 5)
            nc.vector.tensor_scalar(g8[:, 6], g8[:, 0], 0.5, 0.5, ALU.mult, ALU.add).then_inc(sm_g, 1)
            nc.vector.scalar_tensor_tensor(out=g8[:, 3], in0=g8[:, 1], scalar=0.0, in1=g8[:, 2], op0=ALU.max,
                                           op1=ALU.add).then_inc(sm_g, 1)
            dve.wait_ge(sm_g, 7)
            nc.vector.tensor_tensor(g8[:, 4], g8[:, 3], vec[0:NS, NEA:NEA + 4], ALU.mult).then_inc(sm_g, 1)
            dve.wait_ge(sm_g, 9)
            for half_, row in enumerate((6, 5)):
                nc.vector.tensor_tensor(gdg[:, :, half_ * H:(half_ + 1) * H], g8[:, row].unsqueeze(1).to_broadcast([NS, NS, H]),
                                        ident[0:NS, 0:NS].unsqueeze(2).to_broadcast([NS, NS, H]), ALU.mult).then_inc(sm_gd, 1)
            dve.wait_ge(sm_gb, 1)
            nc.vector.tensor_copy(gvb[:].rearrange("p s a h -> p (s a h)"), ring[2][:, 0:64]).then_inc(sm_gb, 1)
            dve.wait_ge(sm_tile, 24)
            nc.vector.tensor_copy(pj[:].rearrange("p t s -> p (t s)"), ring[3][:, 0:192]).then_inc(sm_pj, 1)
            dve.wait_ge(sm_pj, 1)
            cwb = lambda j: cw[:, :, j:j + 1].to_broadcast([P, NQ, NS])
            nc.vector.tensor_tensor(ct[:], pj[:, 0:NQ], cwb(CK - 1), ALU.mult).then_inc(sm_cv, 1)
            for j in range(CK - 1):
                dve.wait_ge(sm_cv, 2 * j + 1)
                nc.vector.tensor_tensor(sqs[:], cbuf[:, :, :, j], cwb(j), ALU.mult).then_inc(sm_cv, 1)
                dve.wait_ge(sm_cv, 2 * j + 2)
                nc.vector.tensor_tensor(ct[:], ct[:], sqs[:], ALU.add).then_inc(sm_cv, 1)
            nc.vector.tensor_copy(cnew[:, :, :, 0:CK - 2], cbuf[:, :, :, 1:CK - 1])
            nc.vector.tensor_copy(cnew[:, :, :, CK - 2], pj[:, 0:NQ]).then_inc(sm_new, 1)
            nc.vector.tensor_copy(pnew[:, :, :, 0:PB - 1], pbuf[:, :, :, 1:PB])
            nc.vector.tensor_copy(pnew[:, :, :, PB - 1], pj[:, 20:24]).then_inc(sm_new, 1)
            for g in range(NG):
                w = 2 << g
                nc.vector.tensor_reduce(pls[:, g], pbuf[:, g, :, PB - (w - 1):PB], AX.X, ALU.add).then_inc(sm_pl, 1)
            dve.wait_ge(sm_pl, 4)
            nc.vector.tensor_tensor(pls[:], pls[:], pj[:, 20:24], ALU.add).then_inc(sm_pl, 1)
            dve.wait_ge(sm_pl, 5)
            for g in range(NG):
                nc.vector.scalar_tensor_tensor(out=pls[:, g], in0=pls[:, g], scalar=1.0 / (2 << g), in1=pj[:, 20 + g],
                                               op0=ALU.mult, op1=ALU.subtract).then_inc(sm_pl, 1)
            dve.wait_ge(sm_z, 1)
            nc.vector.scalar_tensor_tensor(out=zs[:], in0=zs[:], scalar=1.0, in1=pj[:, 12:20], op0=ALU.add,
                                           op1=ALU.mult).then_inc(sm_z, 1)
            dve.wait_ge(sm_plp, 1)
            dve.wait_ge(sm_z, 2)
            for g in range(NG):
                nc.vector.scalar_tensor_tensor(out=ym[:, g], in0=ring[4][:, g * NS:(g + 1) * NS], scalar=vec[:, PSC + g:PSC + g + 1],
                                               in1=zs[:, 4 + g], op0=ALU.mult, op1=ALU.mult).then_inc(sm_ym, 1)
            dve.wait_ge(sm_cv, 8)
            nc.vector.tensor_tensor(sqs[:, 0:8], cs[:, 0:8], cs[:, 0:8], ALU.mult)
            nc.vector.tensor_tensor(sqs[:, 8:12], cs[:, 0:4], cs[:, 4:8], ALU.mult).then_inc(sm_s2, 1)
            for e in range(2):
                nc.vector.tensor_copy(kq[:, :, :, e].rearrange("p s h -> p h s"), cs[:, 4 * e:4 * e + 4]).then_inc(sm_s2, 1)
            dve.wait_ge(sm_s2p, 1)
            nc.vector.tensor_scalar(sst[:, 0:8], ring[5][:, 0:64].rearrange("p (t s) -> p t s", t=8), EPS, None,
                                    ALU.add).then_inc(sm_rk, 1)
            nc.vector.tensor_copy(sst[:, 8:12].rearrange("p t s -> p (t s)"), ring[5][:, 64:96]).then_inc(sm_rk, 1)
            dve.wait_ge(sm_kv, 1)
            dve.wait_ge(sm_rk, 3)
            t0, t1 = (ring[0][:, 0:64].rearrange("p (s h e) -> p e h s", s=NS, h=H)[:, e] for e in range(2))
            be, eg_ = (gvb[:, :, e].rearrange("p s h -> p h s") for e in range(2))
            nc.vector.tensor_tensor(dl[:, 0], t0, eg_, ALU.mult).then_inc(sm_d, 1)
            nc.vector.tensor_tensor(dl[:, 1], t1, eg_, ALU.mult).then_inc(sm_d, 1)
            dve.wait_ge(sm_d, 1)
            nc.vector.tensor_tensor(dl[:, 0], dl[:, 0], rk[:, 1], ALU.mult).then_inc(sm_d, 1)
            dve.wait_ge(sm_d, 3)
            nc.vector.tensor_tensor(dl[:, 0], cs[:, 8:12], dl[:, 0], ALU.subtract).then_inc(sm_d, 1)
            dve.wait_ge(sm_d, 4)
            nc.vector.tensor_tensor(dl[:, 0], dl[:, 0], be, ALU.mult).then_inc(sm_d, 1)
            dve.wait_ge(sm_d, 5)
            nc.vector.tensor_tensor(dl[:, 2].rearrange("p h s -> p (h s)").rearrange("p (s h) -> p h s", h=H), dl[:, 0], rk[:, 1],
                                    ALU.mult).then_inc(sm_d, 1)
            dve.wait_ge(sm_d, 6)
            dps = dl[:, 2].rearrange("p h s -> p (h s)").rearrange("p (s h) -> p h s", h=H)
            nc.vector.tensor_tensor(dl[:, 0], dps, sst[:, 8:12], ALU.mult).then_inc(sm_o, 1)
            dve.wait_ge(sm_o, 1)
            nc.vector.tensor_tensor(dl[:, 1], dl[:, 1], dl[:, 0], ALU.add).then_inc(sm_o, 1)
            dve.wait_ge(sm_o, 2)
            nc.vector.tensor_tensor(dl[:, 3], dl[:, 1], dl[:, 1], ALU.mult).then_inc(sm_o, 1)
            dve.wait_ge(sm_dt, 1)
            nc.vector.tensor_copy(drow[:].rearrange("p a c -> p (a c)"), ring[2][0:32, 0:256]).then_inc(sm_dt, 1)
            dve.wait_ge(sm_dt, 2)
            nc.vector.tensor_tensor(krow[:], drow[:, 0].unsqueeze(1).to_broadcast([32, 32, P]),
                                    ident[0:32, 0:32].unsqueeze(2).to_broadcast([32, 32, P]), ALU.mult).then_inc(sm_dt, 1)
            dve.wait_ge(sm_on, 1)
            nc.vector.tensor_scalar(rk[:, 0], ring[1][:, 0:32].rearrange("p (h s) -> p h s", h=H), 1.0 / P, None,
                                    ALU.mult).then_inc(sm_on, 1)
            nc.vector.tensor_scalar(dl[:, 0], sst[:, 4:8], EPS * P, None, ALU.mult).then_inc(sm_on, 1)
            dve.wait_ge(sm_on, 3)
            nc.vector.tensor_tensor(rk[:, 0], rk[:, 0], dl[:, 0], ALU.add).then_inc(sm_on, 1)
            dve.wait_ge(sm_on, 5)
            nc.vector.tensor_tensor(dl[:, 1], dl[:, 1], rk[:, 1], ALU.mult).then_inc(sm_on, 1)
            dve.wait_ge(sm_on, 6)
            nc.vector.scalar_tensor_tensor(out=ym[:, 4:8], in0=dl[:, 1], scalar=vec[:, ONW:ONW + 1], in1=zs[:, 0:4], op0=ALU.mult,
                                           op1=ALU.mult).then_inc(sm_ym, 1)
            for r in range(NS):
                dve.wait_ge(sm_op, r + 1)
                if r == 0:
                    dve.wait_ge(sm_kv, 1)
                nc.vector.tensor_tensor(ssm[:, r], ssm[:, r], gvb[:, r, 1].unsqueeze(2).to_broadcast([P, H, P]),
                                        ALU.mult).then_inc(sm_oe, 1)
                dve.wait_ge(sm_oe, r + 1)
                nc.vector.tensor_tensor(ssm[:, r], ssm[:, r], heads(acc[r % 2]), ALU.add).then_inc(sm_snew, 1)
            dve.wait_ge(sm_tile, NW)
            nc.vector.tensor_copy(hs[:].rearrange("p k s -> p (k s)"), ring[3][:, 0:64]).then_inc(sm_ot, 1)
            for m in range(2):
                dve.wait_ge(sm_yt, m + 1)
                nc.vector.tensor_copy(ys[:, m * 512:(m + 1) * 512], ring[4 + m][0:NS, :]).then_inc(*((sm_y, 1) if m else (sm_ot, 1)))
            dve.wait_ge(sm_y, 3)
            dve.wait_ge(sm_gr, 2)
            nc.vector.scalar_tensor_tensor(out=ys[:], in0=ys[:], scalar=s8[:, 6:7], in1=gr8[:], op0=ALU.mult,
                                           op1=ALU.mult).then_inc(sm_y, 1)
            dve.wait_ge(sm_y, 4)
            nc.vector.tensor_tensor(ys[:], ys[:], xs[:], ALU.add).then_inc(sm_y, 1)

        def held(pool):
            pool.nop().then_inc(pool_held, 1)

        def front_rx(pool, it):
            pool.wait_ge(*xsq(it, 3))
            if it is not PROLOGUE:
                pool.wait_ge(*xn(it, -1))
            held(pool)
            nc.gpsimd.tensor_scalar(rx0[:], ssx[:], 1.0 / DM, EPS, ALU.mult, ALU.add).then_inc(rx_0.sem, 1)
            pool.wait_ge(*rx_0(it, 0))
            nc.gpsimd.tensor_tensor(rx[:], rx0[:], mhalf[:, 0:4], ALU.pow).then_inc(rx_f.sem, 1)

        def front_hi(pool, it, m):
            pool.wait_ge(*h_f(it, m))
            held(pool)
            nc.gpsimd.tensor_copy(hhi[:, m], htmp[:, m % 2]).then_inc(h_hi.sem, 1)

        @block.gpsimd
        def _(pool):
            for ev in (w_lo, hist_in, hist_out, sk_0, sk_f, odb_0, u_in, u_out, u_add, win_f, ftab_f, gb_in,
                       sdec_f, o_n0, o_n, o_sq, o_s, ry_0, ry_f):
                pool.nop().then_inc(ev.sem, ev.per)
            pool.dma_start(poolw[:], a["pool_w"]).then_inc(y_out.sem, 16)
            nc.gpsimd.memset(half[:], 0.5)
            nc.gpsimd.memset(mhalf[:], -0.5).then_inc(s_modc, 1)
            pool.wait_ge(s_modc, 1)
            front_rx(pool, PROLOGUE)
            for m in range(8):
                front_hi(pool, PROLOGUE, m)
            for t in range(2):
                pool.wait_ge(*w_hi(0, t))
                nc.gpsimd.tensor_tensor(wlo[:, t], wraw[:, t], whi[:, t].bitcast(F32), ALU.subtract).then_inc(w_lo.sem, 1)

            def split_lo(it, t):
                pool.wait_ge(*w_hi(it + (t + 1) // NW, (t + 1) % NW))
                nc.gpsimd.tensor_tensor(wlo[:, (t + 1) % 2], wraw[:, (t + 1) % 2], whi[:, (t + 1) % 2].bitcast(F32),
                                        ALU.subtract).then_inc(w_lo.sem, 1)

            def u_tile(it, t):
                g = t - UA
                u = ubuf[:, g % 2]
                pool.wait_ge(*pooled_f(it, g - 2))
                pool.wait_ge(*u_out(it, g - 2))
                held(pool)
                nc.gpsimd.tensor_copy(u[:, 0:PB], uhist[:, g]).then_inc(u_in.sem, 1)
                pool.wait_ge(*u_in(it, g))
                pool.wait_ge(*u_f(it, g))
                held(pool)
                nc.gpsimd.tensor_copy(uhist[:, g], u[:, BT:BT + PB]).then_inc(u_out.sem, 1)
                src, base = u, g * (g + 1) // 2
                for s in range(g + 1):
                    dst = win[:, (g + g - s) % 2]
                    lo = (2 << s) - 1
                    if s:
                        pool.wait_ge(*u_add(it, base + s - 1))
                    elif g:
                        pool.wait_ge(*u_add(it, base - 1))
                    if s == 0 or s == 1:
                        pool.wait_ge(*pooled_f(it, g - 1))
                        pool.wait_ge(*pooled_f(it, g - 2))
                        pool.wait_ge(*win_f(it, g - 1))
                    nc.gpsimd.tensor_tensor(dst[:, lo:], src[:, lo:], src[:, lo - (1 << s):BT + PB - (1 << s)],
                                            ALU.add).then_inc(u_add.sem, 1)
                    src = dst
                pool.wait_ge(*u_add(it, base + g))
                pool.wait_ge(*ftab_f(it, -1))
                nc.gpsimd.tensor_tensor(src[:, PB:PB + 16], src[:, PB:PB + 16], ftab[:, g], ALU.mult).then_inc(win_f.sem, 1)

            pool.wait_ge(s_prm2, 128)
            pool.wait_ge(s_const, 64)
            pool.wait_ge(s_pre, 1)
            with pool.Fori(0, NB) as it:
                for t in range(NQ):
                    pool.wait_ge(*conv(it, t - 2))
                    pool.wait_ge(*hist_out(it, t - 2))
                    held(pool)
                    nc.gpsimd.tensor_copy(raw[:, t % 2, 0:CK - 1], hist[:, t]).then_inc(hist_in.sem, 1)
                    if t:
                        split_lo(it, t)
                    pool.wait_ge(*hist_in(it, t))
                    pool.wait_ge(*raw_f(it, t))
                    held(pool)
                    nc.gpsimd.tensor_copy(hist[:, t], raw[:, t % 2, BT:BT + CK - 1]).then_inc(hist_out.sem, 1)
                pool.wait_ge(*ss_ev(it, 7))
                pool.wait_ge(*sk_f(it, -1))
                held(pool)
                nc.gpsimd.tensor_scalar(sk0[:], ssb[:, 0:4].rearrange("p h c -> p c h"), EPS, None, ALU.add).then_inc(sk_0.sem, 1)
                pool.wait_ge(*sk_0(it, 0))
                pool.wait_ge(*rv_f(it, -1))
                nc.gpsimd.tensor_tensor(sk[:].rearrange("p c h -> p (c h)"), sk0[:].rearrange("p c h -> p (c h)"), half[:], ALU.pow).then_inc(sk_f.sem, 1)
                pool.wait_ge(*o_n0(it, -1))
                held(pool)
                nc.gpsimd.tensor_scalar(odb[:], ssb[:, 4:8].rearrange("p h c -> p c h"), EPS, EPS * P, ALU.add, ALU.mult).then_inc(odb_0.sem, 1)
                for c, p, sc, q, thirds in PLAN:
                    if c is not None and p == 0:
                        pool.wait_ge(*job["gb"](it, c - 1))
                        pool.wait_ge(*g_g(it, 0))
                        held(pool)
                        nc.gpsimd.tensor_copy(gb4[:], bc(gg[:, c])).then_inc(gb_in.sem, 1)
                    for n in thirds:
                        if n < 36 and n % 3 == 0:
                            split_lo(it, 12 + n // 3)
                        if n % 3 == 2 and UA <= 12 + n // 3 < OUT:
                            u_tile(it, 12 + n // 3)
                    if sc is not None and q == 0:
                        pool.wait_ge(*g_eg(it, 0))
                        pool.wait_ge(*s_f(it, sc - 1))
                        nc.gpsimd.tensor_tensor(sdec[:], st[:], bc(eg[:, 1, sc]), ALU.mult).then_inc(sdec_f.sem, 1)
                    if sc is not None and q == 2:
                        pool.wait_ge(*o_sq4(it, 4 * sc + 3))
                        pool.wait_ge(*o_n(it, sc - 1))
                        pool.wait_ge(*odb_0(it, 0))
                        held(pool)
                        nc.gpsimd.tensor_scalar(on0[:], oss[:], 1.0 / P, None, ALU.mult).then_inc(o_n0.sem, 1)
                        pool.wait_ge(*o_n0(it, sc))
                        nc.gpsimd.tensor_tensor(on0[:], on0[:], odb[:, sc], ALU.add).then_inc(o_n.sem, 1)
                        pool.wait_ge(*o_n(it, sc))
                        pool.wait_ge(*o_s(it, sc - 1))
                        nc.gpsimd.tensor_tensor(on[:], on0[:], mhalf[:, 0:H], ALU.pow).then_inc(o_sq.sem, 1)
                        pool.wait_ge(*o_sq(it, sc))
                        nc.gpsimd.tensor_tensor(ao[:], ao[:], bc(on[:]), ALU.mult).then_inc(o_s.sem, 1)
                front_rx(pool, it)
                for m in range(8):
                    split_lo(it, OUT + m)
                    if m == 0:
                        pool.wait_ge(*proj(it, OUT - 1))
                    front_hi(pool, it, m)
                split_lo(it, NW)
                pool.wait_ge(*ysq(it, 3))
                pool.wait_ge(*ry_f(it, -1))
                held(pool)
                nc.gpsimd.tensor_scalar(ry0[:], ssy[:], 1.0 / DM, EPS, ALU.mult, ALU.add).then_inc(ry_0.sem, 1)
                pool.wait_ge(*ry_0(it, 0))
                pool.wait_ge(*yn_f(it, -1))
                nc.gpsimd.tensor_tensor(ry[:], ry0[:], mhalf[:, 0:4], ALU.pow).then_inc(ry_f.sem, 1)
                for t in range(4):
                    pool.wait_ge(*yr_f(it, t))
                    pool.dma_start(a["y"][it, t], ytok[:, t]).then_inc(y_out.sem, 16)
                pool.wait_ge(*win_f(it, NG - 1))
                held(pool)
                nc.gpsimd.memset(ftab[:], 1.0).then_inc(ftab_f.sem, 1)

            pool.wait_ge(*yr_f(NB - 1, 3))
            pool.wait_ge(*y_out(NB - 1, 3))
            pool.wait_ge(*w_lo(NB, 1))
            nc.gpsimd.memset(spw[:, 0], -0.5)
            nc.gpsimd.memset(spw[:, 1], 0.5).then_inc(s_modc, 1)
            pool.wait_ge(sm_sq, 1)
            nc.gpsimd.tensor_scalar(s8[:, 1:2], s8[:, 0:1], 1.0 / DM, EPS, ALU.mult, ALU.add).then_inc(sm_r, 1)
            pool.wait_ge(sm_r, 1)
            nc.gpsimd.tensor_tensor(s8[:, 2:3], s8[:, 1:2], mhalf[0:NS, 0:1], ALU.pow).then_inc(sm_r, 1)
            pool.wait_ge(sm_rk, 2)
            pool.wait_ge(s_modc, 2)
            nc.gpsimd.tensor_tensor(rk[:, 1].rearrange("p h s -> p (h s)"), sst[:, 0:4].rearrange("p h s -> p (h s)"), spw[:, 0],
                                    ALU.pow).then_inc(sm_rk, 1)
            pool.wait_ge(sm_on, 4)
            pool.wait_ge(sm_d, 6)
            nc.gpsimd.tensor_tensor(rk[:, 1].rearrange("p h s -> p (h s)"), rk[:, 0].rearrange("p h s -> p (h s)"), spw[:, 0],
                                    ALU.pow).then_inc(sm_on, 1)
            pool.wait_ge(sm_y, 2)
            nc.gpsimd.tensor_scalar(s8[:, 5:6], s8[:, 4:5], 1.0 / DM, EPS, ALU.mult, ALU.add).then_inc(sm_r, 1)
            pool.wait_ge(sm_r, 3)
            nc.gpsimd.tensor_tensor(s8[:, 6:7], s8[:, 5:6], mhalf[0:NS, 0:1], ALU.pow).then_inc(sm_y, 1)

        def front_pe(pe, it, m):
            bank_free(pe, it, "xf", m, (xn, 3))
            for t in range(4):
                last = nc.tensor.transpose(bank("xf", m)[:, t * P:(t + 1) * P], xb[:, t, m * P:(m + 1) * P], ident[:])
            last.then_inc(job["xf"].sem, 1)

        @block.tensor
        def _(pe):
            for ev in [proj] + [e for k, e in job.items() if k != "xf"]:
                pe.nop().then_inc(ev.sem, ev.per)
            pe.wait_ge(s_const, 64)
            pe.wait_ge(s_pre, 1)
            pe.wait_ge(s_cact, 1)
            for m in range(24):
                pe.wait_ge(ada_in[m % 8], 16 * (m // 8 + 1))
                for k in range(KT):
                    last = nc.tensor.matmul(ring[0][:, m * 9:(m + 1) * 9], wada[:, m % 8, k], cin[:, k, :],
                                            start=(k == 0), stop=(k == KT - 1))
                last.then_inc(s_mod, 1)
            pe.wait_ge(s_pre, 2)
            for m in range(8):
                last = nc.tensor.transpose(ring[1 + m // 4][0:1, (m % 4) * P:(m % 4 + 1) * P], mod[:, 16 + m, 0:1], ident[:])
                if m % 4 == 3:
                    last.then_inc(s_tr, 1)
            for m in range(2):
                pe.wait_ge(s_trc, m + 1)
                nc.tensor.matmul(ring[3 + m][:], ones[0:1, :], grow[0:1, m * 512:(m + 1) * 512], start=True,
                                 stop=True).then_inc(s_row, 1)
            pe.wait_ge(s_rowc, 2)
            for m in range(8):
                if m >= BANKS:
                    pe.wait_ge(h_f.sem, m - BANKS + 1)
                front_pe(pe, PROLOGUE, m)

            def tile(it, t, third=None):
                hi, lo = (hhi, hlo) if t < OUT else (yhi, ylo)
                ks = range(KT) if third is None else (range(0, 3), range(3, 6), range(6, 8))[third]
                for k in ks:
                    if k == 0:
                        pe.wait_ge(*w_lo(it, t))
                        tile_reader(pe, it, t)
                        if t == OUT:
                            pe.wait_ge(*ylo_f(it, 7))
                    if t == 0:
                        pe.wait_ge(*h_lo(it, k - 8))
                    nc.tensor.matmul(acc[t % 2][:], whi[:, t % 2, k], hi[:, k], start=(k == 0), stop=False)
                    nc.tensor.matmul(acc[t % 2][:], whi[:, t % 2, k], lo[:, k], start=False, stop=False)
                    last = nc.tensor.matmul(acc[t % 2][:], wlo[:, t % 2, k], hi[:, k], start=False, stop=(k == KT - 1))
                if ks[-1] == KT - 1:
                    last.then_inc(proj.sem, 1)

            def four(it, kind, i, left, right, *needs, n=C):
                bank_free(pe, it, kind, i, *needs)
                for h in range(H):
                    last = nc.tensor.matmul(bank(kind, i)[:, h * n:(h + 1) * n], left(h), right(h), start=True, stop=True)
                last.then_inc(job[kind].sem, 1)

            def turn(it, kind, n, what, *needs):
                bank_free(pe, it, kind, n, *needs)
                for h in range(H):
                    last = nc.tensor.transpose(bank(kind, n)[:, h * C:(h + 1) * C], what(h), ident[:])
                last.then_inc(job[kind].sem, 1)

            with pe.Fori(0, NB) as it:
                for t in range(NQ):
                    tile(it, t)
                    if t == 1:
                        bank_free(pe, it, "gates")
                        for k in range(KT):
                            nc.tensor.matmul(bank("gates")[0:8, :], wgh[:, k], hhi[:, k], start=(k == 0), stop=False)
                            nc.tensor.matmul(bank("gates")[0:8, :], wgh[:, k], hlo[:, k], start=False, stop=False)
                            last = nc.tensor.matmul(bank("gates")[0:8, :], wgl[:, k], hhi[:, k], start=False,
                                                    stop=(k == KT - 1))
                        last.then_inc(job["gates"].sem, 1)
                    if t == 2:
                        bank_free(pe, it, "gt", 0, (g_c, 0))
                        pe.nop().then_inc(pe_held, 1)
                        for c in range(NC):
                            last = nc.tensor.transpose(bank("gt")[:, c * 8:(c + 1) * 8], gsb[:, c * C:(c + 1) * C], ident[0:8, 0:8])
                        last.then_inc(job["gt"].sem, 1)
                    if t == 5:
                        bank_free(pe, it, "gc", 0, (g_g, 0))
                        g16 = gg[:].rearrange("p c h -> p (c h)")
                        nc.tensor.matmul(bank("gc")[:, 0:16], upper[:], g16, start=True, stop=True)
                        nc.tensor.matmul(bank("gc")[:, 16:32], ones[:], g16, start=True, stop=True).then_inc(job["gc"].sem, 1)
                    if t >= 2 and t - 2 < 8:
                        bank_free(pe, it, "ss", t - 2, (sq, t - 2))
                        for c in range(NC):
                            last = nc.tensor.matmul(bank("ss", t - 2)[:, c:c + 1], tmpa[:, t % 2, c * C:(c + 1) * C],
                                                    ones[:, 0:1], start=True, stop=True)
                        last.then_inc(job["ss"].sem, 1)
                for c, p, sc, q, thirds in PLAN:
                    for n in thirds:
                        if n < 36:
                            tile(it, 12 + n // 3, n % 3)
                        g = pool_after(n)
                        if g is not None:
                            bank_free(pe, it, "pool", g, (pooled_f, g))
                            nc.tensor.matmul(bank("pool", g)[:], poolw[:, g], pooled[:, g % 2], start=True,
                                             stop=True).then_inc(job["pool"].sem, 1)
                    if c is not None:
                        s = slice(c * C, (c + 1) * C)
                        if p == 0:
                            turn(it, "kt", c, lambda h: cq[:, h, s], (silu, NQ - 1))
                            turn(it, "vt", c, lambda h: cq[:, 8 + h, s])
                            four(it, "gb", c, lambda h: gb4[:, h], lambda h: upper[:], (gb_in, c))
                        elif p == 1:
                            four(it, "kk", c, lambda h: cq[:, h, s], lambda h: cq[:, h, s])
                            four(it, "qk", c, lambda h: cq[:, h, s], lambda h: cq[:, 4 + h, s])
                        elif p == 2:
                            turn(it, "xt", c, lambda h: yv[:, c % 2, h], (y_1, c))
                        elif p % 2:
                            i = c * NL + (p - 3) // 2
                            x_ready = (x_0, c) if p == 3 else (x_l, c * (NL - 1) + (p - 3) // 2 - 1)
                            sz = LEVELS[(p - 3) // 2]
                            four(it, "w", i, lambda h: lt[:, h], lambda h: head_blocks(xv[:, h], sz, 0), x_ready, n=C // 2)
                        else:
                            lv = (p - 4) // 2
                            sz = LEVELS[lv]
                            i = c * NL + lv
                            ready = [(w_f, i)] + ([(y_l, i - 1)] if lv else [])
                            if lv < NL - 1:
                                four(it, "xx", c * (NL - 1) + lv, lambda h: yv[:, c % 2, h],
                                     lambda h: head_blocks(wb[:, h], sz, 0), *ready, n=C // 2)
                            four(it, "yy", i, lambda h: wb[:, h], lambda h: head_blocks(yv[:, c % 2, h], sz, 1), *ready,
                                 n=C // 2)
                    if sc is not None:
                        s = slice(sc * C, (sc + 1) * C)
                        if q == 0:
                            four(it, "ks", sc, lambda h: cq[:, h, s], lambda h: st[:, h], (s_f, sc - 1))
                            four(it, "qs", sc, lambda h: cq[:, 4 + h, s], lambda h: st[:, h])
                        elif q == 1:
                            four(it, "u", sc, lambda h: yv[:, sc % 2, h], lambda h: rv[:, sc % 2, h],
                                 (r_f, sc), (y_l, sc * NL + NL - 1))
                        elif q == 2:
                            four(it, "su", sc, lambda h: ktok[:, sc % 2, h], lambda h: ve[:, h], (ve_f, sc), (kt_f, sc))
                            four(it, "mv", sc, lambda h: mtb[:, sc % 2, h], lambda h: ub[:, h], (u_c, sc), (mt_f, sc))
                        else:
                            turn(it, "ot", sc, lambda h: ao[:, h], (o_s, sc))
                for m in range(8):
                    tile(it, OUT + m)
                    if m >= 1:
                        turn(it, "yt", m - 1, lambda t: ytt[:, (m - 1) % 2, t * P:(t + 1) * P], (ytt_f, m - 1))
                    front_pe(pe, it, m)
                turn(it, "yt", 7, lambda t: ytt[:, 1, t * P:(t + 1) * P], (ytt_f, 7))

            pe.wait_ge(*yr_f(NB - 1, 3))
            pe.wait_ge(*h_lo(NB - 1, 7))
            pe.wait_ge(*s_f(NB - 1, NC - 1))
            for m in range(8):
                last = nc.tensor.transpose(ring[4 + m // 4][0:NS, (m % 4) * P:(m % 4 + 1) * P], mod[:, 16 + m, 1:1 + NS], ident[:])
                if m % 4 == 3:
                    last.then_inc(sm_gt, 1)
            pe.wait_ge(sm_xn, 1)
            for k in range(KT):
                last = nc.tensor.transpose(ring[0][:, k * NS:(k + 1) * NS], ys[:, k * P:(k + 1) * P], ident[0:NS, 0:NS])
            last.then_inc(sm_xt, 1)
            pe.wait_ge(sm_h, 2)
            for k in range(KT):
                last = nc.tensor.matmul(ring[1][0:NS, 0:8], hs[:, k], wgr[:, k], start=(k == 0), stop=(k == KT - 1))
            last.then_inc(sm_gp, 1)

            def sample_tile(n, rhs, col):
                pe.wait_ge(sm_w[n % 8], 16 * (24 // 8 + n // 8 + 1))
                for k in range(KT):
                    last = nc.tensor.matmul(ring[3][:, col * NS:(col + 1) * NS], wring[:, n % 8, k], rhs[:, k], start=(k == 0),
                                            stop=(k == KT - 1))
                last.then_inc(sm_tile, 1)

            for n in range(24):
                sample_tile(n, hs, n)
            pe.wait_ge(sm_gd, 2)
            nc.tensor.matmul(ring[2][:, 0:64], ones[0:NS, :], gdg[:].rearrange("p s e -> p (s e)"), start=True,
                             stop=True).then_inc(sm_gb, 1)
            pe.wait_ge(sm_pl, 9)
            pe.wait_ge(sm_gr, 2)
            for g in range(NG):
                last = nc.tensor.matmul(ring[4][:, g * NS:(g + 1) * NS], poolw[:, g], pls[:, g], start=True, stop=True)
            last.then_inc(sm_plp, 1)
            pe.wait_ge(sm_s2, 3)
            nc.tensor.matmul(ring[5][:, 0:96], ones[:], sqs[:].rearrange("p t s -> p (t s)"), start=True, stop=True).then_inc(sm_s2p, 1)
            pe.wait_ge(sm_ssm, 16)
            for s in range(NS):
                for h in range(H):
                    col = 2 * (s * H + h)
                    last = nc.tensor.matmul(ring[0][:, col:col + 2], ssm[:, s, h], kq[:, s, h], start=True, stop=True)
            last.then_inc(sm_kv, 1)
            pe.wait_ge(sm_d, 6)
            pe.wait_ge(sm_gb, 2)
            nc.tensor.transpose(ring[2][0:32, 0:P], kq[:, :, :, 0].rearrange("p s h -> p (s h)"), ident[:])
            nc.tensor.transpose(ring[2][0:32, P:2 * P], dl[:, 2].rearrange("p h s -> p (h s)"), ident[:]).then_inc(sm_dt, 1)
            pe.wait_ge(sm_o, 3)
            nc.tensor.matmul(ring[1][:, 0:32], ones[:], dl[:, 3].rearrange("p h s -> p (h s)"), start=True, stop=True).then_inc(sm_on, 1)
            pe.wait_ge(sm_dt, 3)
            for s in range(NS):
                if s >= 2:
                    pe.wait_ge(sm_snew, s - 1)
                for h in range(H):
                    last = nc.tensor.matmul(acc[s % 2][:, h * P:(h + 1) * P], krow[:, s * H + h], drow[:, 1], start=True, stop=True)
                last.then_inc(sm_op, 1)
            pe.wait_ge(sm_ym, 5)
            for n in range(24, NW):
                sample_tile(n, ym, n - 24)
            pe.wait_ge(sm_ot, 1)
            for m in range(8):
                last = nc.tensor.transpose(ring[4 + m // 4][0:NS, (m % 4) * P:(m % 4 + 1) * P], hs[:, m], ident[:])
                if m % 4 == 3:
                    last.then_inc(sm_yt, 1)


def layouts(i):
    import numpy as np

    f = lambda n: np.asarray(i[n])

    def tiles(w):
        return w.reshape(KT, P, -1, P).transpose(2, 1, 0, 3)

    w_in = f("w_in")[0]
    u, za, q, k, v, zb = (w_in[:, s:s + 512] for s in range(0, 3072, 512))
    x = f("x_prompt")[0].reshape(NB, 4, P, DM).transpose(0, 2, 1, 3)
    perm = lambda w: np.concatenate([w[..., 512:1024], w[..., 0:512], w[..., 1024:1536]], -1)
    j = np.arange(P)
    lm = []
    for s in (1,) + LEVELS:
        lm.append((j[:, None] // (2 * s) == j[None, :] // (2 * s)) & (j[:, None] // s < j[None, :] // s))
    lm[1:] = [m.T for m in lm[1:]]
    cnt = np.minimum(np.arange(16)[None] + 1, 2 << np.arange(NG)[:, None])
    ftab = (2 << np.arange(NG))[:, None] / cnt
    return {
        "x": np.concatenate([x, x[:1]]),
        "c_all": np.concatenate([f("c_prompt"), f("c_sample")]).T.reshape(KT, P, 1 + NS).transpose(1, 0, 2),
        "w": np.concatenate([tiles(np.concatenate([k, q, v, zb, za, u], 1)), tiles(f("w_out")[0])]),
        "w_gate": w_in[:, 3072:].reshape(KT, P, 8).transpose(1, 0, 2),
        "w_ada": tiles(f("w_ada")[0]),
        "b_ada": f("b_ada")[0].reshape(24, P).T,
        "pre_w": f("pre_norm_w")[0].reshape(KT, P).T,
        "post_w": f("post_norm_w"),
        "conv_w": perm(f("conv_w")[0]).reshape(CK, NQ, P).transpose(2, 1, 0),
        "pool_w": f("pool_w")[0].transpose(1, 0, 2),
        "pool_scale": f("pool_scale")[0].reshape(NG, P).T,
        "a_log": f("a_log"), "dt_bias": f("dt_bias"),
        "o_norm": f("o_norm_w")[0].reshape(P, 1),
        "ident": np.eye(P, dtype=np.float32),
        "upper": (j[:, None] <= j[None, :]).astype(np.float32),
        "dmask": np.where(j[:, None] <= j[None, :], 0.0, -30000.0).astype(np.float32),
        "lmask": np.stack(lm, 1).astype(np.float32),
        "ftab": np.broadcast_to(ftab.astype(np.float32), (P, NG, 16)),
        "xs": f("x_sample").reshape(NS, DM),
        "s_conv": perm(f("state_conv")[0]).reshape(NS, CK - 1, NQ, P).transpose(3, 2, 0, 1),
        "s_pool": f("state_pool")[0].reshape(NS, PB, NG, P).transpose(3, 2, 0, 1),
        "s_ssm": f("state_ssm")[0].transpose(2, 0, 1, 3),
    }


OUTS = {"y": (NB, 4, P, DM), "o_pool": (P, NG, PB), "o_conv": (P, NQ, CK - 1), "o_ssm": (P, H, P),
        "ys": (NS, DM), "o_spool": (P, NG, NS, PB), "o_sconv": (P, NQ, NS, CK - 1), "o_sssm": (P, NS, H, P)}


def gather(r):
    import numpy as np

    def unperm(h):
        return np.concatenate([h[4:8], h[0:4], h[8:12]])

    return (
        r["y"].transpose(0, 1, 2, 3).reshape(1, SEQ, DM),
        r["ys"].reshape(NS, 1, DM),
        r["o_pool"].transpose(2, 1, 0).reshape(1, 1, PB, NG * P),
        unperm(r["o_conv"].transpose(1, 2, 0)).transpose(1, 0, 2).reshape(1, 1, CK - 1, NQ * P),
        r["o_ssm"].transpose(1, 0, 2)[None, None],
        r["o_spool"].transpose(2, 3, 1, 0).reshape(1, NS, PB, NG * P),
        unperm(r["o_sconv"].transpose(1, 2, 3, 0)).transpose(1, 2, 0, 3).reshape(1, NS, CK - 1, NQ * P),
        r["o_sssm"].transpose(1, 2, 0, 3)[None],
    )


def kernel(**inputs):
    import numpy as _np
    import concourse.bacc as _bacc
    from concourse.bass_utils import run_bass_kernel_spmd as _run

    nc = _bacc.Bacc("TRN2", target_bir_lowering=False, num_devices=1)
    arrays, aps = {}, {}
    for name, value in layouts(inputs).items():
        arrays[f"in_{name}"] = _np.ascontiguousarray(value)
        aps[name] = nc.dram_tensor(f"in_{name}", value.shape, F32, kind="ExternalInput").ap()
    for name, shape in OUTS.items():
        aps[name] = nc.dram_tensor(f"out_{name}", shape, F32, kind="ExternalOutput").ap()
    layer_kernel(nc, aps)
    r = _run(nc, [arrays], core_ids=[0]).results[0]
    return gather({name: r[f"out_{name}"] for name in OUTS})
```

```python
from contextlib import ExitStack

import concourse.bass as bass
from concourse import mybir

F32 = mybir.dt.float32
F32R = mybir.dt.float32r
BF16 = mybir.dt.bfloat16
ALU = mybir.AluOpType
ACT = mybir.ActivationFunctionType
AX = mybir.AxisListType

P = 128
DM = 1024
KT = DM // P
SEQ = 2048
BT = 512
NB = SEQ // BT
C = 128
NC = BT // C
H = 4
NQ = 12
NG = 4
CK = 4
PB = 15
NS = 8
NW = 32
ZB, ZA, UA, OUT = 12, 16, 20, 24
EPS = 1e-6
LEVELS = (2, 4, 8, 16, 32, 64)
NL = len(LEVELS)
NPREP = 3 + 2 * NL
SLOTS = (NC + 1) * NPREP
THIRDS = 42
BANKS = 6


class Event:

    def __init__(self, sem, per, step=1, credit=None, at=0, turns=1):
        self.sem, self.per, self.step = sem, per, step
        self.credit = per if credit is None else credit
        self.at, self.turns = at, turns

    def rank(self, n):
        return n * self.turns + self.at

    def __call__(self, it, n):
        return self.sem, (it * (self.per * self.turns * self.step)
                          + (self.credit * self.turns + self.rank(n) + 1) * self.step)


def scan_step(p):
    at = [1 + i * ((NPREP - 2) // 4) for i in range(4)]
    return at.index(p) if p in at else None


def slot_plan():
    out, n = [], 0
    for k in range(SLOTS):
        r, p = divmod(k, NPREP)
        q = scan_step(p)
        upto = min(THIRDS, (k + 1) * THIRDS // (SLOTS - NPREP) + 1)
        out.append((r if r < NC else None, p, r - 1 if r > 0 and q is not None else None, q,
                    list(range(n, upto))))
        n = upto
    return out


PLAN = slot_plan()


def pool_after(n):
    g, rest = divmod(n - 3 * (UA - 12) - 8, 3)
    return g if rest == 0 and 0 <= g < NG else None


SAMPLE_SLOT = {"conv": 2, "square": 4, "root": 5, "delta": 9, "rows": 11, "mean": 12, "gate": 38, "pool": 54,
               "pooled": 56, "mixed": 57}
SAMPLE_JOBS = ("sp", "sg", "sb", "s2", "kv", "dt", "son", "spl", "sgt", "sop", "syt")


def absent(kind, last):
    return kind == "xf" if last else kind in SAMPLE_JOBS


def psum_jobs():
    jobs = []
    for t in range(NQ):
        jobs.append(("sp", t))
        if t == 1:
            jobs.append(("gates", 0))
        if t == 2:
            jobs.append(("gt", 0))
        if t == 5:
            jobs.append(("gc", 0))
        if t >= 2 and t - 2 < 8:
            jobs.append(("ss", t - 2))
        if t == 6:
            jobs.append(("sg", 0))
    jobs.append(("sb", 0))
    for slot, (c, p, sc, q, thirds) in enumerate(PLAN):
        for n in thirds:
            if n < 36 and n % 3 == 0:
                jobs.append(("sp", 12 + n // 3))
            if pool_after(n) is not None:
                jobs.append(("pool", pool_after(n)))
        if c is not None:
            if p == 0:
                jobs += [("kt", c), ("vt", c), ("gb", c)]
            elif p == 1:
                jobs += [("kk", c), ("qk", c)]
            elif p == 2:
                jobs.append(("xt", c))
            elif p % 2:
                jobs.append(("w", c * NL + (p - 3) // 2))
            else:
                lv = (p - 4) // 2
                if lv < NL - 1:
                    jobs.append(("xx", c * (NL - 1) + lv))
                jobs.append(("yy", c * NL + lv))
        if sc is not None:
            jobs += {0: [("ks", sc), ("qs", sc)], 1: [("u", sc)], 2: [("su", sc), ("mv", sc)],
                     3: [("ot", sc)]}[q]
        jobs += {"square": [("s2", 0), ("kv", 0)], "rows": [("dt", 0), ("son", 0)], "pooled": [("spl", 0)]}.get(
            next((n for n, at in SAMPLE_SLOT.items() if at == slot), None), [])
    for m in range(8):
        jobs.append(("sp", OUT + m))
        if m >= 1:
            jobs.append(("yt", m - 1))
        jobs.append(("xf", m))
        jobs.append(("sop", m))
    jobs += [("yt", 7), ("sgt", 0), ("sgt", 1), ("syt", 0), ("syt", 1)]
    return jobs


JOBS = psum_jobs()
JOB_AT = {job: n for n, job in enumerate(JOBS)}


def sample_plan_steps():
    steps = {"conv": ["cv0", "cv1", "cv2", "cv3", "cv4", "cv5", "cv6"], "square": ["sq0", "sq1", "kq0", "kq1"],
             "root": ["sst0", "sst1", "d0", "d1"], "delta": ["d2", "d3", "d4", "d5", "o0", "o1", "o2"],
             "mean": ["drow", "ms0", "ms1", "ms2"], "gate": ["zs", "on", "ymb"],
             "pool": [f"pl{i}" for i in range(9)], "mixed": ["ym0", "ym1", "ym2", "yma"]}
    out = []
    for slot, (c, p, sc, q, thirds) in enumerate(PLAN):
        out += [f"pj{12 + n // 3}" for n in thirds if n < 36 and n % 3 == 0]
        for name, at in SAMPLE_SLOT.items():
            if at == slot:
                out += steps.get(name, [])
    return out


def sample_out_steps():
    out = []
    for m in range(9):
        out += [f"pj{OUT + m}"] if m < 8 else []
        out += ["krow"] if m == 0 else []
        out += [f"se{m - 1}", f"sn{m - 1}"] if m else []
        out += ["gr0", "gr1"] if m == 8 else []
    return out


SAMPLE_STEPS = {
    "pe": ["hs"] + [f"{kind}{n}" for kind, n in JOBS if kind in SAMPLE_JOBS],
    "act": ["x_sq", "g_tanh", "g_abs", "g_exp", "g_ln", "g_eg", "silu", "z_tanh", "y_sq"],
    "pool": ["rx0", "rx", "half", "rk", "rstd", "ry0", "ry"],
    "dve": (["xn", "h0", "h"] + [f"pj{t}" for t in range(8)] + ["g_a"] + ["pj8"] + ["g_beta", "g_sp", "g_g"] + ["pj9", "pj10"]
            + ["g_d0", "g_d1", "pj11", "gvb"] + sample_plan_steps() + sample_out_steps() + ["ys0", "ys1", "yn", "yr"]),
}


def layer_kernel(nc, a):
    ctx = ExitStack()
    with ctx:
        def sb(name, shape, dt=F32):
            return ctx.enter_context(nc.sbuf_tensor(name, shape, dt))

        def over(name, base, offset, shape, dt=F32):
            return nc.alloc_sbuf_tensor_at(name, shape, dt, offset=base + offset)

        def region(name, nbytes):
            sb(name, [P, nbytes // 4])
            return nc.sbuf_base - nbytes

        def event(name, per, step=1, credit=None):
            return Event(ctx.enter_context(nc.semaphore(name)), per, step, credit)

        def chain(name, per, *steps):
            shared = ctx.enter_context(nc.semaphore(name))
            return [Event(shared, per, at=i, turns=len(steps)) for i in range(len(steps))]

        def sem(name):
            return ctx.enter_context(nc.semaphore(name))

        KB = 1024
        ra = region("region_a", 32 * KB)
        cq = over("cq", ra, 0, [P, NQ, BT])
        mtb = over("mtb", ra, 24 * KB, [P, 2, H, C])
        yv = over("yv", ra, 28 * KB, [P, 2, H, C])
        yhi = over("yhi", ra, 0, [P, KT, BT], F32R)
        ylo = over("ylo", ra, 16 * KB, [P, KT, BT], F32R)
        rb = region("region_b", 16 * KB)
        ktok = over("ktok", rb, 0, [P, 2, H, C])
        rv = over("rv", rb, 4 * KB, [P, 2, H, C])
        ub = over("ub", rb, 8 * KB, [P, H, C])
        ve = over("ve", rb, 10 * KB, [P, H, C])
        ao = over("ao", rb, 12 * KB, [P, H, C])
        tks = over("tks", rb, 14 * KB, [P, H, C])
        xres = over("xres", rb, 0, [P, 4, DM])
        rc = region("region_c", 16 * KB)
        y32 = over("y32", rc, 0, [P, KT, BT])
        ytok = over("ytok", rc, 0, [P, 4, DM])
        rd = region("region_d", 32 * KB)
        hhi = over("hhi", rd, 0, [P, KT, BT], F32R)
        hlo = over("hlo", rd, 16 * KB, [P, KT, BT], F32R)
        re_ = region("region_e", 40 * KB)
        rf = region("region_f", 4 * KB)
        htmp = over("htmp", rf, 0, [P, 2, BT])
        rg = region("region_g", 4 * KB)
        cacc = over("cacc", rg, 0, [P, 2, BT])
        rh = region("region_h", 2 * KB)
        gsb = over("gsb", rh, 0, [8, BT])
        wraw = over("wraw", re_, 0, [P, 2, KT, P])
        whi = over("whi", re_, 8 * KB, [P, 2, KT, P], F32R)
        wlo = over("wlo", re_, 16 * KB, [P, 2, KT, P], F32R)
        xb = over("xb", re_, 24 * KB, [P, 4, DM])

        tmpa = sb("tmpa", [P, 2, BT])
        ytt = sb("ytt", [P, 2, BT])
        raw = sb("raw", [P, 2, BT + CK - 1])
        ubuf = sb("ubuf", [P, 2, BT + PB])
        win = sb("win", [P, 2, BT + PB])
        pooled = sb("pooled", [P, 2, BT])
        dcy = sb("dcy", [P, H, C])
        lt = sb("lt", [P, H, C])
        xv = sb("xv", [P, H, C])
        wb = sb("wb", [P, H, C])
        st = sb("st", [P, H, C])
        sdec = sb("sdec", [P, H, C])
        gb4 = sb("gb4", [P, H, C])
        junk = sb("junk", [P, DM], BF16)
        hist = sb("hist", [P, NQ, CK - 1])
        uhist = sb("uhist", [P, NG, PB])
        ident = sb("ident", [P, P])
        upper = sb("upper", [P, P])
        ones = sb("ones", [P, P])
        dmask = sb("dmask", [P, P])
        lmask = sb("lmask", [P, NL + 1, P])
        gpw = sb("gpw", [P, DM])
        poolw = sb("poolw", [P, NG, P])
        wgr = sb("wgr", [P, KT, 8])
        wgh = sb("wgh", [P, KT, 8], F32R)
        wgl = sb("wgl", [P, KT, 8], F32R)
        cw = sb("cw", [P, NQ, CK])
        vec = sb("vec", [P, 64])
        bada = sb("bada", [P, 24])
        ftab = sb("ftab", [P, NG, 16])
        cin = sb("cin", [P, KT, 1 + NS])
        mod = sb("mod", [P, 24, 1 + NS])
        amul = sb("amul", [P, KT, 1 + NS])
        wada = [over(f"wada{j}", base, off, [P, KT, BT]) for j, (base, off) in enumerate(
            ((rd, 0), (rd, 16 * KB), (ra, 0), (ra, 16 * KB), (rc, 0), (rb, 0)))]
        rows9 = [t[0:1 + NS, j] for t in (tmpa, ytt, pooled) for j in range(2)]
        grow = ubuf[0:1].rearrange("p a b -> p (a b)")[:, 0:DM]
        pwr = win[0:1].rearrange("p a b -> p (a b)")[:, 0:DM]
        ssx = sb("ssx", [P, 4]); rx0 = sb("rx0", [P, 4]); rx = sb("rx", [P, 4])
        ssy = sb("ssy", [P, 4]); ry0 = sb("ry0", [P, 4]); ry = sb("ry", [P, 4])
        half = sb("half", [P, 16]); mhalf = sb("mhalf", [P, 16])
        ga = sb("ga", [P, NC, H]); gab = sb("gab", [P, NC, H]); gl1 = sb("gl1", [P, NC, H])
        gsp = sb("gsp", [P, NC, H]); gg = sb("gg", [P, NC, H])
        btt = sb("btt", [P, NC, H]); beta = sb("beta", [P, NC, H])
        gcs = sb("gcs", [P, 2, NC, H]); eg = sb("eg", [P, 2, NC, H])
        gd = sb("gd", [P, NC, H]); ekg = sb("ekg", [P, NC, H])
        ssb = sb("ssb", [P, 8, NC])
        kk1 = sb("kk1", [P, NC, H]); kk2 = sb("kk2", [P, NC, H]); bb = sb("bb", [P, NC, H]); bke = sb("bke", [P, NC, H])
        sk0 = sb("sk0", [P, NC, H]); sk = sb("sk", [P, NC, H]); odb = sb("odb", [P, NC, H])
        oss = sb("oss", [P, H]); on0 = sb("on0", [P, H]); on = sb("on", [P, H])

        hs = sb("hs", [P, KT, NS])
        g8, gdg, s8 = sb("g8", [NS, 8, H]), sb("gdg", [NS, NS, 2 * H]), sb("s8", [NS, 8])
        xrow = gpw[0:NS, :]
        ssm = over("ssm", re_, 24 * KB, [P, NS, H, P])
        cbuf = over("cbuf", rf, 0, [P, CK - 1, NQ, NS])
        pbuf = over("pbuf", rf, 1152, [P, PB, NG, NS])
        pj = over("pj", rf, 3072, [P, 24, NS])
        gvb = over("gvb", rf, 3840, [P, NS, 2, H])
        ct, cs = over("ct", rg, 0, [P, NQ, NS]), over("cs", rg, 384, [P, NQ, NS])
        sqs = over("sqs", rg, 768, [P, NQ, NS])
        sst = over("sst", rg, 1152, [P, NQ, NS])
        kq = over("kq", rg, 1536, [P, NS, H, 2])
        zs, ym = over("zs", rg, 1792, [P, 8, NS]), over("ym", rg, 2048, [P, 8, NS])
        pls = over("pls", rg, 2304, [P, NG, NS])
        rk = over("rk", rg, 2432, [P, 2, H, NS])
        dl = over("dl", rg, 2688, [P, 4, H, NS])
        spw = over("spw", rg, 3200, [P, NS * H])
        drow = over("drow", rh, 0, [NS * H, 2, P])
        krow = over("krow", rd, 0, [NS * H, NS * H, P])
        xs, pw8, gr8, ys = (over(n, rd, (16 + 4 * j) * KB, [NS, DM]) for j, n in enumerate(("xs", "pw8", "gr8", "ys")))

        PREW, PSC, ONW, NEA, DTB = 0, 8, 12, 13, 17

        acc = [ctx.enter_context(nc.psum_tensor(f"acc{i}", [P, BT], F32)) for i in range(2)]
        ring = [ctx.enter_context(nc.psum_tensor(f"ring{i}", [P, BT], F32)) for i in range(BANKS)]

        def bank(kind, n=0):
            return ring[JOB_AT[kind, n] % BANKS]

        def heads(t):
            return t[:, :].rearrange("p (h c) -> p h c", h=H)

        def bc(col, n=C):
            return col.unsqueeze(2).to_broadcast([P, H, n])

        def packed(t, s):
            return t[:, 0:H * C // 2].rearrange("p (b s) -> p b s", s=s)

        def half_blocks(t, s, odd):
            return t.rearrange("p h (b two s) -> p (h b) two s", two=2, s=s)[:, :, odd]

        def head_blocks(t, s, odd):
            return t.rearrange("p (b two s) -> p b two s", two=2, s=s)[:, :, odd]

        def level_mask(lv):
            return mbc(lmask[:, 1 + lv])

        def mbc(m):
            return m.unsqueeze(1).to_broadcast([P, H, C])

        x_in = event("x_in", 1, 16)
        xres_in = event("xres_in", 1, 16)
        w_in0, w_in1 = event("w_in0", NW // 2, 16), event("w_in1", NW // 2, 16)
        w_in = [w_in0, w_in1]
        y_out = event("y_out", 4, 16, 1)
        w_hi, w_lo = event("w_hi", NW), event("w_lo", NW)
        proj = event("proj", NW)
        raw_f, hist_in, hist_out = event("raw_f", NQ), event("hist_in", NQ), event("hist_out", NQ)
        conv_a, conv, silu = event("conv_a", 3 * NQ), event("conv", NQ), event("silu", NQ)
        sq = event("sq", 8)
        ss_ev = event("ss_ev", 8)
        g_c, g_y, g_b, g_sp, g_g, gc_f, g_d, k_1, k_2, b_f, bke_f = chain(
            "dve_factors", 1, "g_c", "g_y", "g_b", "g_sp", "g_g", "gc_f", "g_d", "k_1", "k_2", "b_f", "bke_f")
        g_t, g_ab, g_e, g_l, g_eg, g_ekg = chain("act_factors", 1, "g_t", "g_ab", "g_e", "g_l", "g_eg", "g_ekg")
        sk_0, sk_f, odb_0, ry_0, ry_f, ftab_f = chain(
            "pool_factors", 1, "sk_0", "sk_f", "odb_0", "ry_0", "ry_f", "ftab_f")
        tanh_f, z_f = event("tanh_f", 8), event("z_f", 8)
        u_f, u_in, u_out, u_add, win_f = (event("u_f", 4), event("u_in", 4), event("u_out", 4),
                                          event("u_add", 10), event("win_f", 4))
        pooled_f, ya_f = event("pooled_f", 4), event("ya_f", 4)
        kt_f, gb_in, d_e, x_0 = (event(n, NC) for n in ("kt_f", "gb_in", "d_e", "x_0"))
        rv_f, d_1, d_2, d_b, lt_f, mt_f, y_0, y_1 = chain(
            "dve_prep", NC, "rv_f", "d_1", "d_2", "d_b", "lt_f", "mt_f", "y_0", "y_1")
        w_f, y_l, x_l = event("w_f", NC * NL), event("y_l", NC * NL), event("x_l", NC * (NL - 1))
        ks_t, r_f, ao_f, ve_f, s_f, o_f, yb_f = chain(
            "dve_scan", NC, "ks_t", "r_f", "ao_f", "ve_f", "s_f", "o_f", "yb_f")
        o_n0, o_n, o_sq, o_s = chain("pool_norm", NC, "o_n0", "o_n", "o_sq", "o_s")
        sdec_f, u_c = event("sdec_f", NC), event("u_c", NC)
        o_sq4 = event("o_sq4", 4 * NC)
        yhi_f, ylo_f, ytt_f, ytok_f = (event(n, 8) for n in ("yhi_f", "ylo_f", "ytt_f", "ytok_f"))
        ysq, yn_f, yr_f = event("ysq", 4), event("yn_f", 4), event("yr_f", 4)
        xsq, rx_0, rx_f, xn = event("xsq", 4), event("rx_0", 1), event("rx_f", 1), event("xn", 4)
        h_f, h_hi, h_lo = event("h_f", 8), event("h_hi", 8), event("h_lo", 8)
        per_job = {"gates": 1, "gt": 1, "gc": 1, "ss": 8, "pool": 4, "w": NC * NL, "xx": NC * (NL - 1), "yy": NC * NL,
                   "yt": 8, "xf": 8}
        job = {kind: event("job_" + kind, per_job.get(kind, NC)) for kind in dict.fromkeys(k for k, _ in JOBS)}
        reader = {"gates": [g_c], "gt": [g_y, g_t], "gc": [gc_f], "ss": [ss_ev], "pool": [ya_f], "kt": [kt_f], "vt": [rv_f],
                  "gb": [d_1], "kk": [lt_f], "qk": [mt_f], "xt": [x_0], "w": [w_f], "xx": [x_l], "yy": [y_l],
                  "ks": [ks_t], "qs": [ao_f], "u": [u_c], "su": [s_f], "mv": [o_f], "ot": [yb_f],
                  "yt": [ytok_f], "xf": [h_f]}
        one = {"gates", "gc"}

        s_const, s_prm, s_prm2, s_pre, s_end = (sem(n) for n in ("s_const", "s_prm", "s_prm2", "s_pre", "s_end"))
        s_cact, s_mod, s_modc, s_rows, s_tr, s_trc, s_row, s_rowc = (sem(n) for n in (
            "s_cact", "s_mod", "s_modc", "s_rows", "s_tr", "s_trc", "s_row", "s_rowc"))
        ada_in = [sem(f"ada_in{i}") for i in range(6)]
        out_sem = sem("out_sem")
        pool_held, pe_held = sem("pool_held"), sem("pe_held")
        sm_x0, sm_x, sm_st, sm_ssm = (sem(n) for n in ("sm_x0", "sm_x", "sm_st", "sm_ssm"))
        sample_sem = {who: sem("sample_" + who) for who in SAMPLE_STEPS}
        taken = dict.fromkeys(SAMPLE_STEPS, 0)

        def done(who, step):
            return sample_sem[who], SAMPLE_STEPS[who].index(step) + 1

        def step(who, name):
            assert SAMPLE_STEPS[who][taken[who]] == name, (who, name, SAMPLE_STEPS[who][taken[who]])
            taken[who] += 1
            return sample_sem[who], 1

        sample_reader = {"sp": lambda n: done("dve", f"pj{n}"), "sg": lambda n: done("dve", "g_a"),
                         "sb": lambda n: done("dve", "gvb"), "s2": lambda n: done("dve", "sst1"),
                         "kv": lambda n: done("dve", "d1"), "dt": lambda n: done("dve", "drow"),
                         "son": lambda n: done("dve", "ms0"), "spl": lambda n: done("dve", "yma"),
                         "sgt": lambda n: done("dve", f"gr{n}"), "sop": lambda n: done("dve", f"sn{n}"),
                         "syt": lambda n: done("dve", f"ys{n}")}

        def bank_free(eng, it, kind, n=0, *needs):
            before, late = JOB_AT[kind, n], False
            last = it is LAST
            while True:
                before -= BANKS
                if before < 0:
                    before += -(-(len(JOBS) - before % BANKS) // BANKS) * BANKS
                    late, last = True, False
                if not absent(JOBS[before][0], last):
                    break
            needs = list(needs)
            pk, pn = JOBS[before]
            if pk in SAMPLE_JOBS:
                eng.wait_ge(*sample_reader[pk](pn))
            elif not (late and it is PROLOGUE):
                needs += [(ev, pn - ev.per if late else pn) for ev in reader[pk]]
            latest = {}
            for ev, m in needs:
                if ev.sem not in latest or ev.rank(m) > latest[ev.sem][0]:
                    latest[ev.sem] = ev.rank(m), ev, m
            for _, ev, m in latest.values():
                eng.wait_ge(*ev(it, m))

        PROLOGUE, LAST = -1, NB - 1

        def prep_of(k):
            return PLAN[k]

        def tile_reader(eng, it, t):
            t = t - 2
            if t < 0:
                eng.wait_ge(*ytt_f(it, t))
            elif t < NQ:
                eng.wait_ge(*raw_f(it, t))
            elif t < UA:
                eng.wait_ge(*z_f(it, t - ZB))
            elif t < OUT:
                eng.wait_ge(*u_f(it, t - UA))
            else:
                eng.wait_ge(*ytt_f(it, t - OUT))

        spare = [b for n, b in enumerate(ring) if n not in {JOB_AT["xf", m] % BANKS for m in range(8)}]
        assert len(spare) == 3

        block = ctx.enter_context(nc.Block())

        @block.sync
        def _(sp):
            for ev in (xres_in, w_in0, w_in1):
                sp.nop().then_inc(ev.sem, ev.per * ev.step)
            for dst, src in ((ident, a["ident"]), (upper, a["upper"]), (dmask, a["dmask"]), (lmask, a["lmask"])):
                sp.dma_start(dst[:], src).then_inc(s_const, 16)
            for dst, src in ((cin, a["c_all"]), (bada, a["b_ada"]), (vec[:, PREW:PREW + 8], a["pre_w"])):
                sp.dma_start(dst[:], src).then_inc(s_prm, 16)
            sp.dma_start(wada[0][:], a["w_ada"][0]).then_inc(ada_in[0], 16)
            sp.dma_start(xb[:], a["x"][0]).then_inc(x_in.sem, 16)
            sp.dma_start(xrow, a["xs"]).then_inc(sm_x0, 16)
            for j in range(1, 4):
                sp.dma_start(wada[j][:], a["w_ada"][j]).then_inc(ada_in[j], 16)
            for dst, src in ((vec[:, PSC:PSC + 4], a["pool_scale"]), (vec[:, ONW:ONW + 1], a["o_norm"]),
                             (vec[:, NEA:NEA + 4], a["a_log"].to_broadcast([P, H])),
                             (vec[:, DTB:DTB + 4], a["dt_bias"].to_broadcast([P, H])),
                             (cw, a["conv_w"]), (wgr, a["w_gate"]), (ftab, a["ftab"]),
                             (pwr, a["post_w"]), (grow, a["b_gate"])):
                sp.dma_start(dst[:], src).then_inc(s_prm2, 16)
            for j in range(4, 6):
                sp.dma_start(wada[j][:], a["w_ada"][j]).then_inc(ada_in[j], 16)
            for t in range(2):
                sp.dma_start(wraw[:, t], a["w"][t]).then_inc(w_in[t].sem, 16)
            def block_of(it, last=False):
                sp.wait_ge(*job["xf"](it, -1))
                if last:
                    sp.wait_ge(*h_lo(it, -1))
                    for dst, src in ((cbuf, a["s_conv"]), (pbuf, a["s_pool"])):
                        sp.dma_start(dst[:], src).then_inc(sm_st, 16)
                    sp.dma_start(ssm[:], a["s_ssm"]).then_inc(sm_ssm, 16)
                else:
                    sp.dma_start(xb[:], a["x"][it + 1]).then_inc(x_in.sem, 16)
                for t in range(NW - 2 if last else NW):
                    sp.wait_ge(*w_lo(it, t))
                    if last:
                        sp.wait_ge(*done("pe", f"sp{t}"))
                    sp.dma_start(wraw[:, t % 2], a["w"][(t + 2) % NW]).then_inc(w_in[t % 2].sem, 16)
                    if t == OUT:
                        sp.wait_ge(*job["su"](it, NC - 1))
                        sp.wait_ge(*job["mv"](it, NC - 1))
                        sp.wait_ge(*job["ot"](it, NC - 1))
                        sp.dma_start(xres[:], a["x"][it]).then_inc(xres_in.sem, 16)

            with sp.Fori(0, NB - 1) as it:
                block_of(it)
            block_of(LAST, last=True)
            sp.wait_ge(*proj(LAST, OUT - 1))
            sp.dma_start(xs[:], a["xs"]).then_inc(sm_x, 16)
            sp.dma_start(pw8[:], a["post_w"].to_broadcast([NS, DM])).then_inc(sm_x, 16)
            sp.wait_ge(s_end, 1)
            sp.dma_start(a["o_ssm"], st[:]).then_inc(out_sem, 16)
            sp.dma_start(a["o_conv"], hist[:]).then_inc(out_sem, 16)
            sp.dma_start(a["o_pool"], uhist[:]).then_inc(out_sem, 16)
            sp.wait_ge(sm_st, 32)
            sp.wait_ge(*done("dve", "pj23"))
            rows = lambda o: o.rearrange("j p t s -> p j t s")
            sp.dma_start(rows(a["o_sconv"])[:, 0:CK - 2], cbuf[:, 1:CK - 1]).then_inc(out_sem, 16)
            sp.dma_start(a["o_sconv"][CK - 2], pj[:, 0:NQ]).then_inc(out_sem, 16)
            sp.dma_start(rows(a["o_spool"])[:, 0:PB - 1], pbuf[:, 1:PB]).then_inc(out_sem, 16)
            sp.dma_start(a["o_spool"][PB - 1], pj[:, 20:24]).then_inc(out_sem, 16)
            for r in range(NS):
                sp.wait_ge(*done("dve", f"sn{r}"))
                sp.dma_start(a["o_sssm"][:, r], ssm[:, r]).then_inc(out_sem, 16)
            sp.wait_ge(*done("dve", "yr"))
            sp.dma_start(a["ys"], ys[:]).then_inc(out_sem, 16)
            sp.wait_ge(*y_out(LAST, 3))
            sp.wait_ge(out_sem, 16 * (8 + NS))

        def front_act(act, it):
            act.wait_ge(*x_in(it, 0))
            for t in range(4):
                if it is not PROLOGUE or t > 0:
                    act.wait_ge(*xsq(it, t - 1))
                if t == 0 and it is not PROLOGUE:
                    act.wait_ge(*rx_0(it, -1))
                    act.wait_ge(*ysq(it, -1))
                nc.scalar.activation(junk[:, :], xb[:, t, :], ACT.Square,
                                     accum_out=ssx[:, t:t + 1]).then_inc(xsq.sem, 1)

        def front_h(act, it, m):
            act.wait_ge(*job["xf"](it, m))
            if m >= 2 or it is not PROLOGUE:
                act.wait_ge(*h_lo(it, m - 2))
            nc.scalar.activation(htmp[:, m % 2], bank("xf", m)[:], ACT.Identity, bias=mod[:, m, 0:1],
                                 scale=amul[:, m, 0:1]).then_inc(h_f.sem, 1)

        @block.scalar
        def _(act):
            for ev in (w_hi, raw_f, silu, sq, g_ab, g_e, g_l, g_t, g_eg, g_ekg, tanh_f, u_f, kt_f, d_e, x_0,
                       u_c, o_sq4, yhi_f, ytt_f, ysq):
                act.nop().then_inc(ev.sem, ev.per)
            act.wait_ge(s_prm, 48)
            nc.scalar.activation(cin[:], cin[:], ACT.Silu).then_inc(s_cact, 1)
            front_act(act, PROLOGUE)
            act.wait_ge(sm_x0, 16)
            act.wait_ge(*xsq(PROLOGUE, 3))
            nc.scalar.activation(junk[0:NS, :], xrow, ACT.Square, accum_out=s8[:, 0:1]).then_inc(*step("act", "x_sq"))
            act.wait_ge(s_prm2, 144)
            nc.scalar.activation(vec[:, NEA:NEA + 4], vec[:, NEA:NEA + 4], ACT.Exp).then_inc(s_cact, 1)
            act.wait_ge(s_pre, 5)
            for m in range(8):
                front_h(act, PROLOGUE, m)
            for t in range(2):
                act.wait_ge(*w_in[t](0, 0))
                nc.scalar.activation(whi[:, t], wraw[:, t], ACT.Copy).then_inc(w_hi.sem, 1)

            def split_hi(it, t):
                act.wait_ge(*w_in[(t + 1) % 2](it + (t + 1) // NW, (t + 1) % NW // 2))
                act.wait_ge(*proj(it, t - 1))
                nc.scalar.activation(whi[:, (t + 1) % 2], wraw[:, (t + 1) % 2], ACT.Copy).then_inc(w_hi.sem, 1)

            def tile(it, t):
                act.wait_ge(*proj(it, t))
                if t < NQ:
                    act.wait_ge(*conv(it, t - 2))
                    act.wait_ge(*hist_out(it, t - 2))
                    nc.scalar.activation(raw[:, t % 2, CK - 1:], acc[t % 2][:], ACT.Copy).then_inc(raw_f.sem, 1)
                elif t < UA:
                    z = t - ZB
                    if z == 0:
                        act.wait_ge(*job["ss"](it, 7))
                        act.wait_ge(*job["ss"](it, 6))
                    act.wait_ge(*z_f(it, z - 2))
                    nc.scalar.activation(tmpa[:, t % 2], acc[t % 2][:], ACT.Tanh, scale=0.5).then_inc(tanh_f.sem, 1)
                elif t < OUT:
                    g = t - UA
                    act.wait_ge(*pooled_f(it, g - 2))
                    act.wait_ge(*u_out(it, g - 2))
                    nc.scalar.activation(ubuf[:, g % 2, PB:], acc[t % 2][:], ACT.Copy).then_inc(u_f.sem, 1)
                else:
                    m = t - OUT
                    act.wait_ge(*job["yt"](it, m - 2))
                    nc.scalar.activation(ytt[:, m % 2], acc[t % 2][:], ACT.Copy).then_inc(ytt_f.sem, 1)

            def silu_sq(it, t):
                act.wait_ge(*conv(it, t))
                if t == 0:
                    act.wait_ge(*proj(it, -1))
                nc.scalar.activation(cq[:, t], cacc[:, t % 2], ACT.Silu).then_inc(silu.sem, 1)
                if t < 8:
                    act.wait_ge(*silu(it, t))
                    if t < 2:
                        act.wait_ge(*z_f(it, -1 - t % 2))
                        act.wait_ge(*z_f(it, -1))
                    else:
                        act.wait_ge(*job["ss"](it, t - 2))
                    nc.scalar.activation(tmpa[:, t % 2], cq[:, t], ACT.Square).then_inc(sq.sem, 1)

            def block_of(it, last=False):
                for t in range(NQ):
                    if t:
                        split_hi(it, t)
                    if t == 2:
                        act.wait_ge(*job["gt"](it, 0))
                        act.wait_ge(*g_b(it, -1))
                        nc.scalar.activation(btt[:], bank("gt")[:, 0:32].rearrange("p (c e) -> p c e", c=NC)[:, :, 0:4],
                                             ACT.Tanh, scale=0.5).then_inc(g_t.sem, 1)
                        act.wait_ge(*g_y(it, 0))
                        nc.scalar.activation(gab[:], ga[:], ACT.Abs).then_inc(g_ab.sem, 1)
                        act.wait_ge(*g_ab(it, 0))
                        act.wait_ge(*g_sp(it, -1))
                        nc.scalar.activation(gl1[:], gab[:], ACT.Exp, scale=-1.0).then_inc(g_e.sem, 1)
                        act.wait_ge(*g_e(it, 0))
                        nc.scalar.activation(gl1[:], gl1[:], ACT.Ln, bias=1.0).then_inc(g_l.sem, 1)
                    tile(it, t)
                    if t >= 1:
                        silu_sq(it, t - 1)
                    if last and t == 8:
                        act.wait_ge(*done("pe", "sg0"))
                        nc.scalar.activation(g8[:, 0], bank("sg")[0:NS, 0:4], ACT.Tanh, scale=0.5).then_inc(*step("act", "g_tanh"))
                        act.wait_ge(*done("dve", "g_a"))
                        nc.scalar.activation(g8[:, 2], g8[:, 1], ACT.Abs).then_inc(*step("act", "g_abs"))
                        act.wait_ge(*done("act", "g_abs"))
                        nc.scalar.activation(g8[:, 2], g8[:, 2], ACT.Exp, scale=-1.0).then_inc(*step("act", "g_exp"))
                        act.wait_ge(*done("act", "g_exp"))
                        nc.scalar.activation(g8[:, 2], g8[:, 2], ACT.Ln, bias=1.0).then_inc(*step("act", "g_ln"))
                    if last and t == 10:
                        act.wait_ge(*done("dve", "g_g"))
                        nc.scalar.activation(g8[:, 5], g8[:, 4], ACT.Exp).then_inc(*step("act", "g_eg"))
                silu_sq(it, NQ - 1)
                act.wait_ge(*gc_f(it, 0))
                act.wait_ge(*yb_f(it, -1))
                nc.scalar.activation(eg[:], gcs[:], ACT.Exp).then_inc(g_eg.sem, 1)
                act.wait_ge(*g_d(it, 0))
                nc.scalar.activation(ekg[:], gd[:], ACT.Exp).then_inc(g_ekg.sem, 1)
                for slot, (c, p, sc, q, thirds) in enumerate(PLAN):
                    for n in thirds:
                        if n < 36 and n % 3 == 0:
                            split_hi(it, 12 + n // 3)
                        if n < 36 and n % 3 == 2:
                            tile(it, 12 + n // 3)
                    if c is not None and p == 0:
                        act.wait_ge(*job["kt"](it, c))
                        act.wait_ge(*job["su"](it, c - 2)) if c >= 2 else act.wait_ge(*yr_f(it, -1))
                        nc.scalar.activation(ktok[:, c % 2], heads(bank("kt", c)), ACT.Copy).then_inc(kt_f.sem, 1)
                        act.wait_ge(*d_2(it, c))
                        nc.scalar.activation(dcy[:], dcy[:], ACT.Exp).then_inc(d_e.sem, 1)
                    elif c is not None and p == 2:
                        act.wait_ge(*job["xt"](it, c))
                        act.wait_ge(*job["w"](it, c * NL - 1))
                        nc.scalar.activation(xv[:], heads(bank("xt", c)), ACT.Copy).then_inc(x_0.sem, 1)
                    if q == 1 and sc is not None:
                        act.wait_ge(*job["u"](it, sc))
                        act.wait_ge(*ve_f(it, sc - 1))
                        act.wait_ge(*job["mv"](it, sc - 1)) if sc else act.wait_ge(*yr_f(it, -1))
                        nc.scalar.activation(ub[:], heads(bank("u", sc)), ACT.Copy).then_inc(u_c.sem, 1)
                    if q == 2 and sc is not None:
                        act.wait_ge(*o_f(it, sc))
                        act.wait_ge(*o_n0(it, sc - 1))
                        for h in range(H):
                            act.wait_ge(*o_sq4(it, 4 * sc + h - 1))
                            if h == 0 and sc == 0:
                                act.wait_ge(*xsq(it, -1))
                                act.wait_ge(*ysq(it, -1))
                            nc.scalar.activation(junk[:, 0:C], ao[:, h], ACT.Square,
                                                 accum_out=oss[:, h:h + 1]).then_inc(o_sq4.sem, 1)
                    if last and slot == SAMPLE_SLOT["conv"]:
                        act.wait_ge(*done("dve", "cv6"))
                        nc.scalar.activation(cs[:], ct[:], ACT.Silu).then_inc(*step("act", "silu"))
                    if last and slot == SAMPLE_SLOT["gate"]:
                        act.wait_ge(*done("dve", "pj19"))
                        nc.scalar.activation(zs[:], pj[:, 12:20], ACT.Tanh, scale=0.5).then_inc(*step("act", "z_tanh"))
                for m in range(8):
                    act.wait_ge(*yb_f(it, NC - 1))
                    act.wait_ge(*job["ot"](it, NC - 1))
                    act.wait_ge(*ya_f(it, NG - 1))
                    nc.scalar.activation(yhi[:, m], y32[:, m], ACT.Copy).then_inc(yhi_f.sem, 1)
                act.wait_ge(*o_sq4(it, 4 * NC - 1))
                if not last:
                    front_act(act, it)
                for m in range(8):
                    if not (last and m == 7):
                        split_hi(it, OUT + m)
                    tile(it, OUT + m)
                    if not last:
                        front_h(act, it, m)
                if not last:
                    split_hi(it, NW)
                for t in range(4):
                    act.wait_ge(*ytok_f(it, 7))
                    act.wait_ge(*ry_0(it, -1))
                    act.wait_ge(*ysq(it, t - 1))
                    if not last:
                        act.wait_ge(*xsq(it, 3))
                    nc.scalar.activation(junk[:, :], ytok[:, t], ACT.Square, accum_out=ssy[:, t:t + 1]).then_inc(ysq.sem, 1)


            with act.Fori(0, NB - 1) as it:
                block_of(it)
            block_of(LAST, last=True)
            act.wait_ge(*done("dve", "ys1"))
            act.wait_ge(*ysq(LAST, 3))
            nc.scalar.activation(junk[0:NS, :], ys[:], ACT.Square, accum_out=s8[:, 4:5]).then_inc(*step("act", "y_sq"))

        def front_xn(dve, it):
            dve.wait_ge(*rx_f(it, 0))
            for t in range(4):
                nc.vector.tensor_scalar(xb[:, t], xb[:, t], rx[:, t:t + 1], None, ALU.mult).then_inc(xn.sem, 1)

        def front_lo(dve, it, m):
            dve.wait_ge(*h_hi(it, m))
            nc.vector.tensor_tensor(hlo[:, m], htmp[:, m % 2], hhi[:, m].bitcast(F32), ALU.subtract).then_inc(h_lo.sem, 1)

        @block.vector
        def _(dve):
            for ev in (conv_a, conv, ss_ev, g_c, g_y, g_sp, g_g, g_b, gc_f, g_d, k_1, k_2, b_f, bke_f, z_f, pooled_f, ya_f,
                       rv_f, d_1, d_2, d_b, lt_f, mt_f, y_0, y_1, y_l, x_l, w_f, ks_t, r_f, ao_f, ve_f, s_f, o_f, yb_f,
                       ylo_f, ytok_f, yn_f, yr_f):
                dve.nop().then_inc(ev.sem, ev.per)
            nc.vector.memset(st[:], 0.0)
            nc.vector.memset(ones[:], 1.0)
            nc.vector.memset(hist[:], 0.0)
            nc.vector.memset(uhist[:], 0.0).then_inc(s_pre, 1)
            for j in range(4):
                dve.wait_ge(s_mod, j + 1)
                nc.vector.tensor_copy(rows9[j], acc[j % 2][0:1 + NS, :]).then_inc(s_rows, 1)
                if j == 1:
                    front_xn(dve, PROLOGUE)
                    dve.wait_ge(*done("pool", "rx"))
                    nc.vector.tensor_scalar(xrow, xrow, s8[:, 2:3], None, ALU.mult).then_inc(*step("dve", "xn"))
            dve.wait_ge(s_tr, 1)
            dve.wait_ge(s_prm, 48)
            nc.vector.tensor_tensor(mod[:, 0:16], spare[0][:, 0:144].rearrange("p (m s) -> p m s", m=16),
                                    bada[:, 0:16].unsqueeze(2).to_broadcast([P, 16, 1 + NS]), ALU.add).then_inc(s_pre, 1)
            dve.wait_ge(s_pre, 2)
            nc.vector.tensor_scalar(amul[:], mod[:, 8:16], 1.0, None, ALU.add).then_inc(s_pre, 1)
            dve.wait_ge(s_pre, 3)
            nc.vector.tensor_tensor(amul[:], amul[:], vec[:, PREW:PREW + 8].unsqueeze(2).to_broadcast([P, 8, 1 + NS]),
                                    ALU.mult).then_inc(s_pre, 1)
            dve.wait_ge(s_cact, 2)
            dve.wait_ge(s_prm2, 144)
            nc.vector.tensor_scalar(vec[:, NEA:NEA + 4], vec[:, NEA:NEA + 4], -1.0, None, ALU.mult)
            nc.vector.tensor_scalar(vec[:, PSC:PSC + 5], vec[:, PSC:PSC + 5], 0.5, None, ALU.mult)
            nc.vector.tensor_copy(wgh[:], wgr[:]).then_inc(s_pre, 1)
            dve.wait_ge(s_pre, 5)
            nc.vector.tensor_tensor(wgl[:], wgr[:], wgh[:].bitcast(F32), ALU.subtract).then_inc(s_pre, 1)
            for m in range(8):
                front_lo(dve, PROLOGUE, m)
                if m in (4, 7):
                    j = 4 if m == 4 else 5
                    dve.wait_ge(s_mod, j + 1)
                    nc.vector.tensor_copy(rows9[j], acc[j % 2][0:1 + NS, :]).then_inc(s_rows, 1)
            dve.wait_ge(*done("pe", "hs"))
            nc.vector.tensor_tensor(hs[:], spare[2][:, 0:64].rearrange("p (k s) -> p k s", k=KT), amul[:, :, 1:1 + NS],
                                    ALU.mult).then_inc(*step("dve", "h0"))
            dve.wait_ge(*done("dve", "h0"))
            nc.vector.tensor_tensor(hs[:], hs[:], mod[:, 0:8, 1:1 + NS], ALU.add).then_inc(*step("dve", "h"))
            for m in range(2):
                cols = slice(m * BT, (m + 1) * BT)
                dve.wait_ge(s_rows, 5 + m)
                nc.vector.tensor_tensor(grow[:, cols], grow[:, cols], rows9[4 + m][0:1], ALU.add).then_inc(s_trc, 1)
                dve.wait_ge(s_trc, 2 * m + 1)
                nc.vector.tensor_tensor(grow[:, cols], grow[:, cols], pwr[:, cols], ALU.mult).then_inc(s_trc, 1)
            dve.wait_ge(s_tr, 2)
            nc.vector.tensor_tensor(mod[:, 16:24], spare[1][:, 0:72].rearrange("p (m s) -> p m s", m=8),
                                    bada[:, 16:24].unsqueeze(2).to_broadcast([P, 8, 1 + NS]), ALU.add)
            for m in range(2):
                dve.wait_ge(s_row, m + 1)
                nc.vector.tensor_copy(gpw[:, m * 512:(m + 1) * 512], (spare[2], spare[0])[m][:]).then_inc(s_rowc, 1)

            def convolve(it, t):
                r = raw[:, t % 2]
                dve.wait_ge(*raw_f(it, t))
                dve.wait_ge(*hist_in(it, t))
                dve.wait_ge(*silu(it, t - 2))
                nc.vector.tensor_scalar(cacc[:, t % 2], r[:, 0:BT], cw[:, t, 0:1], None, ALU.mult).then_inc(conv_a.sem, 1)
                for j in range(1, CK):
                    dve.wait_ge(*conv_a(it, 3 * t + j - 1))
                    nc.vector.scalar_tensor_tensor(out=cacc[:, t % 2], in0=r[:, j:j + BT], scalar=cw[:, t, j:j + 1],
                                                   in1=cacc[:, t % 2], op0=ALU.mult, op1=ALU.add
                                                   ).then_inc((conv_a if j < CK - 1 else conv).sem, 1)

            def stat(it, t):
                dve.wait_ge(*job["ss"](it, t))
                if t == 0:
                    dve.wait_ge(*k_1(it, -1))
                    dve.wait_ge(*odb_0(it, -1))
                nc.vector.tensor_copy(ssb[:, t], bank("ss", t)[:, 0:NC]).then_inc(ss_ev.sem, 1)

            def zmul(it, t):
                z = t - ZB
                yk = y32[:, (z + 4) % 8]
                dve.wait_ge(*tanh_f(it, z))
                if z == 0:
                    dve.wait_ge(*y_out(it, -1))
                nc.vector.scalar_tensor_tensor(out=yk, in0=tmpa[:, t % 2], scalar=1.0, in1=acc[t % 2][:],
                                               op0=ALU.add, op1=ALU.mult).then_inc(z_f.sem, 1)

            def sample_tile(it, t):
                dve.wait_ge(*done("pe", f"sp{t}"))
                if t == 0:
                    dve.wait_ge(*h_lo(it, -1))
                if t >= OUT:
                    nc.vector.tensor_copy(hs[:, t - OUT], bank("sp", t)[:, 0:NS]).then_inc(*step("dve", f"pj{t}"))
                else:
                    nc.vector.tensor_copy(pj[:, t], bank("sp", t)[:, 0:NS]).then_inc(*step("dve", f"pj{t}"))

            def sample_slot(it, slot):
                def s(name):
                    return step("dve", name)

                def after(name, who="dve"):
                    dve.wait_ge(*done(who, name))

                if slot == SAMPLE_SLOT["conv"]:
                    def taps(j):
                        return cw[:, :, j:j + 1].to_broadcast([P, NQ, NS])

                    dve.wait_ge(*silu(it, NQ - 1))
                    dve.wait_ge(sm_st, 32)
                    nc.vector.tensor_tensor(ct[:], pj[:, 0:NQ], taps(CK - 1), ALU.mult).then_inc(*s("cv0"))
                    for j in range(CK - 1):
                        after(f"cv{2 * j}")
                        nc.vector.tensor_tensor(sqs[:], cbuf[:, j], taps(j), ALU.mult).then_inc(*s(f"cv{2 * j + 1}"))
                        after(f"cv{2 * j + 1}")
                        nc.vector.tensor_tensor(ct[:], ct[:], sqs[:], ALU.add).then_inc(*s(f"cv{2 * j + 2}"))
                if slot == SAMPLE_SLOT["square"]:
                    after("silu", "act")
                    nc.vector.tensor_tensor(sqs[:, 0:8], cs[:, 0:8], cs[:, 0:8], ALU.mult).then_inc(*s("sq0"))
                    nc.vector.tensor_tensor(sqs[:, 8:12], cs[:, 0:4], cs[:, 4:8], ALU.mult).then_inc(*s("sq1"))
                    for e in range(2):
                        nc.vector.tensor_copy(kq[:, :, :, e].rearrange("p s h -> p h s"), cs[:, 4 * e:4 * e + 4]
                                              ).then_inc(*s(f"kq{e}"))
                if slot == SAMPLE_SLOT["root"]:
                    after("s20", "pe")
                    nc.vector.tensor_scalar(sst[:, 0:8], bank("s2")[:, 0:64].rearrange("p (t s) -> p t s", t=8), EPS, None,
                                            ALU.add).then_inc(*s("sst0"))
                    nc.vector.tensor_copy(sst[:, 8:12].rearrange("p t s -> p (t s)"), bank("s2")[:, 64:96]).then_inc(*s("sst1"))
                    after("kv0", "pe")
                    t0, t1 = (bank("kv")[:, 0:64].rearrange("p (s h e) -> p e h s", s=NS, h=H)[:, e] for e in range(2))
                    eg_ = gvb[:, :, 1].rearrange("p s h -> p h s")
                    nc.vector.tensor_tensor(dl[:, 0], t0, eg_, ALU.mult).then_inc(*s("d0"))
                    nc.vector.tensor_tensor(dl[:, 1], t1, eg_, ALU.mult).then_inc(*s("d1"))
                if slot == SAMPLE_SLOT["delta"]:
                    after("rk", "pool")
                    be = gvb[:, :, 0].rearrange("p s h -> p h s")
                    dps = dl[:, 2].rearrange("p h s -> p (h s)").rearrange("p (s h) -> p h s", h=H)
                    after("d0")
                    nc.vector.tensor_tensor(dl[:, 0], dl[:, 0], rk[:, 1], ALU.mult).then_inc(*s("d2"))
                    after("d2")
                    nc.vector.tensor_tensor(dl[:, 0], cs[:, 8:12], dl[:, 0], ALU.subtract).then_inc(*s("d3"))
                    after("d3")
                    nc.vector.tensor_tensor(dl[:, 0], dl[:, 0], be, ALU.mult).then_inc(*s("d4"))
                    after("d4")
                    nc.vector.tensor_tensor(dps, dl[:, 0], rk[:, 1], ALU.mult).then_inc(*s("d5"))
                    after("d5")
                    nc.vector.tensor_tensor(dl[:, 0], dps, sst[:, 8:12], ALU.mult).then_inc(*s("o0"))
                    after("o0")
                    nc.vector.tensor_tensor(dl[:, 1], dl[:, 1], dl[:, 0], ALU.add).then_inc(*s("o1"))
                    after("o1")
                    nc.vector.tensor_tensor(dl[:, 3], dl[:, 1], dl[:, 1], ALU.mult).then_inc(*s("o2"))
                if slot == SAMPLE_SLOT["mean"]:
                    after("dt0", "pe")
                    dve.wait_ge(*job["gt"](it, 0))
                    nc.vector.tensor_copy(drow[:].rearrange("p a c -> p (a c)"), bank("dt")[0:32, 0:256]).then_inc(*s("drow"))
                    after("son0", "pe")
                    nc.vector.tensor_scalar(rk[:, 0], bank("son")[:, 0:32].rearrange("p (h s) -> p h s", h=H), 1.0 / P, None,
                                            ALU.mult).then_inc(*s("ms0"))
                    nc.vector.tensor_scalar(dl[:, 0], sst[:, 4:8], EPS * P, None, ALU.mult).then_inc(*s("ms1"))
                    after("ms1")
                    nc.vector.tensor_tensor(rk[:, 0], rk[:, 0], dl[:, 0], ALU.add).then_inc(*s("ms2"))
                if slot == SAMPLE_SLOT["gate"]:
                    after("z_tanh", "act")
                    nc.vector.scalar_tensor_tensor(out=zs[:], in0=zs[:], scalar=1.0, in1=pj[:, 12:20], op0=ALU.add,
                                                   op1=ALU.mult).then_inc(*s("zs"))
                    after("rstd", "pool")
                    nc.vector.tensor_tensor(dl[:, 1], dl[:, 1], rk[:, 1], ALU.mult).then_inc(*s("on"))
                    after("on")
                    nc.vector.scalar_tensor_tensor(out=ym[:, 4:8], in0=dl[:, 1], scalar=vec[:, ONW:ONW + 1], in1=zs[:, 0:4],
                                                   op0=ALU.mult, op1=ALU.mult).then_inc(*s("ymb"))
                if slot == SAMPLE_SLOT["pool"]:
                    for g in range(NG):
                        w = 2 << g
                        nc.vector.tensor_reduce(pls[:, g], pbuf[:, PB - (w - 1):PB, g].rearrange("p j s -> p s j"), AX.X,
                                                ALU.add).then_inc(*s(f"pl{g}"))
                    after("pl3")
                    nc.vector.tensor_tensor(pls[:], pls[:], pj[:, 20:24], ALU.add).then_inc(*s("pl4"))
                    after("pl4")
                    for g in range(NG):
                        nc.vector.scalar_tensor_tensor(out=pls[:, g], in0=pls[:, g], scalar=1.0 / (2 << g), in1=pj[:, 20 + g],
                                                       op0=ALU.mult, op1=ALU.subtract).then_inc(*s(f"pl{5 + g}"))
                if slot == SAMPLE_SLOT["mixed"]:
                    after("spl0", "pe")
                    after("zs")
                    for g in range(NG):
                        nc.vector.scalar_tensor_tensor(out=ym[:, g], in0=bank("spl")[:, g * NS:(g + 1) * NS],
                                                       scalar=vec[:, PSC + g:PSC + g + 1], in1=zs[:, 4 + g], op0=ALU.mult,
                                                       op1=ALU.mult).then_inc(*s("yma" if g == 3 else f"ym{g}"))

            def sample_out(it, m):
                def s(name):
                    return step("dve", name)

                if m < 8:
                    if m == 0:
                        dve.wait_ge(*done("pe", "sp23"))
                    sample_tile(it, OUT + m)
                if m == 0:
                    dve.wait_ge(*proj(it, OUT - 1))
                    dve.wait_ge(*done("dve", "drow"))
                    nc.vector.tensor_tensor(krow[:], drow[:, 0].unsqueeze(1).to_broadcast([32, 32, P]),
                                            ident[0:32, 0:32].unsqueeze(2).to_broadcast([32, 32, P]), ALU.mult).then_inc(*s("krow"))
                if m >= 1:
                    r = m - 1
                    nc.vector.tensor_tensor(ssm[:, r], ssm[:, r], gvb[:, r, 1].unsqueeze(2).to_broadcast([P, H, P]),
                                            ALU.mult).then_inc(*s(f"se{r}"))
                    dve.wait_ge(*done("pe", f"sop{r}"))
                    dve.wait_ge(*done("dve", f"se{r}"))
                    nc.vector.tensor_tensor(ssm[:, r], ssm[:, r], heads(bank("sop", r)), ALU.add).then_inc(*s(f"sn{r}"))
                if m == 8:
                    dve.wait_ge(sm_x, 32)
                    for e in range(2):
                        dve.wait_ge(*done("pe", f"sgt{e}"))
                        nc.vector.tensor_tensor(gr8[:, e * 512:(e + 1) * 512], bank("sgt", e)[0:NS, :],
                                                pw8[:, e * 512:(e + 1) * 512], ALU.mult).then_inc(*s(f"gr{e}"))

            def block_of(it, last=False):
                for t in range(NQ):
                    if t == 1:
                        dve.wait_ge(*job["gates"](it, 0))
                        dve.wait_ge(*job["gt"](it, -1))
                        nc.vector.tensor_copy(gsb[:], bank("gates")[0:8, :]).then_inc(g_c.sem, 1)
                    if t == 2:
                        dve.wait_ge(*job["gt"](it, 0))
                        dve.wait_ge(*g_t(it, 0))
                        dve.wait_ge(*g_sp(it, -1))
                        nc.vector.tensor_tensor(ga[:], bank("gt")[:, 0:32].rearrange("p (c e) -> p c e", c=NC)[:, :, 4:8],
                                                vec[:, DTB:DTB + 4].unsqueeze(1).to_broadcast([P, NC, H]), ALU.add
                                                ).then_inc(g_y.sem, 1)
                        dve.wait_ge(*g_t(it, 0))
                        dve.wait_ge(*b_f(it, -1))
                        nc.vector.tensor_scalar(beta[:], btt[:], 0.5, 0.5, ALU.mult, ALU.add).then_inc(g_b.sem, 1)
                    convolve(it, t)
                    if t == 2:
                        dve.wait_ge(*g_l(it, 0))
                        dve.wait_ge(*g_y(it, 0))
                        nc.vector.scalar_tensor_tensor(out=gsp[:], in0=ga[:], scalar=0.0, in1=gl1[:], op0=ALU.max,
                                                       op1=ALU.add).then_inc(g_sp.sem, 1)
                        dve.wait_ge(*g_sp(it, 0))
                        dve.wait_ge(*job["gc"](it, -1))
                        dve.wait_ge(*gb_in(it, -1))
                        nc.vector.tensor_tensor(gg[:], gsp[:], vec[:, NEA:NEA + 4].unsqueeze(1).to_broadcast([P, NC, H]),
                                                ALU.mult).then_inc(g_g.sem, 1)
                    if t == 5:
                        dve.wait_ge(*job["gc"](it, 0))
                        dve.wait_ge(*g_eg(it, -1))
                        dve.wait_ge(*d_1(it, -1))
                        nc.vector.tensor_copy(gcs[:].rearrange("p a c h -> p (a c h)"), bank("gc")[:, 0:32]).then_inc(gc_f.sem, 1)
                        dve.wait_ge(*gc_f(it, 0))
                        dve.wait_ge(*g_ekg(it, -1))
                        nc.vector.tensor_tensor(gd[:], gcs[:, 1], gcs[:, 0], ALU.subtract).then_inc(g_d.sem, 1)
                    if 2 <= t < 10:
                        stat(it, t - 2)
                    if last:
                        sample_tile(it, t)
                        if t == 7:
                            dve.wait_ge(*done("act", "g_tanh"))
                            nc.vector.tensor_tensor(g8[:, 1], bank("sg")[0:NS, 4:8], vec[0:NS, DTB:DTB + 4], ALU.add
                                                    ).then_inc(*step("dve", "g_a"))
                        if t == 8:
                            dve.wait_ge(*done("act", "g_ln"))
                            nc.vector.tensor_scalar(g8[:, 6], g8[:, 0], 0.5, 0.5, ALU.mult, ALU.add).then_inc(*step("dve", "g_beta"))
                            nc.vector.scalar_tensor_tensor(out=g8[:, 3], in0=g8[:, 1], scalar=0.0, in1=g8[:, 2], op0=ALU.max,
                                                           op1=ALU.add).then_inc(*step("dve", "g_sp"))
                            dve.wait_ge(*done("dve", "g_sp"))
                            nc.vector.tensor_tensor(g8[:, 4], g8[:, 3], vec[0:NS, NEA:NEA + 4], ALU.mult
                                                    ).then_inc(*step("dve", "g_g"))
                        if t == 10:
                            dve.wait_ge(*done("act", "g_eg"))
                            for e, row in enumerate((6, 5)):
                                nc.vector.tensor_tensor(gdg[:, :, e * H:(e + 1) * H],
                                                        g8[:, row].unsqueeze(1).to_broadcast([NS, NS, H]),
                                                        ident[0:NS, 0:NS].unsqueeze(2).to_broadcast([NS, NS, H]), ALU.mult
                                                        ).then_inc(*step("dve", f"g_d{e}"))
                if last:
                    dve.wait_ge(*done("pe", "sb0"))
                    nc.vector.tensor_copy(gvb[:].rearrange("p s a h -> p (s a h)"), bank("sb")[:, 0:64]).then_inc(*step("dve", "gvb"))
                dve.wait_ge(*ss_ev(it, 7))
                nc.vector.tensor_scalar(kk1[:], ssb[:, 0:4].rearrange("p h c -> p c h"), EPS, None, ALU.add).then_inc(k_1.sem, 1)
                dve.wait_ge(*k_1(it, 0))
                nc.vector.reciprocal(kk2[:], kk1[:]).then_inc(k_2.sem, 1)
                dve.wait_ge(*k_2(it, 0))
                nc.vector.tensor_tensor(bb[:], beta[:], kk2[:], ALU.mult).then_inc(b_f.sem, 1)
                dve.wait_ge(*b_f(it, 0))
                dve.wait_ge(*g_ekg(it, 0))
                nc.vector.tensor_tensor(bke[:], bb[:], ekg[:], ALU.mult).then_inc(bke_f.sem, 1)

                for slot, (c, p, sc, q, thirds) in enumerate(PLAN):
                    for n in thirds:
                        t = 12 + n // 3
                        if n % 3 == 2 and t < UA:
                            zmul(it, t)
                        if last and n % 3 == 0 and t < OUT:
                            sample_tile(it, t)
                        if n % 3 == 2 and UA <= t - 1 < OUT:
                            g = t - 1 - UA
                            dve.wait_ge(*win_f(it, g))
                            dve.wait_ge(*job["pool"](it, g - 2))
                            nc.vector.scalar_tensor_tensor(out=pooled[:, g % 2], in0=win[:, g % 2, PB:],
                                                           scalar=1.0 / (2 << g), in1=ubuf[:, g % 2, PB:],
                                                           op0=ALU.mult, op1=ALU.subtract).then_inc(pooled_f.sem, 1)
                        g = pool_after(n)
                        if g is not None:
                            dve.wait_ge(*job["pool"](it, g))
                            dve.wait_ge(*z_f(it, 4 + g))
                            nc.vector.scalar_tensor_tensor(out=y32[:, g], in0=bank("pool", g)[:], scalar=vec[:, PSC + g:PSC + g + 1],
                                                           in1=y32[:, g], op0=ALU.mult, op1=ALU.mult).then_inc(ya_f.sem, 1)
                    if c is not None and p == 0:
                        dve.wait_ge(*job["vt"](it, c))
                        dve.wait_ge(*sk_f(it, 0))
                        dve.wait_ge(*job["u"](it, c - 2)) if c >= 2 else dve.wait_ge(*yr_f(it, -1))
                        nc.vector.tensor_tensor(rv[:, c % 2], heads(bank("vt", c)), bc(sk[:, c]), ALU.mult).then_inc(rv_f.sem, 1)
                        dve.wait_ge(*job["gb"](it, c))
                        dve.wait_ge(*mt_f(it, c - 1))
                        nc.vector.tensor_tensor(dcy[:], heads(bank("gb", c)), bc(gcs[:, 0, c]), ALU.subtract).then_inc(d_1.sem, 1)
                        dve.wait_ge(*d_1(it, c))
                        nc.vector.tensor_tensor(dcy[:], dcy[:], mbc(dmask[:]), ALU.min).then_inc(d_2.sem, 1)
                        dve.wait_ge(*d_e(it, c))
                        nc.vector.tensor_tensor(dcy[:], dcy[:], bc(bb[:, c]), ALU.mult).then_inc(d_b.sem, 1)
                    elif c is not None and p == 1:
                        dve.wait_ge(*d_b(it, c))
                        dve.wait_ge(*job["kk"](it, c))
                        dve.wait_ge(*job["w"](it, c * NL - 1))
                        nc.vector.tensor_tensor(lt[:], heads(bank("kk", c)), dcy[:], ALU.mult).then_inc(lt_f.sem, 1)
                        dve.wait_ge(*job["qk"](it, c))
                        if c >= 2:
                            dve.wait_ge(*job["mv"](it, c - 2))
                        elif c == 0:
                            dve.wait_ge(*proj(it, -1))
                        nc.vector.tensor_tensor(mtb[:, c % 2], heads(bank("qk", c)), dcy[:], ALU.mult).then_inc(mt_f.sem, 1)
                        dve.wait_ge(*lt_f(it, c))
                        if c >= 2:
                            dve.wait_ge(*job["u"](it, c - 2))
                        nc.vector.tensor_tensor(yv[:, c % 2], lt[:], mbc(lmask[:, 0]), ALU.mult).then_inc(y_0.sem, 1)
                        dve.wait_ge(*y_0(it, c))
                        nc.vector.tensor_tensor(yv[:, c % 2], mbc(ident[:]), yv[:, c % 2], ALU.subtract).then_inc(y_1.sem, 1)
                    elif c is not None and p >= 3 and p % 2:
                        lv = (p - 3) // 2
                        i = c * NL + lv
                        dve.wait_ge(*job["w"](it, i))
                        dve.wait_ge(*job["yy"](it, i - 1))
                        sz = LEVELS[lv]
                        nc.vector.tensor_tensor(
                            wb[:].rearrange("p h (b two s) -> p (h b) two s", two=2, s=sz),
                            packed(bank("w", i), sz).unsqueeze(2).to_broadcast([P, H * C // (2 * sz), 2, sz]),
                            level_mask(lv), ALU.mult).then_inc(w_f.sem, 1)
                    elif c is not None and p >= 4:
                        lv = (p - 4) // 2
                        sz = LEVELS[lv]
                        if lv < NL - 1:
                            i = c * (NL - 1) + lv
                            dve.wait_ge(*job["xx"](it, i))
                            if lv == 0:
                                dve.wait_ge(*x_0(it, c))
                            else:
                                dve.wait_ge(*x_l(it, i - 1))
                            xe = half_blocks(xv[:], sz, 0)
                            nc.vector.tensor_tensor(xe, xe, packed(bank("xx", i), sz), ALU.subtract).then_inc(x_l.sem, 1)
                        i = c * NL + lv
                        dve.wait_ge(*job["yy"](it, i))
                        if lv == 0:
                            dve.wait_ge(*y_1(it, c))
                        else:
                            dve.wait_ge(*y_l(it, i - 1))
                        yo = half_blocks(yv[:, c % 2], sz, 1)
                        nc.vector.tensor_tensor(yo, yo, packed(bank("yy", i), sz), ALU.subtract).then_inc(y_l.sem, 1)
                    if sc is not None and q == 0:
                        dve.wait_ge(*job["ks"](it, sc))
                        dve.wait_ge(*g_eg(it, 0))
                        dve.wait_ge(*r_f(it, sc - 1))
                        if sc == 0:
                            dve.wait_ge(*yr_f(it, -1))
                        nc.vector.tensor_tensor(tks[:], heads(bank("ks", sc)), bc(eg[:, 0, sc]), ALU.mult).then_inc(ks_t.sem, 1)
                        dve.wait_ge(*ks_t(it, sc))
                        dve.wait_ge(*rv_f(it, sc))
                        nc.vector.tensor_tensor(rv[:, sc % 2], rv[:, sc % 2], tks[:], ALU.subtract).then_inc(r_f.sem, 1)
                        dve.wait_ge(*job["qs"](it, sc))
                        dve.wait_ge(*job["ot"](it, sc - 1))
                        nc.vector.tensor_tensor(ao[:], heads(bank("qs", sc)), bc(eg[:, 0, sc]), ALU.mult).then_inc(ao_f.sem, 1)
                    if sc is not None and q == 1:
                        dve.wait_ge(*u_c(it, sc))
                        dve.wait_ge(*job["su"](it, sc - 1))
                        dve.wait_ge(*bke_f(it, 0))
                        if sc == 0:
                            dve.wait_ge(*yr_f(it, -1))
                        nc.vector.tensor_tensor(ve[:], ub[:], bc(bke[:, sc]), ALU.mult).then_inc(ve_f.sem, 1)
                    if sc is not None and q == 2:
                        dve.wait_ge(*job["su"](it, sc))
                        dve.wait_ge(*sdec_f(it, sc))
                        nc.vector.tensor_tensor(st[:], sdec[:], heads(bank("su", sc)), ALU.add).then_inc(s_f.sem, 1)
                        dve.wait_ge(*job["mv"](it, sc))
                        dve.wait_ge(*ao_f(it, sc))
                        nc.vector.tensor_tensor(ao[:], ao[:], heads(bank("mv", sc)), ALU.add).then_inc(o_f.sem, 1)
                    if sc is not None and q == 3:
                        dve.wait_ge(*job["ot"](it, sc))
                        dve.wait_ge(*z_f(it, 3))
                        yo = y32[:, 4:8, sc * C:(sc + 1) * C]
                        nc.vector.scalar_tensor_tensor(out=yo, in0=heads(bank("ot", sc)), scalar=vec[:, ONW:ONW + 1], in1=yo,
                                                       op0=ALU.mult, op1=ALU.mult).then_inc(yb_f.sem, 1)
                    if last:
                        sample_slot(it, slot)
                for m in range(8):
                    dve.wait_ge(*yhi_f(it, m))
                    if m == 0:
                        dve.wait_ge(*job["mv"](it, NC - 1))
                        dve.wait_ge(*ya_f(it, NG - 1))
                        dve.wait_ge(*yb_f(it, NC - 1))
                    nc.vector.tensor_tensor(ylo[:, m], y32[:, m], yhi[:, m].bitcast(F32), ALU.subtract).then_inc(ylo_f.sem, 1)
                if not last:
                    front_xn(dve, it)
                for m in range(8):
                    if m >= 1:
                        dve.wait_ge(*job["yt"](it, m - 1))
                        dve.wait_ge(*ylo_f(it, 7))
                        nc.vector.tensor_copy(ytok[:, :, (m - 1) * P:m * P], heads(bank("yt", m - 1))).then_inc(ytok_f.sem, 1)
                    if last:
                        sample_out(it, m)
                    else:
                        front_lo(dve, it, m)
                if last:
                    sample_out(it, 8)
                dve.wait_ge(*job["yt"](it, 7))
                nc.vector.tensor_copy(ytok[:, :, 7 * P:8 * P], heads(bank("yt", 7))).then_inc(ytok_f.sem, 1)
                dve.wait_ge(*ry_f(it, 0))
                dve.wait_ge(*ytok_f(it, 7))
                for t in range(4):
                    nc.vector.scalar_tensor_tensor(out=ytok[:, t], in0=ytok[:, t], scalar=ry[:, t:t + 1], in1=gpw[:],
                                                   op0=ALU.mult, op1=ALU.mult).then_inc(yn_f.sem, 1)
                dve.wait_ge(*xres_in(it, 0))
                for t in range(4):
                    dve.wait_ge(*yn_f(it, t))
                    nc.vector.tensor_tensor(ytok[:, t], ytok[:, t], xres[:, t], ALU.add).then_inc(yr_f.sem, 1)

            with dve.Fori(0, NB - 1) as it:
                block_of(it)
            block_of(LAST, last=True)
            dve.wait_ge(*s_f(LAST, NC - 1))
            dve.wait_ge(*hist_out(LAST, NQ - 1))
            dve.wait_ge(*u_out(LAST, NG - 1))
            dve.nop().then_inc(s_end, 1)
            for e in range(2):
                dve.wait_ge(*done("pe", f"syt{e}"))
                nc.vector.tensor_copy(ys[:, e * 512:(e + 1) * 512], bank("syt", e)[0:NS, :]).then_inc(*step("dve", f"ys{e}"))
            dve.wait_ge(*done("pool", "ry"))
            nc.vector.scalar_tensor_tensor(out=ys[:], in0=ys[:], scalar=s8[:, 6:7], in1=gr8[:], op0=ALU.mult,
                                           op1=ALU.mult).then_inc(*step("dve", "yn"))
            dve.wait_ge(*done("dve", "yn"))
            nc.vector.tensor_tensor(ys[:], ys[:], xs[:], ALU.add).then_inc(*step("dve", "yr"))

        def held(pool):
            pool.nop().then_inc(pool_held, 1)

        def front_rx(pool, it):
            pool.wait_ge(*xsq(it, 3))
            if it is not PROLOGUE:
                pool.wait_ge(*xn(it, -1))
            held(pool)
            nc.gpsimd.tensor_scalar(rx0[:], ssx[:], 1.0 / DM, EPS, ALU.mult, ALU.add).then_inc(rx_0.sem, 1)
            pool.wait_ge(*rx_0(it, 0))
            nc.gpsimd.tensor_tensor(rx[:], rx0[:], mhalf[:, 0:4], ALU.pow).then_inc(rx_f.sem, 1)

        def front_hi(pool, it, m):
            pool.wait_ge(*h_f(it, m))
            held(pool)
            nc.gpsimd.tensor_copy(hhi[:, m], htmp[:, m % 2]).then_inc(h_hi.sem, 1)

        @block.gpsimd
        def _(pool):
            for ev in (w_lo, hist_in, hist_out, sk_0, sk_f, odb_0, u_in, u_out, u_add, win_f, ftab_f, gb_in,
                       sdec_f, o_n0, o_n, o_sq, o_s, ry_0, ry_f):
                pool.nop().then_inc(ev.sem, ev.per)
            pool.dma_start(poolw[:], a["pool_w"]).then_inc(y_out.sem, 16)
            nc.gpsimd.memset(half[:], 0.5)
            nc.gpsimd.memset(mhalf[:], -0.5).then_inc(s_modc, 1)
            pool.wait_ge(s_modc, 1)
            front_rx(pool, PROLOGUE)
            pool.wait_ge(*done("act", "x_sq"))
            nc.gpsimd.tensor_scalar(s8[:, 1:2], s8[:, 0:1], 1.0 / DM, EPS, ALU.mult, ALU.add).then_inc(*step("pool", "rx0"))
            pool.wait_ge(*done("pool", "rx0"))
            nc.gpsimd.tensor_tensor(s8[:, 2:3], s8[:, 1:2], mhalf[0:NS, 0:1], ALU.pow).then_inc(*step("pool", "rx"))
            for m in range(8):
                front_hi(pool, PROLOGUE, m)
            for t in range(2):
                pool.wait_ge(*w_hi(0, t))
                nc.gpsimd.tensor_tensor(wlo[:, t], wraw[:, t], whi[:, t].bitcast(F32), ALU.subtract).then_inc(w_lo.sem, 1)

            def split_lo(it, t):
                pool.wait_ge(*w_hi(it + (t + 1) // NW, (t + 1) % NW))
                nc.gpsimd.tensor_tensor(wlo[:, (t + 1) % 2], wraw[:, (t + 1) % 2], whi[:, (t + 1) % 2].bitcast(F32),
                                        ALU.subtract).then_inc(w_lo.sem, 1)

            def u_tile(it, t):
                g = t - UA
                u = ubuf[:, g % 2]
                pool.wait_ge(*pooled_f(it, g - 2))
                pool.wait_ge(*u_out(it, g - 2))
                held(pool)
                nc.gpsimd.tensor_copy(u[:, 0:PB], uhist[:, g]).then_inc(u_in.sem, 1)
                pool.wait_ge(*u_in(it, g))
                pool.wait_ge(*u_f(it, g))
                held(pool)
                nc.gpsimd.tensor_copy(uhist[:, g], u[:, BT:BT + PB]).then_inc(u_out.sem, 1)
                src, base = u, g * (g + 1) // 2
                for s in range(g + 1):
                    dst = win[:, (g + g - s) % 2]
                    lo = (2 << s) - 1
                    if s:
                        pool.wait_ge(*u_add(it, base + s - 1))
                    elif g:
                        pool.wait_ge(*u_add(it, base - 1))
                    if s == 0 or s == 1:
                        pool.wait_ge(*pooled_f(it, g - 1))
                        pool.wait_ge(*pooled_f(it, g - 2))
                        pool.wait_ge(*win_f(it, g - 1))
                    nc.gpsimd.tensor_tensor(dst[:, lo:], src[:, lo:], src[:, lo - (1 << s):BT + PB - (1 << s)],
                                            ALU.add).then_inc(u_add.sem, 1)
                    src = dst
                pool.wait_ge(*u_add(it, base + g))
                pool.wait_ge(*ftab_f(it, -1))
                nc.gpsimd.tensor_tensor(src[:, PB:PB + 16], src[:, PB:PB + 16], ftab[:, g], ALU.mult).then_inc(win_f.sem, 1)

            pool.wait_ge(s_prm2, 144)
            pool.wait_ge(s_const, 64)
            pool.wait_ge(s_pre, 1)
            def block_of(it, last=False):
                for t in range(NQ):
                    pool.wait_ge(*conv(it, t - 2))
                    pool.wait_ge(*hist_out(it, t - 2))
                    held(pool)
                    nc.gpsimd.tensor_copy(raw[:, t % 2, 0:CK - 1], hist[:, t]).then_inc(hist_in.sem, 1)
                    if t:
                        split_lo(it, t)
                    pool.wait_ge(*hist_in(it, t))
                    pool.wait_ge(*raw_f(it, t))
                    held(pool)
                    nc.gpsimd.tensor_copy(hist[:, t], raw[:, t % 2, BT:BT + CK - 1]).then_inc(hist_out.sem, 1)
                pool.wait_ge(*ss_ev(it, 7))
                pool.wait_ge(*sk_f(it, -1))
                held(pool)
                nc.gpsimd.tensor_scalar(sk0[:], ssb[:, 0:4].rearrange("p h c -> p c h"), EPS, None, ALU.add).then_inc(sk_0.sem, 1)
                pool.wait_ge(*sk_0(it, 0))
                pool.wait_ge(*rv_f(it, -1))
                nc.gpsimd.tensor_tensor(sk[:].rearrange("p c h -> p (c h)"), sk0[:].rearrange("p c h -> p (c h)"), half[:], ALU.pow).then_inc(sk_f.sem, 1)
                pool.wait_ge(*o_n0(it, -1))
                held(pool)
                nc.gpsimd.tensor_scalar(odb[:], ssb[:, 4:8].rearrange("p h c -> p c h"), EPS, EPS * P, ALU.add, ALU.mult).then_inc(odb_0.sem, 1)
                for slot, (c, p, sc, q, thirds) in enumerate(PLAN):
                    if c is not None and p == 0:
                        pool.wait_ge(*job["gb"](it, c - 1))
                        pool.wait_ge(*g_g(it, 0))
                        held(pool)
                        nc.gpsimd.tensor_copy(gb4[:], bc(gg[:, c])).then_inc(gb_in.sem, 1)
                    for n in thirds:
                        if n < 36 and n % 3 == 0:
                            split_lo(it, 12 + n // 3)
                        if n % 3 == 2 and UA <= 12 + n // 3 < OUT:
                            u_tile(it, 12 + n // 3)
                    if sc is not None and q == 0:
                        pool.wait_ge(*g_eg(it, 0))
                        pool.wait_ge(*s_f(it, sc - 1))
                        nc.gpsimd.tensor_tensor(sdec[:], st[:], bc(eg[:, 1, sc]), ALU.mult).then_inc(sdec_f.sem, 1)
                    if sc is not None and q == 2:
                        pool.wait_ge(*o_sq4(it, 4 * sc + 3))
                        pool.wait_ge(*o_n(it, sc - 1))
                        pool.wait_ge(*odb_0(it, 0))
                        held(pool)
                        nc.gpsimd.tensor_scalar(on0[:], oss[:], 1.0 / P, None, ALU.mult).then_inc(o_n0.sem, 1)
                        pool.wait_ge(*o_n0(it, sc))
                        nc.gpsimd.tensor_tensor(on0[:], on0[:], odb[:, sc], ALU.add).then_inc(o_n.sem, 1)
                        pool.wait_ge(*o_n(it, sc))
                        pool.wait_ge(*o_s(it, sc - 1))
                        nc.gpsimd.tensor_tensor(on[:], on0[:], mhalf[:, 0:H], ALU.pow).then_inc(o_sq.sem, 1)
                        pool.wait_ge(*o_sq(it, sc))
                        nc.gpsimd.tensor_tensor(ao[:], ao[:], bc(on[:]), ALU.mult).then_inc(o_s.sem, 1)
                    if last and slot == SAMPLE_SLOT["root"]:
                        pool.wait_ge(*silu(it, NQ - 1))
                        nc.gpsimd.memset(spw[:], -0.5).then_inc(*step("pool", "half"))
                        pool.wait_ge(*done("dve", "sst1"))
                        pool.wait_ge(*done("pool", "half"))
                        nc.gpsimd.tensor_tensor(rk[:, 1].rearrange("p h s -> p (h s)"), sst[:, 0:4].rearrange("p h s -> p (h s)"),
                                                spw[:], ALU.pow).then_inc(*step("pool", "rk"))
                    if last and slot == SAMPLE_SLOT["mean"]:
                        pool.wait_ge(*done("dve", "ms2"))
                        nc.gpsimd.tensor_tensor(rk[:, 1].rearrange("p h s -> p (h s)"), rk[:, 0].rearrange("p h s -> p (h s)"),
                                                spw[:], ALU.pow).then_inc(*step("pool", "rstd"))
                if not last:
                    front_rx(pool, it)
                for m in range(8):
                    if not (last and m == 7):
                        split_lo(it, OUT + m)
                    if m == 0 and not last:
                        pool.wait_ge(*proj(it, OUT - 1))
                    if not last:
                        front_hi(pool, it, m)
                if not last:
                    split_lo(it, NW)
                pool.wait_ge(*ysq(it, 3))
                pool.wait_ge(*ry_f(it, -1))
                held(pool)
                nc.gpsimd.tensor_scalar(ry0[:], ssy[:], 1.0 / DM, EPS, ALU.mult, ALU.add).then_inc(ry_0.sem, 1)
                pool.wait_ge(*ry_0(it, 0))
                pool.wait_ge(*yn_f(it, -1))
                nc.gpsimd.tensor_tensor(ry[:], ry0[:], mhalf[:, 0:4], ALU.pow).then_inc(ry_f.sem, 1)
                for t in range(4):
                    pool.wait_ge(*yr_f(it, t))
                    pool.dma_start(a["y"][it, t], ytok[:, t]).then_inc(y_out.sem, 16)
                pool.wait_ge(*win_f(it, NG - 1))
                held(pool)
                nc.gpsimd.memset(ftab[:], 1.0).then_inc(ftab_f.sem, 1)


            with pool.Fori(0, NB - 1) as it:
                block_of(it)
            block_of(LAST, last=True)
            pool.wait_ge(*done("act", "y_sq"))
            nc.gpsimd.tensor_scalar(s8[:, 5:6], s8[:, 4:5], 1.0 / DM, EPS, ALU.mult, ALU.add).then_inc(*step("pool", "ry0"))
            pool.wait_ge(*done("pool", "ry0"))
            nc.gpsimd.tensor_tensor(s8[:, 6:7], s8[:, 5:6], mhalf[0:NS, 0:1], ALU.pow).then_inc(*step("pool", "ry"))

        def front_pe(pe, it, m):
            bank_free(pe, it, "xf", m, (xn, 3))
            for t in range(4):
                last = nc.tensor.transpose(bank("xf", m)[:, t * P:(t + 1) * P], xb[:, t, m * P:(m + 1) * P], ident[:])
            last.then_inc(job["xf"].sem, 1)

        @block.tensor
        def _(pe):
            for ev in [proj] + [e for k, e in job.items() if k != "xf"]:
                pe.nop().then_inc(ev.sem, ev.per)
            pe.wait_ge(s_const, 64)
            pe.wait_ge(s_pre, 1)
            pe.wait_ge(s_cact, 1)
            def turn_rows(j, dst, col):
                pe.wait_ge(s_rows, j + 1)
                for i in range(4):
                    last = nc.tensor.transpose(dst[:, col + 9 * i:col + 9 * (i + 1)], rows9[j][:, i * P:(i + 1) * P],
                                               ident[0:1 + NS, 0:1 + NS])
                return last

            for j in range(6):
                pe.wait_ge(ada_in[j], 16)
                if j >= 2:
                    pe.wait_ge(s_rows, j - 1)
                for k in range(KT):
                    last = nc.tensor.matmul(acc[j % 2][0:1 + NS, :], cin[:, k, :], wada[j][:, k], start=(k == 0),
                                            stop=(k == KT - 1))
                last.then_inc(s_mod, 1)
                if 1 <= j <= 3:
                    turn_rows(j - 1, spare[0], (j - 1) * 36)
                if j == 2:
                    for m in range(3):
                        front_pe(pe, PROLOGUE, m)
                if j == 3:
                    turn_rows(3, spare[0], 108).then_inc(s_tr, 1)
                    pe.wait_ge(*done("dve", "xn"))
                    for k in range(KT):
                        last = nc.tensor.transpose(spare[2][:, k * NS:(k + 1) * NS], xrow[:, k * P:(k + 1) * P], ident[0:NS, 0:NS])
                    last.then_inc(*step("pe", "hs"))
                    for m in range(3, 5):
                        front_pe(pe, PROLOGUE, m)
                if j == 4:
                    for m in range(5, 8):
                        front_pe(pe, PROLOGUE, m)
            turn_rows(4, spare[1], 0)
            turn_rows(5, spare[1], 36).then_inc(s_tr, 1)
            pe.wait_ge(s_pre, 2)
            pe.wait_ge(*done("dve", "h"))
            for m in range(2):
                pe.wait_ge(s_trc, 2 * m + 2)
                nc.tensor.matmul((spare[2], spare[0])[m][:], ones[0:1, :], grow[0:1, m * 512:(m + 1) * 512], start=True,
                                 stop=True).then_inc(s_row, 1)
            pe.wait_ge(s_rowc, 2)

            def tile(it, t, third=None):
                hi, lo = (hhi, hlo) if t < OUT else (yhi, ylo)
                ks = range(KT) if third is None else (range(0, 3), range(3, 6), range(6, 8))[third]
                for k in ks:
                    if k == 0:
                        pe.wait_ge(*w_lo(it, t))
                        tile_reader(pe, it, t)
                        if t == OUT:
                            pe.wait_ge(*ylo_f(it, 7))
                    if t == 0:
                        pe.wait_ge(*h_lo(it, k - 8))
                    nc.tensor.matmul(acc[t % 2][:], whi[:, t % 2, k], hi[:, k], start=(k == 0), stop=False)
                    nc.tensor.matmul(acc[t % 2][:], whi[:, t % 2, k], lo[:, k], start=False, stop=False)
                    last = nc.tensor.matmul(acc[t % 2][:], wlo[:, t % 2, k], hi[:, k], start=False, stop=(k == KT - 1))
                if ks[-1] == KT - 1:
                    last.then_inc(proj.sem, 1)

            def four(it, kind, i, left, right, *needs, n=C):
                bank_free(pe, it, kind, i, *needs)
                for h in range(H):
                    last = nc.tensor.matmul(bank(kind, i)[:, h * n:(h + 1) * n], left(h), right(h), start=True, stop=True)
                last.then_inc(job[kind].sem, 1)

            def turn(it, kind, n, what, *needs):
                bank_free(pe, it, kind, n, *needs)
                for h in range(H):
                    last = nc.tensor.transpose(bank(kind, n)[:, h * C:(h + 1) * C], what(h), ident[:])
                last.then_inc(job[kind].sem, 1)

            def sample_tile(it, t):
                rhs = hs if t < OUT else ym
                pe.wait_ge(*w_lo(it, t))
                if t == 0:
                    pe.wait_ge(*done("dve", "h"))
                if t == OUT:
                    pe.wait_ge(*done("dve", "yma"))
                    pe.wait_ge(*done("dve", "ymb"))
                bank_free(pe, it, "sp", t)
                for k in range(KT):
                    last = nc.tensor.matmul(bank("sp", t)[:, 0:NS], wraw[:, t % 2, k], rhs[:, k], start=(k == 0), stop=(k == KT - 1))
                last.then_inc(*step("pe", f"sp{t}"))

            def sample_slot(it, slot):
                if slot == SAMPLE_SLOT["square"]:
                    bank_free(pe, it, "s2")
                    pe.wait_ge(*done("dve", "sq1"))
                    nc.tensor.matmul(bank("s2")[:, 0:96], ones[:], sqs[:].rearrange("p t s -> p (t s)"), start=True,
                                     stop=True).then_inc(*step("pe", "s20"))
                    bank_free(pe, it, "kv")
                    pe.wait_ge(*done("dve", "kq1"))
                    pe.wait_ge(sm_ssm, 16)
                    for s in range(NS):
                        for h in range(H):
                            col = 2 * (s * H + h)
                            last = nc.tensor.matmul(bank("kv")[:, col:col + 2], ssm[:, s, h], kq[:, s, h], start=True, stop=True)
                    last.then_inc(*step("pe", "kv0"))
                if slot == SAMPLE_SLOT["rows"]:
                    bank_free(pe, it, "dt")
                    pe.wait_ge(*done("dve", "d5"))
                    nc.tensor.transpose(bank("dt")[0:32, 0:P], kq[:, :, :, 0].rearrange("p s h -> p (s h)"), ident[:])
                    nc.tensor.transpose(bank("dt")[0:32, P:2 * P], dl[:, 2].rearrange("p h s -> p (h s)"), ident[:]
                                        ).then_inc(*step("pe", "dt0"))
                    bank_free(pe, it, "son")
                    pe.wait_ge(*done("dve", "o2"))
                    nc.tensor.matmul(bank("son")[:, 0:32], ones[:], dl[:, 3].rearrange("p h s -> p (h s)"), start=True,
                                     stop=True).then_inc(*step("pe", "son0"))
                if slot == SAMPLE_SLOT["pooled"]:
                    bank_free(pe, it, "spl")
                    pe.wait_ge(*done("dve", "pl8"))
                    for g in range(NG):
                        last = nc.tensor.matmul(bank("spl")[:, g * NS:(g + 1) * NS], poolw[:, g], pls[:, g], start=True, stop=True)
                    last.then_inc(*step("pe", "spl0"))

            def sample_state(it, m):
                bank_free(pe, it, "sop", m)
                pe.wait_ge(*done("dve", "krow"))
                for h in range(H):
                    last = nc.tensor.matmul(bank("sop", m)[:, h * P:(h + 1) * P], krow[:, m * H + h], drow[:, 1], start=True,
                                            stop=True)
                last.then_inc(*step("pe", f"sop{m}"))

            def sample_rows(it, kind, what):
                for m in range(8):
                    if m % 4 == 0:
                        bank_free(pe, it, kind, m // 4)
                    last = nc.tensor.transpose(bank(kind, m // 4)[0:NS, (m % 4) * P:(m % 4 + 1) * P], what(m), ident[:])
                    if m % 4 == 3:
                        last.then_inc(*step("pe", f"{kind}{m // 4}"))

            def block_of(it, last=False):
                for t in range(NQ):
                    if last:
                        sample_tile(it, t)
                    tile(it, t)
                    if t == 1:
                        bank_free(pe, it, "gates")
                        for k in range(KT):
                            nc.tensor.matmul(bank("gates")[0:8, :], wgh[:, k], hhi[:, k], start=(k == 0), stop=False)
                            nc.tensor.matmul(bank("gates")[0:8, :], wgh[:, k], hlo[:, k], start=False, stop=False)
                            mm = nc.tensor.matmul(bank("gates")[0:8, :], wgl[:, k], hhi[:, k], start=False,
                                                    stop=(k == KT - 1))
                        mm.then_inc(job["gates"].sem, 1)
                    if t == 2:
                        bank_free(pe, it, "gt", 0, (g_c, 0))
                        pe.nop().then_inc(pe_held, 1)
                        for c in range(NC):
                            mm = nc.tensor.transpose(bank("gt")[:, c * 8:(c + 1) * 8], gsb[:, c * C:(c + 1) * C], ident[0:8, 0:8])
                        mm.then_inc(job["gt"].sem, 1)
                    if t == 5:
                        bank_free(pe, it, "gc", 0, (g_g, 0))
                        g16 = gg[:].rearrange("p c h -> p (c h)")
                        nc.tensor.matmul(bank("gc")[:, 0:16], upper[:], g16, start=True, stop=True)
                        nc.tensor.matmul(bank("gc")[:, 16:32], ones[:], g16, start=True, stop=True).then_inc(job["gc"].sem, 1)
                    if t >= 2 and t - 2 < 8:
                        bank_free(pe, it, "ss", t - 2, (sq, t - 2))
                        for c in range(NC):
                            mm = nc.tensor.matmul(bank("ss", t - 2)[:, c:c + 1], tmpa[:, t % 2, c * C:(c + 1) * C],
                                                    ones[:, 0:1], start=True, stop=True)
                        mm.then_inc(job["ss"].sem, 1)
                    if last and t == 6:
                        bank_free(pe, it, "sg")
                        for k in range(KT):
                            mm = nc.tensor.matmul(bank("sg")[0:NS, 0:8], hs[:, k], wgr[:, k], start=(k == 0), stop=(k == KT - 1))
                        mm.then_inc(*step("pe", "sg0"))
                if last:
                    bank_free(pe, it, "sb")
                    pe.wait_ge(*done("dve", "g_d1"))
                    nc.tensor.matmul(bank("sb")[:, 0:64], ones[0:NS, :], gdg[:].rearrange("p s e -> p (s e)"), start=True,
                                     stop=True).then_inc(*step("pe", "sb0"))
                for slot, (c, p, sc, q, thirds) in enumerate(PLAN):
                    for n in thirds:
                        if last and n < 36 and n % 3 == 0:
                            sample_tile(it, 12 + n // 3)
                        if n < 36:
                            tile(it, 12 + n // 3, n % 3)
                        g = pool_after(n)
                        if g is not None:
                            bank_free(pe, it, "pool", g, (pooled_f, g))
                            nc.tensor.matmul(bank("pool", g)[:], poolw[:, g], pooled[:, g % 2], start=True,
                                             stop=True).then_inc(job["pool"].sem, 1)
                    if c is not None:
                        s = slice(c * C, (c + 1) * C)
                        if p == 0:
                            turn(it, "kt", c, lambda h: cq[:, h, s], (silu, NQ - 1))
                            turn(it, "vt", c, lambda h: cq[:, 8 + h, s])
                            four(it, "gb", c, lambda h: gb4[:, h], lambda h: upper[:], (gb_in, c))
                        elif p == 1:
                            four(it, "kk", c, lambda h: cq[:, h, s], lambda h: cq[:, h, s])
                            four(it, "qk", c, lambda h: cq[:, h, s], lambda h: cq[:, 4 + h, s])
                        elif p == 2:
                            turn(it, "xt", c, lambda h: yv[:, c % 2, h], (y_1, c))
                        elif p % 2:
                            i = c * NL + (p - 3) // 2
                            x_ready = (x_0, c) if p == 3 else (x_l, c * (NL - 1) + (p - 3) // 2 - 1)
                            sz = LEVELS[(p - 3) // 2]
                            four(it, "w", i, lambda h: lt[:, h], lambda h: head_blocks(xv[:, h], sz, 0), x_ready, n=C // 2)
                        else:
                            lv = (p - 4) // 2
                            sz = LEVELS[lv]
                            i = c * NL + lv
                            ready = [(w_f, i)] + ([(y_l, i - 1)] if lv else [])
                            if lv < NL - 1:
                                four(it, "xx", c * (NL - 1) + lv, lambda h: yv[:, c % 2, h],
                                     lambda h: head_blocks(wb[:, h], sz, 0), *ready, n=C // 2)
                            four(it, "yy", i, lambda h: wb[:, h], lambda h: head_blocks(yv[:, c % 2, h], sz, 1), *ready,
                                 n=C // 2)
                    if sc is not None:
                        s = slice(sc * C, (sc + 1) * C)
                        if q == 0:
                            four(it, "ks", sc, lambda h: cq[:, h, s], lambda h: st[:, h], (s_f, sc - 1))
                            four(it, "qs", sc, lambda h: cq[:, 4 + h, s], lambda h: st[:, h])
                        elif q == 1:
                            four(it, "u", sc, lambda h: yv[:, sc % 2, h], lambda h: rv[:, sc % 2, h],
                                 (r_f, sc), (y_l, sc * NL + NL - 1))
                        elif q == 2:
                            four(it, "su", sc, lambda h: ktok[:, sc % 2, h], lambda h: ve[:, h], (ve_f, sc), (kt_f, sc))
                            four(it, "mv", sc, lambda h: mtb[:, sc % 2, h], lambda h: ub[:, h], (u_c, sc), (mt_f, sc))
                        else:
                            turn(it, "ot", sc, lambda h: ao[:, h], (o_s, sc))
                    if last:
                        sample_slot(it, slot)
                for m in range(8):
                    if last:
                        sample_tile(it, OUT + m)
                    tile(it, OUT + m)
                    if m >= 1:
                        turn(it, "yt", m - 1, lambda t: ytt[:, (m - 1) % 2, t * P:(t + 1) * P], (ytt_f, m - 1))
                    if not last:
                        front_pe(pe, it, m)
                    if last:
                        sample_state(it, m)
                turn(it, "yt", 7, lambda t: ytt[:, 1, t * P:(t + 1) * P], (ytt_f, 7))
                if last:
                    sample_rows(it, "sgt", lambda e: mod[:, 16 + e, 1:1 + NS])
                    pe.wait_ge(*done("dve", "pj31"))
                    sample_rows(it, "syt", lambda m: hs[:, m])

            with pe.Fori(0, NB - 1) as it:
                block_of(it)
            block_of(LAST, last=True)


def layouts(i):
    import numpy as np

    f = lambda n: np.asarray(i[n])

    def tiles(w):
        return w.reshape(KT, P, -1, P).transpose(2, 1, 0, 3)

    w_in = f("w_in")[0]
    u, za, q, k, v, zb = (w_in[:, s:s + 512] for s in range(0, 3072, 512))
    x = f("x_prompt")[0].reshape(NB, 4, P, DM).transpose(0, 2, 1, 3)
    perm = lambda w: np.concatenate([w[..., 512:1024], w[..., 0:512], w[..., 1024:1536]], -1)
    j = np.arange(P)
    lm = []
    for s in (1,) + LEVELS:
        lm.append((j[:, None] // (2 * s) == j[None, :] // (2 * s)) & (j[:, None] // s < j[None, :] // s))
    lm[1:] = [m.T for m in lm[1:]]
    cnt = np.minimum(np.arange(16)[None] + 1, 2 << np.arange(NG)[:, None])
    ftab = (2 << np.arange(NG))[:, None] / cnt
    return {
        "x": x,
        "c_all": np.concatenate([f("c_prompt"), f("c_sample")]).T.reshape(KT, P, 1 + NS).transpose(1, 0, 2),
        "w": np.concatenate([tiles(np.concatenate([k, q, v, zb, za, u], 1)), tiles(f("w_out")[0])]),
        "w_gate": w_in[:, 3072:].reshape(KT, P, 8).transpose(1, 0, 2),
        "w_ada": f("w_ada")[0].reshape(KT, P, 6, BT).transpose(2, 1, 0, 3),
        "b_ada": f("b_ada")[0].reshape(24, P).T,
        "b_gate": f("b_ada")[:, 2 * DM:],
        "pre_w": f("pre_norm_w")[0].reshape(KT, P).T,
        "post_w": f("post_norm_w"),
        "conv_w": perm(f("conv_w")[0]).reshape(CK, NQ, P).transpose(2, 1, 0),
        "pool_w": f("pool_w")[0].transpose(1, 0, 2),
        "pool_scale": f("pool_scale")[0].reshape(NG, P).T,
        "a_log": f("a_log"), "dt_bias": f("dt_bias"),
        "o_norm": f("o_norm_w")[0].reshape(P, 1),
        "ident": np.eye(P, dtype=np.float32),
        "upper": (j[:, None] <= j[None, :]).astype(np.float32),
        "dmask": np.where(j[:, None] <= j[None, :], 0.0, -30000.0).astype(np.float32),
        "lmask": np.stack(lm, 1).astype(np.float32),
        "ftab": np.broadcast_to(ftab.astype(np.float32), (P, NG, 16)),
        "xs": f("x_sample").reshape(NS, DM),
        "s_conv": perm(f("state_conv")[0]).reshape(NS, CK - 1, NQ, P).transpose(3, 1, 2, 0),
        "s_pool": f("state_pool")[0].reshape(NS, PB, NG, P).transpose(3, 1, 2, 0),
        "s_ssm": f("state_ssm")[0].transpose(2, 0, 1, 3),
    }


OUTS = {"y": (NB, 4, P, DM), "o_pool": (P, NG, PB), "o_conv": (P, NQ, CK - 1), "o_ssm": (P, H, P),
        "ys": (NS, DM), "o_spool": (PB, P, NG, NS), "o_sconv": (CK - 1, P, NQ, NS), "o_sssm": (P, NS, H, P)}


def gather(r):
    import numpy as np

    def unperm(h):
        return np.concatenate([h[4:8], h[0:4], h[8:12]])

    return (
        r["y"].transpose(0, 1, 2, 3).reshape(1, SEQ, DM),
        r["ys"].reshape(NS, 1, DM),
        r["o_pool"].transpose(2, 1, 0).reshape(1, 1, PB, NG * P),
        unperm(r["o_conv"].transpose(1, 2, 0)).transpose(1, 0, 2).reshape(1, 1, CK - 1, NQ * P),
        r["o_ssm"].transpose(1, 0, 2)[None, None],
        r["o_spool"].transpose(3, 0, 2, 1).reshape(1, NS, PB, NG * P),
        unperm(r["o_sconv"].transpose(2, 3, 0, 1)).transpose(1, 2, 0, 3).reshape(1, NS, CK - 1, NQ * P),
        r["o_sssm"].transpose(1, 2, 0, 3)[None],
    )


def kernel(**inputs):
    import numpy as _np
    import concourse.bacc as _bacc
    from concourse.bass_utils import run_bass_kernel_spmd as _run

    nc = _bacc.Bacc("TRN2", target_bir_lowering=False, num_devices=1)
    arrays, aps = {}, {}
    for name, value in layouts(inputs).items():
        arrays[f"in_{name}"] = _np.ascontiguousarray(value)
        aps[name] = nc.dram_tensor(f"in_{name}", value.shape, F32, kind="ExternalInput").ap()
    for name, shape in OUTS.items():
        aps[name] = nc.dram_tensor(f"out_{name}", shape, F32, kind="ExternalOutput").ap()
    layer_kernel(nc, aps)
    r = _run(nc, [arrays], core_ids=[0]).results[0]
    return gather({name: r[f"out_{name}"] for name in OUTS})
```

```python
from contextlib import ExitStack

import concourse.bass as bass
from concourse import mybir

F32 = mybir.dt.float32
F32R = mybir.dt.float32r
BF16 = mybir.dt.bfloat16
ALU = mybir.AluOpType
ACT = mybir.ActivationFunctionType
AX = mybir.AxisListType

P = 128
DM = 1024
KT = DM // P
SEQ = 2048
BT = 512
NB = SEQ // BT
C = 128
NC = BT // C
H = 4
NQ = 12
NG = 4
CK = 4
PB = 15
NS = 8
NW = 32
ZB, ZA, UA, OUT = 12, 16, 20, 24
EPS = 1e-6
LEVELS = (2, 4, 8, 16, 32, 64)
NL = len(LEVELS)
NPREP = 3 + 2 * NL
SLOTS = (NC + 1) * NPREP
PARTS = 8 * (OUT - NQ)
HEAD = 5
TAIL = 2 * 8
FRONT = NC * NPREP - 5
GATES = 3
SUMS = 3
RAW = 3
BANKS = 6


class Event:

    def __init__(self, sem, per, step=1, credit=None, at=0, turns=1):
        self.sem, self.per, self.step = sem, per, step
        self.credit = per if credit is None else credit
        self.at, self.turns = at, turns

    def rank(self, n):
        return n * self.turns + self.at

    def __call__(self, it, n):
        return self.sem, (it * (self.per * self.turns * self.step)
                          + (self.credit * self.turns + self.rank(n) + 1) * self.step)


def scan_step(p):
    at = [1 + i * ((NPREP - 2) // 4) for i in range(4)]
    return at.index(p) if p in at else None


def slot_plan():
    out, n, full = [], 0, SLOTS - NPREP - 3
    for k in range(SLOTS):
        r, p = divmod(k, NPREP)
        q = scan_step(p)
        upto = min(PARTS, HEAD + (k + 1) * (PARTS - HEAD) // full + 1) + max(0, min(TAIL, (k + 1 - full) * TAIL // 3))
        out.append((r if r < NC else None, p, r - 1 if r > 0 and q is not None else None, q,
                    list(range(n, upto))))
        n = upto
    return out


PLAN = slot_plan()


def norm_step(slot):
    for n in (1, 2):
        if slot >= n and PLAN[slot - n][2] is not None and PLAN[slot - n][3] == 2:
            return PLAN[slot - n][2], n
    return None, 0


def split_step(slot):
    return PLAN[slot - 2][2] if slot >= 2 and PLAN[slot - 2][3] == 3 and PLAN[slot - 2][2] != NC - 1 else None


def pool_after(n):
    g, rest = divmod(n - 8 * (UA - NQ) - 23, 8)
    return g if rest == 0 and 0 <= g < NG else None


SAMPLE_SLOT = {"conv": 2, "square": 4, "root": 5, "delta": 9, "rows": 11, "mean": 12, "gate": 38, "pool": 54,
               "pooled": 56, "mixed": 57}
SAMPLE_JOBS = ("sp", "so", "sg", "sb", "s2", "kv", "dt", "son", "spl", "sgt", "sop")


def absent(kind, last):
    return kind == "xf" if last else kind in SAMPLE_JOBS


def psum_jobs():
    jobs = []
    for t in range(NQ):
        if t >= 2:
            jobs.append(("sp", t))
        if t == GATES:
            jobs.append(("gates", 0))
        if t == GATES + 1:
            jobs.append(("gt", 0))
        if t == GATES + 5:
            jobs.append(("gc", 0))
        if t >= SUMS and t - SUMS < 8:
            jobs.append(("ss", t - SUMS))
        if t == 6:
            jobs.append(("sg", 0))
    jobs.append(("sb", 0))
    for slot, (c, p, sc, q, parts) in enumerate(PLAN):
        for n in parts:
            if n < PARTS and n % 8 == 0:
                jobs.append(("sp", NQ + n // 8))
            if pool_after(n) is not None:
                jobs.append(("pool", pool_after(n)))
        if c is not None:
            if p == 0:
                jobs += [("kt", c), ("vt", c), ("gb", c)]
            elif p == 1:
                jobs += [("kk", c), ("qk", c)]
            elif p == 2:
                jobs.append(("xt", c))
            elif p % 2:
                jobs.append(("w", c * NL + (p - 3) // 2))
            else:
                lv = (p - 4) // 2
                if lv < NL - 1:
                    jobs.append(("xx", c * (NL - 1) + lv))
                jobs.append(("yy", c * NL + lv))
        if sc is not None:
            jobs += {0: [("ks", sc), ("qs", sc)], 1: [("u", sc)], 2: [("mv", sc), ("su", sc)],
                     3: [("ot", sc)]}[q]
            if sc == NC - 1 and q == 2:
                early = len(jobs)
                jobs += [("so", 0), ("sp", OUT), ("out", 0), ("out", 1)]
            if sc == NC - 1 and q == 3:
                jobs.append(("sp", OUT + 1))
        jobs += {"square": [("s2", 0), ("kv", 0)], "rows": [("dt", 0), ("son", 0)], "pooled": [("spl", 0)]}.get(
            next((n for n, at in SAMPLE_SLOT.items() if at == slot), None), [])
    for m in range(8):
        jobs.append(("xf", m))
        if m == 4:
            jobs.append(("so", 1))
        if m >= 2:
            jobs.append(("sp", OUT + m))
        if m == 4:
            jobs += [("out", 2), ("out", 3)]
        jobs.append(("sop", m))
    jobs += [("sgt", 0), ("sgt", 1)]
    banks = [n % BANKS for n in range(early)]
    turn = 0
    for kind, n in jobs[early:]:
        if kind == "sp":
            banks.append(None)
        elif kind in ("out", "so"):
            banks.append(4 + n % 2 if kind == "out" else 0)
        else:
            banks.append(1 + turn % 3)
            turn += 1
    return jobs, banks


JOBS, JOB_BANK = psum_jobs()
JOB_AT = {job: n for n, job in enumerate(JOBS)}


def sample_plan_steps():
    steps = {"conv": ["cv0", "cv1", "cv2", "cv3", "cv4", "cv5", "cv6"], "square": ["sq0", "sq1", "kq0", "kq1"],
             "root": ["sst0", "sst1", "d0", "d1"], "delta": ["d2", "d3", "d4", "d5", "o0", "o1", "o2"],
             "mean": ["drow", "ms0", "ms1", "ms2"], "gate": ["zs", "on", "ymb"],
             "pool": [f"pl{i}" for i in range(9)], "mixed": ["ym0", "ym1", "ym2", "yma"]}
    out = []
    for slot, (c, p, sc, q, parts) in enumerate(PLAN):
        out += [f"pj{NQ + n // 8}" for n in parts if n < PARTS and n % 8 == 0]
        for name, at in SAMPLE_SLOT.items():
            if at == slot:
                out += steps.get(name, [])
    return out


def sample_out_steps():
    out = []
    for m in range(9):
        out += ["krow"] if m == 0 else []
        out += ["ys0"] if m == 4 else []
        out += [f"se{m - 1}", f"sn{m - 1}"] if m else []
        out += ["gr0", "gr1"] if m == 8 else []
    return out


SAMPLE_STEPS = {
    "pe": ["hs", "sp0", "sp1"] + [f"{kind}{n}" for kind, n in JOBS if kind in SAMPLE_JOBS and kind != "so"],
    "act": ["x_sq", "g_tanh", "g_abs", "g_exp", "g_ln", "g_eg", "silu", "z_tanh", "y_sq"],
    "pool": ["rx0", "rx", "half", "rk", "rstd", "ry0", "ry"],
    "dve": (["xn", "h0", "h", "pj01", "pj1"] + [f"pj{t}" for t in range(2, 8)] + ["g_a"] + ["pj8"] + ["g_beta", "g_sp", "g_g"] + ["pj9", "pj10"]
            + ["g_d0", "g_d1", "pj11", "gvb"] + sample_plan_steps() + sample_out_steps() + ["ys1", "yn", "yr"]),
}


def layer_kernel(nc, a):
    ctx = ExitStack()
    with ctx:
        def sb(name, shape, dt=F32):
            return ctx.enter_context(nc.sbuf_tensor(name, shape, dt))

        def over(name, base, offset, shape, dt=F32):
            return nc.alloc_sbuf_tensor_at(name, shape, dt, offset=base + offset)

        def region(name, nbytes):
            sb(name, [P, nbytes // 4])
            return nc.sbuf_base - nbytes

        def event(name, per, step=1, credit=None):
            return Event(ctx.enter_context(nc.semaphore(name)), per, step, credit)

        def chain(name, per, *steps):
            shared = ctx.enter_context(nc.semaphore(name))
            return [Event(shared, per, at=i, turns=len(steps)) for i in range(len(steps))]

        def sem(name):
            return ctx.enter_context(nc.semaphore(name))

        KB = 1024
        ra = region("region_a", 32 * KB)
        cq = over("cq", ra, 0, [P, NQ, BT])
        mtb = over("mtb", ra, 24 * KB, [P, 2, H, C])
        yv = over("yv", ra, 28 * KB, [P, 2, H, C])
        yhi = over("yhi", ra, 0, [P, KT, BT], F32R)
        ylo = over("ylo", ra, 16 * KB, [P, KT, BT], F32R)
        rb = region("region_b", 16 * KB)
        ktok = over("ktok", rb, 0, [P, 2, H, C])
        rv = over("rv", rb, 4 * KB, [P, 2, H, C])
        ub = over("ub", rb, 8 * KB, [P, H, C])
        ve = over("ve", rb, 10 * KB, [P, H, C])
        ao = over("ao", rb, 12 * KB, [P, H, C])
        tks = over("tks", rb, 14 * KB, [P, H, C])
        xres = over("xres", rb, 0, [P, 4, DM])
        rc = region("region_c", 16 * KB)
        y32 = over("y32", rc, 0, [P, KT, BT])
        ytok = over("ytok", rc, 0, [P, 4, DM])
        rd = region("region_d", 32 * KB)
        hhi = over("hhi", rd, 0, [P, KT, BT], F32R)
        hlo = over("hlo", rd, 16 * KB, [P, KT, BT], F32R)
        re_ = region("region_e", 40 * KB)
        rf = region("region_f", 4 * KB)
        htmp = over("htmp", rf, 0, [P, 2, BT])
        rg = region("region_g", 4 * KB)
        cacc = over("cacc", rg, 0, [P, 2, BT])
        rh = region("region_h", 2 * KB)
        gsb = over("gsb", rh, 0, [8, BT])
        wraw = over("wraw", re_, 0, [P, 2, KT, P])
        whi = over("whi", re_, 8 * KB, [P, 2, KT, P], F32R)
        wlo = over("wlo", re_, 16 * KB, [P, 2, KT, P], F32R)
        xb = over("xb", re_, 24 * KB, [P, 4, DM])

        tmpa = sb("tmpa", [P, 2, BT])
        raw = sb("raw", [P, RAW, BT + CK - 1])
        ubuf = sb("ubuf", [P, 2, BT + PB])
        win = sb("win", [P, 2, BT + PB])
        pooled = sb("pooled", [P, 2, BT])
        dcy = sb("dcy", [P, H, C])
        lt = sb("lt", [P, H, C])
        xv = sb("xv", [P, H, C])
        wb = sb("wb", [P, H, C])
        st = sb("st", [P, H, C])
        sdec = sb("sdec", [P, H, C])
        gb4 = sb("gb4", [P, H, C])
        junk = sb("junk", [P, DM], BF16)
        hist = sb("hist", [P, NQ, CK - 1])
        uhist = sb("uhist", [P, NG, PB])
        ident = sb("ident", [P, P])
        upper = sb("upper", [P, P])
        ones = sb("ones", [P, P])
        dmask = sb("dmask", [P, P])
        lmask = sb("lmask", [P, NL + 1, P])
        gpw = sb("gpw", [P, DM])
        poolw = sb("poolw", [P, NG, P])
        wgr = sb("wgr", [P, KT, 8])
        wgh = sb("wgh", [P, KT, 8], F32R)
        wgl = sb("wgl", [P, KT, 8], F32R)
        cw = sb("cw", [P, NQ, CK])
        vec = sb("vec", [P, 64])
        bada = sb("bada", [P, 24])
        ftab = sb("ftab", [P, NG, 16])
        cin = sb("cin", [P, KT, 1 + NS])
        mod = sb("mod", [P, 24, 1 + NS])
        amul = sb("amul", [P, KT, 1 + NS])
        wada = [over(f"wada{j}", base, off, [P, KT, BT]) for j, (base, off) in enumerate(
            ((rd, 0), (rd, 16 * KB), (ra, 0), (ra, 16 * KB), (rc, 0), (rb, 0)))]
        rows9 = [t[0:1 + NS, j] for t in (tmpa, htmp, pooled) for j in range(2)]
        grow = ubuf[0:1].rearrange("p a b -> p (a b)")[:, 0:DM]
        pwr = win[0:1].rearrange("p a b -> p (a b)")[:, 0:DM]
        ssx = sb("ssx", [P, 4]); rx0 = sb("rx0", [P, 4]); rx = sb("rx", [P, 4])
        ssy = sb("ssy", [P, 4, 2]); ry0 = sb("ry0", [P, 4]); ry = sb("ry", [P, 4])
        half = sb("half", [P, 16]); mhalf = sb("mhalf", [P, 16])
        ga = sb("ga", [P, NC, H]); gab = sb("gab", [P, NC, H]); gl1 = sb("gl1", [P, NC, H])
        gsp = sb("gsp", [P, NC, H]); gg = sb("gg", [P, NC, H])
        btt = sb("btt", [P, NC, H]); beta = sb("beta", [P, NC, H])
        gcs = sb("gcs", [P, 2, NC, H]); eg = sb("eg", [P, 2, NC, H])
        gd = sb("gd", [P, NC, H]); ekg = sb("ekg", [P, NC, H])
        ssb = sb("ssb", [P, 8, NC])
        kk1 = sb("kk1", [P, NC, H]); kk2 = sb("kk2", [P, NC, H]); bb = sb("bb", [P, NC, H]); bke = sb("bke", [P, NC, H])
        sk0 = sb("sk0", [P, NC, H]); sk = sb("sk", [P, NC, H]); odb = sb("odb", [P, NC, H])
        oss = sb("oss", [P, H]); on0 = sb("on0", [P, H]); on = sb("on", [P, H])

        hs, pj01 = sb("hs", [P, KT, NS]), sb("pj01", [P, 2, NS])
        g8, gdg, s8 = sb("g8", [NS, 8, H]), sb("gdg", [NS, NS, 2 * H]), sb("s8", [NS, 8])
        xrow = gpw[0:NS, :]
        ssm = over("ssm", re_, 24 * KB, [P, NS, H, P])
        cbuf = over("cbuf", rf, 0, [P, CK - 1, NQ, NS])
        pbuf = over("pbuf", rf, 1152, [P, PB, NG, NS])
        pj = over("pj", rf, 3072, [P, 24, NS])
        gvb = over("gvb", rf, 3840, [P, NS, 2, H])
        ct, cs = over("ct", rg, 0, [P, NQ, NS]), over("cs", rg, 384, [P, NQ, NS])
        sqs = over("sqs", rg, 768, [P, NQ, NS])
        sst = over("sst", rg, 1152, [P, NQ, NS])
        kq = over("kq", rg, 1536, [P, NS, H, 2])
        zs, ym = over("zs", rg, 1792, [P, 8, NS]), over("ym", rg, 2048, [P, 8, NS])
        pls = over("pls", rg, 2304, [P, NG, NS])
        rk = over("rk", rg, 2432, [P, 2, H, NS])
        dl = over("dl", rg, 2688, [P, 4, H, NS])
        spw = over("spw", rg, 3200, [P, NS * H])
        drow = over("drow", rh, 0, [NS * H, 2, P])
        krow = over("krow", rd, 0, [NS * H, NS * H, P])
        xs, pw8, gr8, ys = (over(n, rd, (16 + 4 * j) * KB, [NS, DM]) for j, n in enumerate(("xs", "pw8", "gr8", "ys")))

        PREW, PSC, ONW, NEA, DTB = 0, 8, 12, 13, 17

        acc = [ctx.enter_context(nc.psum_tensor(f"acc{i}", [P, BT], F32)) for i in range(2)]
        ring = [ctx.enter_context(nc.psum_tensor(f"ring{i}", [P, BT], F32)) for i in range(BANKS)]

        def bank(kind, n=0):
            return ring[JOB_BANK[JOB_AT[kind, n]]]

        def out_bank(hf, t):
            return acc[t] if t < 2 else bank("out", 2 * hf + t - 2)

        def heads(t):
            return t[:, :].rearrange("p (h c) -> p h c", h=H)

        def bc(col, n=C):
            return col.unsqueeze(2).to_broadcast([P, H, n])

        def packed(t, s):
            return t[:, 0:H * C // 2].rearrange("p (b s) -> p b s", s=s)

        def half_blocks(t, s, odd):
            return t.rearrange("p h (b two s) -> p (h b) two s", two=2, s=s)[:, :, odd]

        def head_blocks(t, s, odd):
            return t.rearrange("p (b two s) -> p b two s", two=2, s=s)[:, :, odd]

        def level_mask(lv):
            return mbc(lmask[:, 1 + lv])

        def mbc(m):
            return m.unsqueeze(1).to_broadcast([P, H, C])

        x_in = event("x_in", 1, 4 * 16)
        xres_in = event("xres_in", 1, 4 * 16)
        w_in0, w_in1 = event("w_in0", NW // 2, 16), event("w_in1", NW // 2, 16)
        w_in = [w_in0, w_in1]
        y_out = event("y_out", 4, 16)
        w_hi, w_lo = event("w_hi", NW), event("w_lo", NW)
        proj = event("proj", NW)
        raw_f, hist_in, hist_out = event("raw_f", NQ), event("hist_in", NQ), event("hist_out", NQ)
        conv_a, conv, silu = event("conv_a", 3 * NQ), event("conv", NQ), event("silu", NQ)
        sq = event("sq", 8)
        ss_ev = event("ss_ev", 8)
        g_c, g_y, g_b, g_sp, g_g, gc_f, g_d, k_1, k_2, b_f, bke_f = chain(
            "dve_factors", 1, "g_c", "g_y", "g_b", "g_sp", "g_g", "gc_f", "g_d", "k_1", "k_2", "b_f", "bke_f")
        g_t, g_ab, g_e, g_l, g_eg, g_ekg = chain("act_factors", 1, "g_t", "g_ab", "g_e", "g_l", "g_eg", "g_ekg")
        sk_0, sk_f, odb_0, ry_f, ftab_f = chain(
            "pool_factors", 1, "sk_0", "sk_f", "odb_0", "ry_f", "ftab_f")
        tanh_f, z_f = event("tanh_f", 8), event("z_f", 8)
        u_f, u_in, u_out, u_add, win_f = (event("u_f", 4), event("u_in", 4), event("u_out", 4),
                                          event("u_add", 10), event("win_f", 4))
        pooled_f, ya_f = event("pooled_f", 4), event("ya_f", 4)
        kt_f, gb_in, d_e, x_0 = (event(n, NC) for n in ("kt_f", "gb_in", "d_e", "x_0"))
        rv_f, d_1, d_2, d_b, lt_f, mt_f, y_0, y_1 = chain(
            "dve_prep", NC, "rv_f", "d_1", "d_2", "d_b", "lt_f", "mt_f", "y_0", "y_1")
        w_f, y_l, x_l = event("w_f", NC * NL), event("y_l", NC * NL), event("x_l", NC * (NL - 1))
        ks_t, r_f, ao_f, ve_f, o_f, s_f, o_n, o_s, yb_f = chain(
            "dve_scan", NC, "ks_t", "r_f", "ao_f", "ve_f", "o_f", "s_f", "o_n", "o_s", "yb_f")
        o_rt = event("o_rt", NC)
        sdec_f, u_c = event("sdec_f", NC), event("u_c", NC)
        o_sq4 = event("o_sq4", 4 * NC)
        yhi_f = event("yhi_f", 8)
        ylo_f = event("ylo_f", 6)
        outp, ysq, ytok_f = event("outp", 6), event("ysq", 8), event("ytok_f", 8)
        yr_f, ry_0 = event("yr_f", 4), event("ry_0", 1)
        xsq, rx_0, rx_f, xn = event("xsq", 4), event("rx_0", 1), event("rx_f", 1), event("xn", 4)
        h_hi, h_lo = event("h_hi", 8), event("h_lo", 8)
        per_job = {"gates": 1, "gt": 1, "gc": 1, "ss": 8, "pool": 4, "w": NC * NL, "xx": NC * (NL - 1), "yy": NC * NL,
                   "out": 4, "xf": 8}
        job = {kind: event("job_" + kind, per_job.get(kind, NC)) for kind in dict.fromkeys(k for k, _ in JOBS)}
        reader = {"gates": [g_c], "gt": [g_y, g_t], "gc": [gc_f], "ss": [ss_ev], "pool": [ya_f], "kt": [kt_f], "vt": [rv_f],
                  "gb": [d_1], "kk": [lt_f], "qk": [mt_f], "xt": [x_0], "w": [w_f], "xx": [x_l], "yy": [y_l],
                  "ks": [ks_t], "qs": [ao_f], "u": [u_c], "su": [s_f], "mv": [o_f], "ot": [yb_f],
                  "out": [ytok_f], "xf": [h_hi]}

        s_const, s_prm, s_prm2, s_pre, s_end = (sem(n) for n in ("s_const", "s_prm", "s_prm2", "s_pre", "s_end"))
        s_cact, s_mod, s_modc, s_rows, s_tr, s_trc, s_row, s_rowc = (sem(n) for n in (
            "s_cact", "s_mod", "s_modc", "s_rows", "s_tr", "s_trc", "s_row", "s_rowc"))
        ada_in = [sem(f"ada_in{i}") for i in range(6)]
        out_sem = sem("out_sem")
        pool_held, pe_held = sem("pool_held"), sem("pe_held")
        sm_x0, sm_x, sm_st, sm_ssm = (sem(n) for n in ("sm_x0", "sm_x", "sm_st", "sm_ssm"))
        sample_sem = {who: sem("sample_" + who) for who in SAMPLE_STEPS}
        taken = dict.fromkeys(SAMPLE_STEPS, 0)

        def done(who, step):
            return sample_sem[who], SAMPLE_STEPS[who].index(step) + 1

        def step(who, name):
            assert SAMPLE_STEPS[who][taken[who]] == name, (who, name, SAMPLE_STEPS[who][taken[who]])
            taken[who] += 1
            return sample_sem[who], 1

        sample_reader = {"so": lambda n: done("dve", f"ys{n}"), "sp": lambda n: done("dve", f"pj{n}"), "sg": lambda n: done("dve", "g_a"),
                         "sb": lambda n: done("dve", "gvb"), "s2": lambda n: done("dve", "sst1"),
                         "kv": lambda n: done("dve", "d1"), "dt": lambda n: done("dve", "drow"),
                         "son": lambda n: done("dve", "ms0"), "spl": lambda n: done("dve", "yma"),
                         "sgt": lambda n: done("dve", f"gr{n}"), "sop": lambda n: done("dve", f"sn{n}")}

        def bank_free(eng, it, kind, n=0, *needs):
            before, late = JOB_AT[kind, n], False
            last = it is LAST
            while True:
                before -= 1
                if before < 0:
                    before, late, last = len(JOBS) - 1, True, False
                if JOB_BANK[before] == JOB_BANK[JOB_AT[kind, n]] and not absent(JOBS[before][0], last):
                    break
            needs = list(needs)
            pk, pn = JOBS[before]
            if pk == "out":
                pn = 4 * (pn // 2) + 2 + pn % 2
            if pk in SAMPLE_JOBS:
                eng.wait_ge(*sample_reader[pk](pn))
            elif not (late and it is PROLOGUE):
                needs += [(ev, pn - ev.per if late else pn) for ev in reader[pk]]
            latest = {}
            for ev, m in needs:
                if ev.sem not in latest or ev.rank(m) > latest[ev.sem][0]:
                    latest[ev.sem] = ev.rank(m), ev, m
            for _, ev, m in latest.values():
                eng.wait_ge(*ev(it, m))

        PROLOGUE, LAST = -1, NB - 1

        def tile_reader(eng, it, t):
            t = t - 2
            if t < 0:
                eng.wait_ge(*ytok_f(it, t - 2))
            elif t < NQ:
                eng.wait_ge(*raw_f(it, t))
            elif t < UA:
                eng.wait_ge(*z_f(it, t - ZB))
            else:
                eng.wait_ge(*u_f(it, t - UA))

        spare = [b for n, b in enumerate(ring) if n not in {JOB_BANK[JOB_AT["xf", m]] for m in range(8)}]
        assert len(spare) == 3

        block = ctx.enter_context(nc.Block())

        @block.sync
        def _(sp):
            for ev in (xres_in, w_in0, w_in1, y_out):
                sp.nop().then_inc(ev.sem, ev.per * ev.step)
            for dst, src in ((ident, a["ident"]), (upper, a["upper"]), (dmask, a["dmask"]), (lmask, a["lmask"])):
                sp.dma_start(dst[:], src).then_inc(s_const, 16)
            for dst, src in ((cin, a["c_all"]), (bada, a["b_ada"]), (vec[:, PREW:PREW + 8], a["pre_w"])):
                sp.dma_start(dst[:], src).then_inc(s_prm, 16)
            sp.dma_start(wada[0][:], a["w_ada"][0]).then_inc(ada_in[0], 16)
            for i in range(4):
                sp.dma_start(xb[:, i], a["x"][0][:, i]).then_inc(x_in.sem, 16)
            sp.dma_start(xrow, a["xs"]).then_inc(sm_x0, 16)
            for j in range(1, 4):
                sp.dma_start(wada[j][:], a["w_ada"][j]).then_inc(ada_in[j], 16)
            for dst, src in ((vec[:, PSC:PSC + 4], a["pool_scale"]), (vec[:, ONW:ONW + 1], a["o_norm"]),
                             (vec[:, NEA:NEA + 4], a["a_log"].to_broadcast([P, H])),
                             (vec[:, DTB:DTB + 4], a["dt_bias"].to_broadcast([P, H])),
                             (cw, a["conv_w"]), (poolw, a["pool_w"]), (wgr, a["w_gate"]), (ftab, a["ftab"]),
                             (pwr, a["post_w"]), (grow, a["b_gate"])):
                sp.dma_start(dst[:], src).then_inc(s_prm2, 16)
            for j in range(4, 6):
                sp.dma_start(wada[j][:], a["w_ada"][j]).then_inc(ada_in[j], 16)
            for t in range(2):
                sp.dma_start(wraw[:, t], a["w"][t]).then_inc(w_in[t].sem, 16)
            for t in range(2):
                sp.wait_ge(*w_lo(0, t))
                sp.wait_ge(*done("pe", f"sp{t}"))
                sp.dma_start(wraw[:, t], a["w"][t + 2]).then_inc(w_in[t].sem, 16)

            def block_of(it, last=False):
                sp.wait_ge(*job["xf"](it, -1))
                if last:
                    sp.wait_ge(*h_lo(it, -1))
                    for dst, src in ((cbuf, a["s_conv"]), (pbuf, a["s_pool"])):
                        sp.dma_start(dst[:], src).then_inc(sm_st, 16)
                    sp.dma_start(ssm[:], a["s_ssm"]).then_inc(sm_ssm, 16)
                for t in range(2, NW - 2 if last else NW + 2):
                    sp.wait_ge(*w_lo(it + t // NW, t % NW))
                    if last:
                        sp.wait_ge(*done("pe", f"sp{t}"))
                    sp.dma_start(wraw[:, t % 2], a["w"][(t + 2) % NW]).then_inc(w_in[t % 2].sem, 16)
                    if 4 <= t < 8 and not last:
                        sp.dma_start(xb[:, t - 4], a["x"][it + 1][:, t - 4]).then_inc(x_in.sem, 16)
                    if t == OUT + 1:
                        sp.wait_ge(*job["su"](it, NC - 1))
                        sp.wait_ge(*job["mv"](it, NC - 1))
                        sp.wait_ge(*job["ot"](it, NC - 1))
                    if OUT < t <= OUT + 4:
                        sp.dma_start(xres[:, t - OUT - 1], a["x"][it][:, t - OUT - 1]).then_inc(xres_in.sem, 16)
                if last:
                    sp.wait_ge(*proj(LAST, OUT - 1))
                    sp.dma_start(xs[:], a["xs"]).then_inc(sm_x, 16)
                    sp.dma_start(pw8[:], a["post_w"].to_broadcast([NS, DM])).then_inc(sm_x, 16)
                for t in range(4):
                    sp.wait_ge(*yr_f(it, t))
                    sp.dma_start(a["y"][it, t], ytok[:, t]).then_inc(y_out.sem, 16)

            with sp.Fori(0, NB - 1) as it:
                block_of(it)
            block_of(LAST, last=True)
            sp.wait_ge(s_end, 1)
            sp.dma_start(a["o_ssm"], st[:]).then_inc(out_sem, 16)
            sp.dma_start(a["o_conv"], hist[:]).then_inc(out_sem, 16)
            sp.dma_start(a["o_pool"], uhist[:]).then_inc(out_sem, 16)
            sp.wait_ge(sm_st, 32)
            sp.wait_ge(*done("dve", "pj23"))
            rows = lambda o: o.rearrange("j p t s -> p j t s")
            sp.dma_start(rows(a["o_sconv"])[:, 0:CK - 2], cbuf[:, 1:CK - 1]).then_inc(out_sem, 16)
            sp.dma_start(a["o_sconv"][CK - 2], pj[:, 0:NQ]).then_inc(out_sem, 16)
            sp.dma_start(rows(a["o_spool"])[:, 0:PB - 1], pbuf[:, 1:PB]).then_inc(out_sem, 16)
            sp.dma_start(a["o_spool"][PB - 1], pj[:, 20:24]).then_inc(out_sem, 16)
            for r in range(NS):
                sp.wait_ge(*done("dve", f"sn{r}"))
                sp.dma_start(a["o_sssm"][:, r], ssm[:, r]).then_inc(out_sem, 16)
            sp.wait_ge(*done("dve", "yr"))
            sp.dma_start(a["ys"], ys[:]).then_inc(out_sem, 16)
            sp.wait_ge(*y_out(LAST, 3))
            sp.wait_ge(out_sem, 16 * (8 + NS))

        def front_act(act, it):
            act.wait_ge(*x_in(it, 0))
            for t in range(4):
                if it is not PROLOGUE or t > 0:
                    act.wait_ge(*xsq(it, t - 1))
                if t == 0 and it is not PROLOGUE:
                    act.wait_ge(*rx_0(it, -1))
                    act.wait_ge(*o_sq4(it, 4 * (NC - 1) - 1))
                nc.scalar.activation(junk[:, :], xb[:, t, :], ACT.Square,
                                     accum_out=ssx[:, t:t + 1]).then_inc(xsq.sem, 1)

        def front_h(act, it, m):
            act.wait_ge(*job["xf"](it, m))
            if m >= 2 or it is not PROLOGUE:
                act.wait_ge(*h_lo(it, m - 2))
            nc.scalar.activation(htmp[:, m % 2], bank("xf", m)[:], ACT.Identity, bias=mod[:, m, 0:1],
                                 scale=amul[:, m, 0:1])
            if m == 0 and it is not PROLOGUE:
                act.wait_ge(*proj(it, OUT - 1))
            nc.scalar.activation(hhi[:, m], bank("xf", m)[:], ACT.Identity, bias=mod[:, m, 0:1],
                                 scale=amul[:, m, 0:1]).then_inc(h_hi.sem, 1)

        @block.scalar
        def _(act):
            for ev in (w_hi, raw_f, silu, sq, g_ab, g_e, g_l, g_t, g_eg, g_ekg, tanh_f, u_f, kt_f, d_e, x_0,
                       u_c, o_sq4, yhi_f, ysq):
                act.nop().then_inc(ev.sem, ev.per)
            act.wait_ge(s_prm, 48)
            nc.scalar.activation(cin[:], cin[:], ACT.Silu).then_inc(s_cact, 1)
            front_act(act, PROLOGUE)
            act.wait_ge(sm_x0, 16)
            act.wait_ge(*xsq(PROLOGUE, 3))
            nc.scalar.activation(junk[0:NS, :], xrow, ACT.Square, accum_out=s8[:, 0:1]).then_inc(*step("act", "x_sq"))
            act.wait_ge(s_prm2, 160)
            nc.scalar.activation(vec[:, NEA:NEA + 4], vec[:, NEA:NEA + 4], ACT.Exp).then_inc(s_cact, 1)
            act.wait_ge(s_pre, 5)
            for m in range(8):
                front_h(act, PROLOGUE, m)
            for t in range(2):
                act.wait_ge(*w_in[t](0, 0))
                nc.scalar.activation(whi[:, t], wraw[:, t], ACT.Copy).then_inc(w_hi.sem, 1)

            def split_hi(it, t):
                act.wait_ge(*w_in[(t + 1) % 2](it + (t + 1) // NW, (t + 1) % NW // 2))
                act.wait_ge(*proj(it, t - 1))
                nc.scalar.activation(whi[:, (t + 1) % 2], wraw[:, (t + 1) % 2], ACT.Copy).then_inc(w_hi.sem, 1)

            def tile(it, t):
                act.wait_ge(*proj(it, t))
                if t < NQ:
                    act.wait_ge(*conv(it, t - RAW))
                    act.wait_ge(*hist_out(it, t - RAW))
                    nc.scalar.activation(raw[:, t % RAW, CK - 1:], acc[t % 2][:], ACT.Copy).then_inc(raw_f.sem, 1)
                elif t < UA:
                    z = t - ZB
                    if z == 0:
                        act.wait_ge(*job["ss"](it, 7))
                        act.wait_ge(*job["ss"](it, 6))
                    act.wait_ge(*z_f(it, z - 2))
                    nc.scalar.activation(tmpa[:, t % 2], acc[t % 2][:], ACT.Tanh, scale=0.5).then_inc(tanh_f.sem, 1)
                elif t < OUT:
                    g = t - UA
                    act.wait_ge(*pooled_f(it, g - 2))
                    act.wait_ge(*u_out(it, g - 2))
                    nc.scalar.activation(ubuf[:, g % 2, PB:], acc[t % 2][:], ACT.Copy).then_inc(u_f.sem, 1)
            def split_cols(cols):
                nc.scalar.activation(yhi[:, 4:8, cols], y32[:, 4:8, cols], ACT.Copy).then_inc(yhi_f.sem, 1)

            def square_rows(it, hf, tiles):
                for t in tiles:
                    act.wait_ge(*(outp(it, 3 * hf + t) if t < 3 else proj(it, OUT + 4 * hf + 3)))
                    act.wait_ge(*ysq(it, 4 * hf + t - 1))
                    if hf == 0 and t == 0:
                        act.wait_ge(*o_sq4(it, 4 * NC - 1))
                        act.wait_ge(*ry_0(it, -1))
                    nc.scalar.activation(junk[:, 0:BT], out_bank(hf, t)[:], ACT.Square, scale=DM ** -0.5,
                                         accum_out=ssy[:, t, hf:hf + 1]).then_inc(ysq.sem, 1)

            def silu_sq(it, t):
                act.wait_ge(*conv(it, t))
                if t == 0:
                    act.wait_ge(*proj(it, -1))
                nc.scalar.activation(cq[:, t], cacc[:, t % 2], ACT.Silu).then_inc(silu.sem, 1)
                if t < 8:
                    act.wait_ge(*silu(it, t))
                    if t < 2:
                        act.wait_ge(*z_f(it, -1 - t % 2))
                        act.wait_ge(*z_f(it, -1))
                    else:
                        act.wait_ge(*job["ss"](it, t - 2))
                    nc.scalar.activation(tmpa[:, t % 2], cq[:, t], ACT.Square).then_inc(sq.sem, 1)

            def block_of(it, last=False):
                for t in range(NQ):
                    if t:
                        split_hi(it, t)
                    tile(it, t)
                    if t >= 2:
                        silu_sq(it, t - 2)
                    if t == GATES + 1:
                        act.wait_ge(*job["gt"](it, 0))
                        act.wait_ge(*g_b(it, -1))
                        nc.scalar.activation(btt[:], bank("gt")[:, 0:32].rearrange("p (c e) -> p c e", c=NC)[:, :, 0:4],
                                             ACT.Tanh, scale=0.5).then_inc(g_t.sem, 1)
                    if t == GATES + 2:
                        act.wait_ge(*g_y(it, 0))
                        nc.scalar.activation(gab[:], ga[:], ACT.Abs).then_inc(g_ab.sem, 1)
                        act.wait_ge(*g_ab(it, 0))
                        act.wait_ge(*g_sp(it, -1))
                        nc.scalar.activation(gl1[:], gab[:], ACT.Exp, scale=-1.0).then_inc(g_e.sem, 1)
                        act.wait_ge(*g_e(it, 0))
                        nc.scalar.activation(gl1[:], gl1[:], ACT.Ln, bias=1.0).then_inc(g_l.sem, 1)
                    if last and t == 8:
                        act.wait_ge(*done("pe", "sg0"))
                        nc.scalar.activation(g8[:, 0], bank("sg")[0:NS, 0:4], ACT.Tanh, scale=0.5).then_inc(*step("act", "g_tanh"))
                        act.wait_ge(*done("dve", "g_a"))
                        nc.scalar.activation(g8[:, 2], g8[:, 1], ACT.Abs).then_inc(*step("act", "g_abs"))
                        act.wait_ge(*done("act", "g_abs"))
                        nc.scalar.activation(g8[:, 2], g8[:, 2], ACT.Exp, scale=-1.0).then_inc(*step("act", "g_exp"))
                        act.wait_ge(*done("act", "g_exp"))
                        nc.scalar.activation(g8[:, 2], g8[:, 2], ACT.Ln, bias=1.0).then_inc(*step("act", "g_ln"))
                    if last and t == 10:
                        act.wait_ge(*done("dve", "g_g"))
                        nc.scalar.activation(g8[:, 5], g8[:, 4], ACT.Exp).then_inc(*step("act", "g_eg"))
                silu_sq(it, NQ - 2)
                silu_sq(it, NQ - 1)
                act.wait_ge(*gc_f(it, 0))
                act.wait_ge(*yb_f(it, -1))
                nc.scalar.activation(eg[:], gcs[:], ACT.Exp).then_inc(g_eg.sem, 1)
                act.wait_ge(*g_d(it, 0))
                nc.scalar.activation(ekg[:], gd[:], ACT.Exp).then_inc(g_ekg.sem, 1)
                for slot, (c, p, sc, q, parts) in enumerate(PLAN):
                    norm, step_ = norm_step(slot)
                    for n in parts:
                        if n <= PARTS and n % 8 == 0:
                            split_hi(it, NQ + n // 8)
                        if n < PARTS and n % 8 == 7:
                            tile(it, NQ + n // 8)
                    if c is not None and p == 0:
                        act.wait_ge(*job["kt"](it, c))
                        act.wait_ge(*job["su"](it, c - 2)) if c >= 2 else act.wait_ge(*yr_f(it, -1))
                        nc.scalar.activation(ktok[:, c % 2], heads(bank("kt", c)), ACT.Copy).then_inc(kt_f.sem, 1)
                        act.wait_ge(*d_2(it, c))
                        nc.scalar.activation(dcy[:], dcy[:], ACT.Exp).then_inc(d_e.sem, 1)
                    elif c is not None and p == 2:
                        act.wait_ge(*job["xt"](it, c))
                        act.wait_ge(*job["w"](it, c * NL - 1))
                        nc.scalar.activation(xv[:], heads(bank("xt", c)), ACT.Copy).then_inc(x_0.sem, 1)
                    if q == 1 and sc is not None:
                        act.wait_ge(*job["u"](it, sc))
                        act.wait_ge(*ve_f(it, sc - 1))
                        act.wait_ge(*job["mv"](it, sc - 1)) if sc else act.wait_ge(*yr_f(it, -1))
                        nc.scalar.activation(ub[:], heads(bank("u", sc)), ACT.Copy).then_inc(u_c.sem, 1)
                    if q == 2 and sc is not None:
                        act.wait_ge(*o_f(it, sc))
                        act.wait_ge(*o_n(it, sc - 1))
                        for h in range(H):
                            act.wait_ge(*o_sq4(it, 4 * sc + h - 1))
                            if h == 0 and sc == 0:
                                act.wait_ge(*ysq(it, -1))
                            if h == 0 and sc == NC - 1 and not last:
                                act.wait_ge(*xsq(it, 3))
                            nc.scalar.activation(junk[:, 0:C], ao[:, h], ACT.Square,
                                                 accum_out=oss[:, h:h + 1]).then_inc(o_sq4.sem, 1)
                    if slot == FRONT and not last:
                        front_act(act, it)
                    if split_step(slot) is not None:
                        ch = split_step(slot)
                        act.wait_ge(*yb_f(it, ch))
                        split_cols(slice(ch * C, (ch + 1) * C))
                    if sc == NC - 1 and q == 0:
                        for m in range(4):
                            act.wait_ge(*job["ks"](it, NC - 1))
                            act.wait_ge(*ya_f(it, NG - 1))
                            nc.scalar.activation(yhi[:, m], y32[:, m], ACT.Copy).then_inc(yhi_f.sem, 1)
                    if last and slot == SAMPLE_SLOT["conv"]:
                        act.wait_ge(*done("dve", "cv6"))
                        nc.scalar.activation(cs[:], ct[:], ACT.Silu).then_inc(*step("act", "silu"))
                    if last and slot == SAMPLE_SLOT["gate"]:
                        act.wait_ge(*done("dve", "pj19"))
                        nc.scalar.activation(zs[:], pj[:, 12:20], ACT.Tanh, scale=0.5).then_inc(*step("act", "z_tanh"))
                split_hi(it, OUT + 1)
                act.wait_ge(*yb_f(it, NC - 1))
                split_cols(slice(BT - C, BT))
                for m in range(8):
                    if not last:
                        front_h(act, it, m)
                    if m >= 2 and not (last and m == 7):
                        split_hi(it, OUT + m)
                    if m == 3:
                        square_rows(it, 0, range(4))
                square_rows(it, 1, range(3))
                if not last:
                    split_hi(it, NW)
                square_rows(it, 1, range(3, 4))

            with act.Fori(0, NB - 1) as it:
                block_of(it)
            block_of(LAST, last=True)
            act.wait_ge(*done("dve", "ys1"))
            act.wait_ge(*ysq(LAST, 7))
            nc.scalar.activation(junk[0:NS, :], ys[:], ACT.Square, accum_out=s8[:, 4:5]).then_inc(*step("act", "y_sq"))

        def front_xn(dve, it):
            dve.wait_ge(*rx_f(it, 0))
            for t in range(4):
                nc.vector.tensor_scalar(xb[:, t], xb[:, t], rx[:, t:t + 1], None, ALU.mult).then_inc(xn.sem, 1)

        def front_lo(dve, it, m):
            dve.wait_ge(*h_hi(it, m))
            nc.vector.tensor_tensor(hlo[:, m], htmp[:, m % 2], hhi[:, m].bitcast(F32), ALU.subtract).then_inc(h_lo.sem, 1)

        @block.vector
        def _(dve):
            for ev in (hist_in, hist_out, conv_a, conv, ss_ev, g_c, g_y, g_sp, g_g, g_b, gc_f, g_d, k_1, k_2, b_f, bke_f, z_f, pooled_f, ya_f,
                       rv_f, d_1, d_2, d_b, lt_f, mt_f, y_0, y_1, y_l, x_l, w_f, ks_t, r_f, ao_f, ve_f, s_f, o_f, o_n, o_s, yb_f,
                       ylo_f, ytok_f, ry_0, yr_f):
                dve.nop().then_inc(ev.sem, ev.per)
            nc.vector.memset(st[:], 0.0)
            nc.vector.memset(ones[:], 1.0)
            nc.vector.memset(hist[:], 0.0)
            nc.vector.memset(uhist[:], 0.0).then_inc(s_pre, 1)
            for j in range(4):
                dve.wait_ge(s_mod, j + 1)
                nc.vector.tensor_copy(rows9[j], acc[j % 2][0:1 + NS, :]).then_inc(s_rows, 1)
                if j == 1:
                    front_xn(dve, PROLOGUE)
                    dve.wait_ge(*done("pool", "rx"))
                    nc.vector.tensor_scalar(xrow, xrow, s8[:, 2:3], None, ALU.mult).then_inc(*step("dve", "xn"))
            dve.wait_ge(s_tr, 1)
            dve.wait_ge(s_prm, 48)
            nc.vector.tensor_tensor(mod[:, 0:16], spare[0][:, 0:144].rearrange("p (m s) -> p m s", m=16),
                                    bada[:, 0:16].unsqueeze(2).to_broadcast([P, 16, 1 + NS]), ALU.add).then_inc(s_pre, 1)
            dve.wait_ge(s_pre, 2)
            nc.vector.tensor_scalar(amul[:], mod[:, 8:16], 1.0, None, ALU.add).then_inc(s_pre, 1)
            dve.wait_ge(s_pre, 3)
            nc.vector.tensor_tensor(amul[:], amul[:], vec[:, PREW:PREW + 8].unsqueeze(2).to_broadcast([P, 8, 1 + NS]),
                                    ALU.mult).then_inc(s_pre, 1)
            dve.wait_ge(s_cact, 2)
            dve.wait_ge(s_prm2, 160)
            nc.vector.tensor_scalar(vec[:, NEA:NEA + 4], vec[:, NEA:NEA + 4], -1.0, None, ALU.mult)
            nc.vector.tensor_scalar(vec[:, PSC:PSC + 5], vec[:, PSC:PSC + 5], 0.5, None, ALU.mult)
            nc.vector.tensor_copy(wgh[:], wgr[:]).then_inc(s_pre, 1)
            dve.wait_ge(s_pre, 5)
            nc.vector.tensor_tensor(wgl[:], wgr[:], wgh[:].bitcast(F32), ALU.subtract).then_inc(s_pre, 1)
            for m in range(8):
                front_lo(dve, PROLOGUE, m)
                if m in (4, 7):
                    j = 4 if m == 4 else 5
                    dve.wait_ge(s_mod, j + 1)
                    nc.vector.tensor_copy(rows9[j], acc[j % 2][0:1 + NS, :]).then_inc(s_rows, 1)
            dve.wait_ge(*done("pe", "hs"))
            nc.vector.tensor_tensor(hs[:], spare[2][:, 0:64].rearrange("p (k s) -> p k s", k=KT), amul[:, :, 1:1 + NS],
                                    ALU.mult).then_inc(*step("dve", "h0"))
            dve.wait_ge(*done("dve", "h0"))
            nc.vector.tensor_tensor(hs[:], hs[:], mod[:, 0:8, 1:1 + NS], ALU.add).then_inc(*step("dve", "h"))
            for m in range(2):
                cols = slice(m * BT, (m + 1) * BT)
                dve.wait_ge(s_rows, 5 + m)
                nc.vector.tensor_tensor(grow[:, cols], grow[:, cols], rows9[4 + m][0:1], ALU.add).then_inc(s_trc, 1)
                dve.wait_ge(s_trc, 2 * m + 1)
                nc.vector.tensor_tensor(grow[:, cols], grow[:, cols], pwr[:, cols], ALU.mult).then_inc(s_trc, 1)
            dve.wait_ge(s_tr, 2)
            nc.vector.tensor_tensor(mod[:, 16:24], spare[1][:, 0:72].rearrange("p (m s) -> p m s", m=8),
                                    bada[:, 16:24].unsqueeze(2).to_broadcast([P, 8, 1 + NS]), ALU.add)
            for m in range(2):
                dve.wait_ge(s_row, m + 1)
                nc.vector.tensor_copy(gpw[:, m * 512:(m + 1) * 512], (spare[2], spare[0])[m][:]).then_inc(s_rowc, 1)
            dve.wait_ge(*done("pe", "sp1"))
            nc.vector.tensor_copy(pj01[:].rearrange("p t s -> p (t s)"), acc[0][:, 0:2 * NS]).then_inc(*step("dve", "pj01"))

            def convolve(it, t):
                r = raw[:, t % RAW]
                dve.wait_ge(*hist_out(it, t - RAW))
                nc.vector.tensor_copy(r[:, 0:CK - 1], hist[:, t]).then_inc(hist_in.sem, 1)
                dve.wait_ge(*raw_f(it, t))
                dve.wait_ge(*hist_in(it, t))
                dve.wait_ge(*silu(it, t - 2))
                nc.vector.tensor_scalar(cacc[:, t % 2], r[:, 0:BT], cw[:, t, 0:1], None, ALU.mult).then_inc(conv_a.sem, 1)
                for j in range(1, CK):
                    dve.wait_ge(*conv_a(it, 3 * t + j - 1))
                    nc.vector.scalar_tensor_tensor(out=cacc[:, t % 2], in0=r[:, j:j + BT], scalar=cw[:, t, j:j + 1],
                                                   in1=cacc[:, t % 2], op0=ALU.mult, op1=ALU.add
                                                   ).then_inc((conv_a if j < CK - 1 else conv).sem, 1)
                nc.vector.tensor_copy(hist[:, t], r[:, BT:BT + CK - 1]).then_inc(hist_out.sem, 1)

            def stat(it, t):
                dve.wait_ge(*job["ss"](it, t))
                if t == 0:
                    dve.wait_ge(*k_1(it, -1))
                    dve.wait_ge(*odb_0(it, -1))
                nc.vector.tensor_copy(ssb[:, t], bank("ss", t)[:, 0:NC]).then_inc(ss_ev.sem, 1)

            def split_y(it, m):
                dve.wait_ge(*yhi_f(it, NC - 1 + m))
                nc.vector.tensor_tensor(ylo[:, m], y32[:, m], yhi[:, m].bitcast(F32), ALU.subtract).then_inc(ylo_f.sem, 1)

            def split_cols(cols):
                nc.vector.tensor_tensor(ylo[:, 4:8, cols], y32[:, 4:8, cols], yhi[:, 4:8, cols].bitcast(F32), ALU.subtract
                                        ).then_inc(ylo_f.sem, 1)

            def weigh_rows(it, hf):
                cols = slice(hf * BT, (hf + 1) * BT)
                for t in range(4):
                    dve.wait_ge(*ysq(it, 4 * hf + t))
                    if hf == 0 and t == 0:
                        dve.wait_ge(*ylo_f(it, 5))
                        dve.wait_ge(*yhi_f(it, 7))
                    nc.vector.tensor_tensor(ytok[:, t, cols], out_bank(hf, t)[:], gpw[:, cols], ALU.mult).then_inc(ytok_f.sem, 1)

            def zmul(it, t):
                z = t - ZB
                yk = y32[:, (z + 4) % 8]
                dve.wait_ge(*tanh_f(it, z))
                if z == 0:
                    dve.wait_ge(*y_out(it, -1))
                nc.vector.scalar_tensor_tensor(out=yk, in0=tmpa[:, t % 2], scalar=1.0, in1=acc[t % 2][:],
                                               op0=ALU.add, op1=ALU.mult).then_inc(z_f.sem, 1)

            def sample_tile(it, t):
                if t == 1:
                    dve.wait_ge(*h_lo(it, -1))
                    dve.wait_ge(*done("dve", "pj01"))
                    nc.vector.tensor_copy(pj[:, 0:2], pj01[:]).then_inc(*step("dve", "pj1"))
                if t < 2:
                    return
                dve.wait_ge(*done("pe", f"sp{t}"))
                nc.vector.tensor_copy(pj[:, t], bank("sp", t)[:, 0:NS]).then_inc(*step("dve", f"pj{t}"))

            def sample_half(it, hf):
                dve.wait_ge(*done("pe", f"sp{OUT + 4 * hf + 3}"))
                nc.vector.tensor_copy(ys[:, hf * BT:(hf + 1) * BT], bank("so", hf)[0:NS, :]).then_inc(*step("dve", f"ys{hf}"))

            def sample_slot(it, slot):
                def s(name):
                    return step("dve", name)

                def after(name, who="dve"):
                    dve.wait_ge(*done(who, name))

                if slot == SAMPLE_SLOT["conv"]:
                    def taps(j):
                        return cw[:, :, j:j + 1].to_broadcast([P, NQ, NS])

                    dve.wait_ge(*silu(it, NQ - 1))
                    dve.wait_ge(sm_st, 32)
                    nc.vector.tensor_tensor(ct[:], pj[:, 0:NQ], taps(CK - 1), ALU.mult).then_inc(*s("cv0"))
                    for j in range(CK - 1):
                        after(f"cv{2 * j}")
                        nc.vector.tensor_tensor(sqs[:], cbuf[:, j], taps(j), ALU.mult).then_inc(*s(f"cv{2 * j + 1}"))
                        after(f"cv{2 * j + 1}")
                        nc.vector.tensor_tensor(ct[:], ct[:], sqs[:], ALU.add).then_inc(*s(f"cv{2 * j + 2}"))
                if slot == SAMPLE_SLOT["square"]:
                    after("silu", "act")
                    nc.vector.tensor_tensor(sqs[:, 0:8], cs[:, 0:8], cs[:, 0:8], ALU.mult).then_inc(*s("sq0"))
                    nc.vector.tensor_tensor(sqs[:, 8:12], cs[:, 0:4], cs[:, 4:8], ALU.mult).then_inc(*s("sq1"))
                    for e in range(2):
                        nc.vector.tensor_copy(kq[:, :, :, e].rearrange("p s h -> p h s"), cs[:, 4 * e:4 * e + 4]
                                              ).then_inc(*s(f"kq{e}"))
                if slot == SAMPLE_SLOT["root"]:
                    after("s20", "pe")
                    nc.vector.tensor_scalar(sst[:, 0:8], bank("s2")[:, 0:64].rearrange("p (t s) -> p t s", t=8), EPS, None,
                                            ALU.add).then_inc(*s("sst0"))
                    nc.vector.tensor_copy(sst[:, 8:12].rearrange("p t s -> p (t s)"), bank("s2")[:, 64:96]).then_inc(*s("sst1"))
                    after("kv0", "pe")
                    t0, t1 = (bank("kv")[:, 0:64].rearrange("p (s h e) -> p e h s", s=NS, h=H)[:, e] for e in range(2))
                    eg_ = gvb[:, :, 1].rearrange("p s h -> p h s")
                    nc.vector.tensor_tensor(dl[:, 0], t0, eg_, ALU.mult).then_inc(*s("d0"))
                    nc.vector.tensor_tensor(dl[:, 1], t1, eg_, ALU.mult).then_inc(*s("d1"))
                if slot == SAMPLE_SLOT["delta"]:
                    after("rk", "pool")
                    be = gvb[:, :, 0].rearrange("p s h -> p h s")
                    dps = dl[:, 2].rearrange("p h s -> p (h s)").rearrange("p (s h) -> p h s", h=H)
                    after("d0")
                    nc.vector.tensor_tensor(dl[:, 0], dl[:, 0], rk[:, 1], ALU.mult).then_inc(*s("d2"))
                    after("d2")
                    nc.vector.tensor_tensor(dl[:, 0], cs[:, 8:12], dl[:, 0], ALU.subtract).then_inc(*s("d3"))
                    after("d3")
                    nc.vector.tensor_tensor(dl[:, 0], dl[:, 0], be, ALU.mult).then_inc(*s("d4"))
                    after("d4")
                    nc.vector.tensor_tensor(dps, dl[:, 0], rk[:, 1], ALU.mult).then_inc(*s("d5"))
                    after("d5")
                    nc.vector.tensor_tensor(dl[:, 0], dps, sst[:, 8:12], ALU.mult).then_inc(*s("o0"))
                    after("o0")
                    nc.vector.tensor_tensor(dl[:, 1], dl[:, 1], dl[:, 0], ALU.add).then_inc(*s("o1"))
                    after("o1")
                    nc.vector.tensor_tensor(dl[:, 3], dl[:, 1], dl[:, 1], ALU.mult).then_inc(*s("o2"))
                if slot == SAMPLE_SLOT["mean"]:
                    after("dt0", "pe")
                    dve.wait_ge(*job["gt"](it, 0))
                    nc.vector.tensor_copy(drow[:].rearrange("p a c -> p (a c)"), bank("dt")[0:32, 0:256]).then_inc(*s("drow"))
                    after("son0", "pe")
                    nc.vector.tensor_scalar(rk[:, 0], bank("son")[:, 0:32].rearrange("p (h s) -> p h s", h=H), 1.0 / P, None,
                                            ALU.mult).then_inc(*s("ms0"))
                    nc.vector.tensor_scalar(dl[:, 0], sst[:, 4:8], EPS * P, None, ALU.mult).then_inc(*s("ms1"))
                    after("ms1")
                    nc.vector.tensor_tensor(rk[:, 0], rk[:, 0], dl[:, 0], ALU.add).then_inc(*s("ms2"))
                if slot == SAMPLE_SLOT["gate"]:
                    after("z_tanh", "act")
                    nc.vector.scalar_tensor_tensor(out=zs[:], in0=zs[:], scalar=1.0, in1=pj[:, 12:20], op0=ALU.add,
                                                   op1=ALU.mult).then_inc(*s("zs"))
                    after("rstd", "pool")
                    nc.vector.tensor_tensor(dl[:, 1], dl[:, 1], rk[:, 1], ALU.mult).then_inc(*s("on"))
                    after("on")
                    nc.vector.scalar_tensor_tensor(out=ym[:, 4:8], in0=dl[:, 1], scalar=vec[:, ONW:ONW + 1], in1=zs[:, 0:4],
                                                   op0=ALU.mult, op1=ALU.mult).then_inc(*s("ymb"))
                if slot == SAMPLE_SLOT["pool"]:
                    for g in range(NG):
                        w = 2 << g
                        nc.vector.tensor_reduce(pls[:, g], pbuf[:, PB - (w - 1):PB, g].rearrange("p j s -> p s j"), AX.X,
                                                ALU.add).then_inc(*s(f"pl{g}"))
                    after("pl3")
                    nc.vector.tensor_tensor(pls[:], pls[:], pj[:, 20:24], ALU.add).then_inc(*s("pl4"))
                    after("pl4")
                    for g in range(NG):
                        nc.vector.scalar_tensor_tensor(out=pls[:, g], in0=pls[:, g], scalar=1.0 / (2 << g), in1=pj[:, 20 + g],
                                                       op0=ALU.mult, op1=ALU.subtract).then_inc(*s(f"pl{5 + g}"))
                if slot == SAMPLE_SLOT["mixed"]:
                    after("spl0", "pe")
                    after("zs")
                    for g in range(NG):
                        nc.vector.scalar_tensor_tensor(out=ym[:, g], in0=bank("spl")[:, g * NS:(g + 1) * NS],
                                                       scalar=vec[:, PSC + g:PSC + g + 1], in1=zs[:, 4 + g], op0=ALU.mult,
                                                       op1=ALU.mult).then_inc(*s("yma" if g == 3 else f"ym{g}"))

            def sample_out(it, m):
                def s(name):
                    return step("dve", name)

                if m == 0:
                    dve.wait_ge(*proj(it, OUT - 1))
                    dve.wait_ge(*done("dve", "drow"))
                    nc.vector.tensor_tensor(krow[:], drow[:, 0].unsqueeze(1).to_broadcast([32, 32, P]),
                                            ident[0:32, 0:32].unsqueeze(2).to_broadcast([32, 32, P]), ALU.mult).then_inc(*s("krow"))
                if m == 4:
                    sample_half(it, 0)
                if m >= 1:
                    r = m - 1
                    nc.vector.tensor_tensor(ssm[:, r], ssm[:, r], gvb[:, r, 1].unsqueeze(2).to_broadcast([P, H, P]),
                                            ALU.mult).then_inc(*s(f"se{r}"))
                    dve.wait_ge(*done("pe", f"sop{r}"))
                    dve.wait_ge(*done("dve", f"se{r}"))
                    nc.vector.tensor_tensor(ssm[:, r], ssm[:, r], heads(bank("sop", r)), ALU.add).then_inc(*s(f"sn{r}"))
                if m == 8:
                    dve.wait_ge(sm_x, 32)
                    for e in range(2):
                        dve.wait_ge(*done("pe", f"sgt{e}"))
                        nc.vector.tensor_tensor(gr8[:, e * 512:(e + 1) * 512], bank("sgt", e)[0:NS, :],
                                                pw8[:, e * 512:(e + 1) * 512], ALU.mult).then_inc(*s(f"gr{e}"))

            def block_of(it, last=False):
                for t in range(NQ):
                    convolve(it, t)
                    if t == GATES:
                        dve.wait_ge(*job["gates"](it, 0))
                        dve.wait_ge(*job["gt"](it, -1))
                        nc.vector.tensor_copy(gsb[:], bank("gates")[0:8, :]).then_inc(g_c.sem, 1)
                    if t == GATES + 1:
                        dve.wait_ge(*job["gt"](it, 0))
                        dve.wait_ge(*g_t(it, 0))
                        dve.wait_ge(*g_sp(it, -1))
                        nc.vector.tensor_tensor(ga[:], bank("gt")[:, 0:32].rearrange("p (c e) -> p c e", c=NC)[:, :, 4:8],
                                                vec[:, DTB:DTB + 4].unsqueeze(1).to_broadcast([P, NC, H]), ALU.add
                                                ).then_inc(g_y.sem, 1)
                        dve.wait_ge(*g_t(it, 0))
                        dve.wait_ge(*b_f(it, -1))
                        nc.vector.tensor_scalar(beta[:], btt[:], 0.5, 0.5, ALU.mult, ALU.add).then_inc(g_b.sem, 1)
                    if t == GATES + 3:
                        dve.wait_ge(*g_l(it, 0))
                        dve.wait_ge(*g_y(it, 0))
                        nc.vector.scalar_tensor_tensor(out=gsp[:], in0=ga[:], scalar=0.0, in1=gl1[:], op0=ALU.max,
                                                       op1=ALU.add).then_inc(g_sp.sem, 1)
                        dve.wait_ge(*g_sp(it, 0))
                        dve.wait_ge(*job["gc"](it, -1))
                        dve.wait_ge(*gb_in(it, -1))
                        nc.vector.tensor_tensor(gg[:], gsp[:], vec[:, NEA:NEA + 4].unsqueeze(1).to_broadcast([P, NC, H]),
                                                ALU.mult).then_inc(g_g.sem, 1)
                    if t == GATES + 5:
                        dve.wait_ge(*job["gc"](it, 0))
                        dve.wait_ge(*g_eg(it, -1))
                        dve.wait_ge(*d_1(it, -1))
                        nc.vector.tensor_copy(gcs[:].rearrange("p a c h -> p (a c h)"), bank("gc")[:, 0:32]).then_inc(gc_f.sem, 1)
                        dve.wait_ge(*gc_f(it, 0))
                        dve.wait_ge(*g_ekg(it, -1))
                        nc.vector.tensor_tensor(gd[:], gcs[:, 1], gcs[:, 0], ALU.subtract).then_inc(g_d.sem, 1)
                    if SUMS <= t < SUMS + 8:
                        stat(it, t - SUMS)
                    if last:
                        sample_tile(it, t)
                        if t == 7:
                            dve.wait_ge(*done("act", "g_tanh"))
                            nc.vector.tensor_tensor(g8[:, 1], bank("sg")[0:NS, 4:8], vec[0:NS, DTB:DTB + 4], ALU.add
                                                    ).then_inc(*step("dve", "g_a"))
                        if t == 8:
                            dve.wait_ge(*done("act", "g_ln"))
                            nc.vector.tensor_scalar(g8[:, 6], g8[:, 0], 0.5, 0.5, ALU.mult, ALU.add).then_inc(*step("dve", "g_beta"))
                            nc.vector.scalar_tensor_tensor(out=g8[:, 3], in0=g8[:, 1], scalar=0.0, in1=g8[:, 2], op0=ALU.max,
                                                           op1=ALU.add).then_inc(*step("dve", "g_sp"))
                            dve.wait_ge(*done("dve", "g_sp"))
                            nc.vector.tensor_tensor(g8[:, 4], g8[:, 3], vec[0:NS, NEA:NEA + 4], ALU.mult
                                                    ).then_inc(*step("dve", "g_g"))
                        if t == 10:
                            dve.wait_ge(*done("act", "g_eg"))
                            for e, row in enumerate((6, 5)):
                                nc.vector.tensor_tensor(gdg[:, :, e * H:(e + 1) * H],
                                                        g8[:, row].unsqueeze(1).to_broadcast([NS, NS, H]),
                                                        ident[0:NS, 0:NS].unsqueeze(2).to_broadcast([NS, NS, H]), ALU.mult
                                                        ).then_inc(*step("dve", f"g_d{e}"))
                if last:
                    dve.wait_ge(*done("pe", "sb0"))
                    nc.vector.tensor_copy(gvb[:].rearrange("p s a h -> p (s a h)"), bank("sb")[:, 0:64]).then_inc(*step("dve", "gvb"))
                dve.wait_ge(*ss_ev(it, 7))
                nc.vector.tensor_scalar(kk1[:], ssb[:, 0:4].rearrange("p h c -> p c h"), EPS, None, ALU.add).then_inc(k_1.sem, 1)
                dve.wait_ge(*k_1(it, 0))
                nc.vector.reciprocal(kk2[:], kk1[:]).then_inc(k_2.sem, 1)
                dve.wait_ge(*k_2(it, 0))
                nc.vector.tensor_tensor(bb[:], beta[:], kk2[:], ALU.mult).then_inc(b_f.sem, 1)
                dve.wait_ge(*b_f(it, 0))
                dve.wait_ge(*g_ekg(it, 0))
                nc.vector.tensor_tensor(bke[:], bb[:], ekg[:], ALU.mult).then_inc(bke_f.sem, 1)

                for slot, (c, p, sc, q, parts) in enumerate(PLAN):
                    norm, step_ = norm_step(slot)
                    for n in parts:
                        t = NQ + n // 8
                        if n % 8 == 7 and t < UA:
                            zmul(it, t)
                        if last and n % 8 == 0 and t < OUT:
                            sample_tile(it, t)
                        if n % 8 == 7 and UA <= t - 1 < OUT:
                            g = t - 1 - UA
                            dve.wait_ge(*win_f(it, g))
                            dve.wait_ge(*job["pool"](it, g - 2))
                            nc.vector.scalar_tensor_tensor(out=pooled[:, g % 2], in0=win[:, g % 2, PB:],
                                                           scalar=1.0 / (2 << g), in1=ubuf[:, g % 2, PB:],
                                                           op0=ALU.mult, op1=ALU.subtract).then_inc(pooled_f.sem, 1)
                        g = pool_after(n)
                        if g is not None:
                            dve.wait_ge(*job["pool"](it, g))
                            dve.wait_ge(*z_f(it, 4 + g))
                            nc.vector.scalar_tensor_tensor(out=y32[:, g], in0=bank("pool", g)[:], scalar=vec[:, PSC + g:PSC + g + 1],
                                                           in1=y32[:, g], op0=ALU.mult, op1=ALU.mult).then_inc(ya_f.sem, 1)
                    if c is not None and p == 0:
                        dve.wait_ge(*job["vt"](it, c))
                        dve.wait_ge(*sk_f(it, 0))
                        dve.wait_ge(*job["u"](it, c - 2)) if c >= 2 else dve.wait_ge(*yr_f(it, -1))
                        nc.vector.tensor_tensor(rv[:, c % 2], heads(bank("vt", c)), bc(sk[:, c]), ALU.mult).then_inc(rv_f.sem, 1)
                        dve.wait_ge(*job["gb"](it, c))
                        dve.wait_ge(*mt_f(it, c - 1))
                        nc.vector.tensor_tensor(dcy[:], heads(bank("gb", c)), bc(gcs[:, 0, c]), ALU.subtract).then_inc(d_1.sem, 1)
                        dve.wait_ge(*d_1(it, c))
                        nc.vector.tensor_tensor(dcy[:], dcy[:], mbc(dmask[:]), ALU.min).then_inc(d_2.sem, 1)
                        dve.wait_ge(*d_e(it, c))
                        nc.vector.tensor_tensor(dcy[:], dcy[:], bc(bb[:, c]), ALU.mult).then_inc(d_b.sem, 1)
                    elif c is not None and p == 1:
                        dve.wait_ge(*d_b(it, c))
                        dve.wait_ge(*job["kk"](it, c))
                        dve.wait_ge(*job["w"](it, c * NL - 1))
                        nc.vector.tensor_tensor(lt[:], heads(bank("kk", c)), dcy[:], ALU.mult).then_inc(lt_f.sem, 1)
                        dve.wait_ge(*job["qk"](it, c))
                        if c >= 2:
                            dve.wait_ge(*job["mv"](it, c - 2))
                        elif c == 0:
                            dve.wait_ge(*proj(it, -1))
                        nc.vector.tensor_tensor(mtb[:, c % 2], heads(bank("qk", c)), dcy[:], ALU.mult).then_inc(mt_f.sem, 1)
                        dve.wait_ge(*lt_f(it, c))
                        if c >= 2:
                            dve.wait_ge(*job["u"](it, c - 2))
                        nc.vector.tensor_tensor(yv[:, c % 2], lt[:], mbc(lmask[:, 0]), ALU.mult).then_inc(y_0.sem, 1)
                        dve.wait_ge(*y_0(it, c))
                        nc.vector.tensor_tensor(yv[:, c % 2], mbc(ident[:]), yv[:, c % 2], ALU.subtract).then_inc(y_1.sem, 1)
                    elif c is not None and p >= 3 and p % 2:
                        lv = (p - 3) // 2
                        i = c * NL + lv
                        dve.wait_ge(*job["w"](it, i))
                        dve.wait_ge(*job["yy"](it, i - 1))
                        sz = LEVELS[lv]
                        if sz == C // 2:
                            nc.vector.tensor_copy(wb[sz:, :, 0:sz], packed(bank("w", i), sz)[sz:]).then_inc(w_f.sem, 1)
                        else:
                            nc.vector.tensor_tensor(
                                wb[:].rearrange("p h (b two s) -> p (h b) two s", two=2, s=sz),
                                packed(bank("w", i), sz).unsqueeze(2).to_broadcast([P, H * C // (2 * sz), 2, sz]),
                                level_mask(lv), ALU.mult).then_inc(w_f.sem, 1)
                    elif c is not None and p >= 4:
                        lv = (p - 4) // 2
                        sz = LEVELS[lv]
                        if lv < NL - 1:
                            i = c * (NL - 1) + lv
                            dve.wait_ge(*job["xx"](it, i))
                            if lv == 0:
                                dve.wait_ge(*x_0(it, c))
                            else:
                                dve.wait_ge(*x_l(it, i - 1))
                            xe = half_blocks(xv[:], sz, 0)
                            nc.vector.tensor_tensor(xe, xe, packed(bank("xx", i), sz), ALU.subtract).then_inc(x_l.sem, 1)
                        i = c * NL + lv
                        dve.wait_ge(*job["yy"](it, i))
                        if lv == 0:
                            dve.wait_ge(*y_1(it, c))
                        else:
                            dve.wait_ge(*y_l(it, i - 1))
                        rows = slice(0, sz if lv == NL - 1 else P)
                        yo = half_blocks(yv[:, c % 2], sz, 1)[rows]
                        nc.vector.tensor_tensor(yo, yo, packed(bank("yy", i), sz)[rows], ALU.subtract).then_inc(y_l.sem, 1)
                    if sc is not None and q == 0:
                        dve.wait_ge(*job["ks"](it, sc))
                        dve.wait_ge(*g_eg(it, 0))
                        dve.wait_ge(*r_f(it, sc - 1))
                        if sc == 0:
                            dve.wait_ge(*yr_f(it, -1))
                        nc.vector.tensor_tensor(tks[:], heads(bank("ks", sc)), bc(eg[:, 0, sc]), ALU.mult).then_inc(ks_t.sem, 1)
                        dve.wait_ge(*ks_t(it, sc))
                        dve.wait_ge(*rv_f(it, sc))
                        nc.vector.tensor_tensor(rv[:, sc % 2], rv[:, sc % 2], tks[:], ALU.subtract).then_inc(r_f.sem, 1)
                        dve.wait_ge(*job["qs"](it, sc))
                        dve.wait_ge(*job["ot"](it, sc - 1))
                        nc.vector.tensor_tensor(ao[:], heads(bank("qs", sc)), bc(eg[:, 0, sc]), ALU.mult).then_inc(ao_f.sem, 1)
                    if sc is not None and q == 1:
                        dve.wait_ge(*u_c(it, sc))
                        dve.wait_ge(*job["su"](it, sc - 1))
                        dve.wait_ge(*bke_f(it, 0))
                        if sc == 0:
                            dve.wait_ge(*yr_f(it, -1))
                        nc.vector.tensor_tensor(ve[:], ub[:], bc(bke[:, sc]), ALU.mult).then_inc(ve_f.sem, 1)
                    if sc is not None and q == 2:
                        if sc == NC - 1:
                            for m in range(2):
                                split_y(it, m)
                        dve.wait_ge(*job["mv"](it, sc))
                        dve.wait_ge(*ao_f(it, sc))
                        nc.vector.tensor_tensor(ao[:], ao[:], heads(bank("mv", sc)), ALU.add).then_inc(o_f.sem, 1)
                        dve.wait_ge(*job["su"](it, sc))
                        dve.wait_ge(*sdec_f(it, sc))
                        nc.vector.tensor_tensor(st[:], sdec[:], heads(bank("su", sc)), ALU.add).then_inc(s_f.sem, 1)
                        if sc == NC - 1:
                            for m in range(2, 4):
                                split_y(it, m)
                    if norm is not None and step_ == 1:
                        dve.wait_ge(*o_sq4(it, 4 * norm + 3))
                        dve.wait_ge(*odb_0(it, 0))
                        dve.wait_ge(*o_rt(it, norm - 1))
                        nc.vector.scalar_tensor_tensor(out=on0[:], in0=oss[:], scalar=1.0 / P, in1=odb[:, norm], op0=ALU.mult,
                                                       op1=ALU.add).then_inc(o_n.sem, 1)
                        if norm == NC - 1:
                            dve.wait_ge(*yhi_f(it, NC - 2))
                            dve.wait_ge(*job["mv"](it, NC - 1))
                            split_cols(slice(0, BT - C))
                    if norm is not None and step_ == 2:
                        dve.wait_ge(*o_rt(it, norm))
                        dve.wait_ge(*o_f(it, norm))
                        nc.vector.tensor_tensor(ao[:], ao[:], bc(on[:]), ALU.mult).then_inc(o_s.sem, 1)
                    if sc is not None and q == 3:
                        dve.wait_ge(*job["ot"](it, sc))
                        dve.wait_ge(*z_f(it, 3))
                        yo = y32[:, 4:8, sc * C:(sc + 1) * C]
                        nc.vector.scalar_tensor_tensor(out=yo, in0=heads(bank("ot", sc)), scalar=vec[:, ONW:ONW + 1], in1=yo,
                                                       op0=ALU.mult, op1=ALU.mult).then_inc(yb_f.sem, 1)
                    if last:
                        sample_slot(it, slot)
                dve.wait_ge(*yhi_f(it, 7))
                split_cols(slice(BT - C, BT))
                if not last:
                    front_xn(dve, it)
                for m in range(8):
                    if last:
                        sample_out(it, m)
                    else:
                        front_lo(dve, it, m)
                    if m == 3:
                        weigh_rows(it, 0)
                if last:
                    sample_out(it, 8)
                weigh_rows(it, 1)
                dve.wait_ge(*ysq(it, 7))
                dve.wait_ge(*ry_f(it, -1))
                nc.vector.scalar_tensor_tensor(out=ry0[:], in0=ssy[:, :, 0], scalar=EPS, in1=ssy[:, :, 1], op0=ALU.add,
                                               op1=ALU.add).then_inc(ry_0.sem, 1)
                dve.wait_ge(*ry_f(it, 0))
                dve.wait_ge(*xres_in(it, 0))
                for t in range(4):
                    dve.wait_ge(*ytok_f(it, 4 + t))
                    nc.vector.scalar_tensor_tensor(out=ytok[:, t], in0=ytok[:, t], scalar=ry[:, t:t + 1], in1=xres[:, t],
                                                   op0=ALU.mult, op1=ALU.add).then_inc(yr_f.sem, 1)

            with dve.Fori(0, NB - 1) as it:
                block_of(it)
            block_of(LAST, last=True)
            dve.wait_ge(*s_f(LAST, NC - 1))
            dve.wait_ge(*hist_out(LAST, NQ - 1))
            dve.wait_ge(*u_out(LAST, NG - 1))
            dve.nop().then_inc(s_end, 1)
            sample_half(LAST, 1)
            dve.wait_ge(*done("pool", "ry"))
            nc.vector.scalar_tensor_tensor(out=ys[:], in0=ys[:], scalar=s8[:, 6:7], in1=gr8[:], op0=ALU.mult,
                                           op1=ALU.mult).then_inc(*step("dve", "yn"))
            dve.wait_ge(*done("dve", "yn"))
            nc.vector.tensor_tensor(ys[:], ys[:], xs[:], ALU.add).then_inc(*step("dve", "yr"))

        def held(pool):
            pool.nop().then_inc(pool_held, 1)

        def front_rx(pool, it):
            pool.wait_ge(*xsq(it, 3))
            if it is not PROLOGUE:
                pool.wait_ge(*xn(it, -1))
            held(pool)
            nc.gpsimd.tensor_scalar(rx0[:], ssx[:], 1.0 / DM, EPS, ALU.mult, ALU.add).then_inc(rx_0.sem, 1)
            pool.wait_ge(*rx_0(it, 0))
            nc.gpsimd.tensor_tensor(rx[:], rx0[:], mhalf[:, 0:4], ALU.pow).then_inc(rx_f.sem, 1)

        @block.gpsimd
        def _(pool):
            for ev in (w_lo, sk_0, sk_f, odb_0, u_in, u_out, u_add, win_f, ftab_f, gb_in,
                       sdec_f, o_rt, ry_f):
                pool.nop().then_inc(ev.sem, ev.per)
            nc.gpsimd.memset(half[:], 0.5)
            nc.gpsimd.memset(mhalf[:], -0.5).then_inc(s_modc, 1)
            pool.wait_ge(s_modc, 1)
            front_rx(pool, PROLOGUE)
            pool.wait_ge(*done("act", "x_sq"))
            nc.gpsimd.tensor_scalar(s8[:, 1:2], s8[:, 0:1], 1.0 / DM, EPS, ALU.mult, ALU.add).then_inc(*step("pool", "rx0"))
            pool.wait_ge(*done("pool", "rx0"))
            nc.gpsimd.tensor_tensor(s8[:, 2:3], s8[:, 1:2], mhalf[0:NS, 0:1], ALU.pow).then_inc(*step("pool", "rx"))
            for t in range(2):
                pool.wait_ge(*w_hi(0, t))
                nc.gpsimd.tensor_tensor(wlo[:, t], wraw[:, t], whi[:, t].bitcast(F32), ALU.subtract).then_inc(w_lo.sem, 1)

            def split_lo(it, t):
                pool.wait_ge(*w_hi(it + (t + 1) // NW, (t + 1) % NW))
                nc.gpsimd.tensor_tensor(wlo[:, (t + 1) % 2], wraw[:, (t + 1) % 2], whi[:, (t + 1) % 2].bitcast(F32),
                                        ALU.subtract).then_inc(w_lo.sem, 1)

            def u_tile(it, t):
                g = t - UA
                u = ubuf[:, g % 2]
                pool.wait_ge(*pooled_f(it, g - 2))
                pool.wait_ge(*u_out(it, g - 2))
                held(pool)
                nc.gpsimd.tensor_copy(u[:, 0:PB], uhist[:, g]).then_inc(u_in.sem, 1)
                pool.wait_ge(*u_in(it, g))
                pool.wait_ge(*u_f(it, g))
                held(pool)
                nc.gpsimd.tensor_copy(uhist[:, g], u[:, BT:BT + PB]).then_inc(u_out.sem, 1)
                src, base = u, g * (g + 1) // 2
                for s in range(g + 1):
                    dst = win[:, (g + g - s) % 2]
                    lo = (2 << s) - 1
                    if s:
                        pool.wait_ge(*u_add(it, base + s - 1))
                    elif g:
                        pool.wait_ge(*u_add(it, base - 1))
                    if s == 0 or s == 1:
                        pool.wait_ge(*pooled_f(it, g - 1))
                        pool.wait_ge(*pooled_f(it, g - 2))
                        pool.wait_ge(*win_f(it, g - 1))
                    nc.gpsimd.tensor_tensor(dst[:, lo:], src[:, lo:], src[:, lo - (1 << s):BT + PB - (1 << s)],
                                            ALU.add).then_inc(u_add.sem, 1)
                    src = dst
                pool.wait_ge(*u_add(it, base + g))
                pool.wait_ge(*ftab_f(it, -1))
                nc.gpsimd.tensor_tensor(src[:, PB:PB + 16], src[:, PB:PB + 16], ftab[:, g], ALU.mult).then_inc(win_f.sem, 1)

            def repeat_g(it, c):
                pool.wait_ge(*job["gb"](it, c - 1))
                pool.wait_ge(*g_g(it, 0))
                held(pool)
                nc.gpsimd.tensor_copy(gb4[:], bc(gg[:, c])).then_inc(gb_in.sem, 1)

            pool.wait_ge(s_prm2, 160)
            pool.wait_ge(s_const, 64)
            pool.wait_ge(s_pre, 1)

            def block_of(it, last=False):
                for t in range(NQ):
                    if t:
                        split_lo(it, t)
                repeat_g(it, 0)
                pool.wait_ge(*ss_ev(it, 7))
                pool.wait_ge(*sk_f(it, -1))
                held(pool)
                nc.gpsimd.tensor_scalar(sk0[:], ssb[:, 0:4].rearrange("p h c -> p c h"), EPS, None, ALU.add).then_inc(sk_0.sem, 1)
                pool.wait_ge(*sk_0(it, 0))
                pool.wait_ge(*rv_f(it, -1))
                nc.gpsimd.tensor_tensor(sk[:].rearrange("p c h -> p (c h)"), sk0[:].rearrange("p c h -> p (c h)"), half[:], ALU.pow).then_inc(sk_f.sem, 1)
                pool.wait_ge(*o_n(it, -1))
                held(pool)
                nc.gpsimd.tensor_scalar(odb[:], ssb[:, 4:8].rearrange("p h c -> p c h"), EPS, EPS * P, ALU.add, ALU.mult).then_inc(odb_0.sem, 1)
                for slot, (c, p, sc, q, parts) in enumerate(PLAN):
                    norm, step_ = norm_step(slot)
                    if c is not None and c < NC - 1 and p == 3:
                        repeat_g(it, c + 1)
                    for n in parts:
                        if n <= PARTS and n % 8 == 0:
                            split_lo(it, NQ + n // 8)
                        if n % 8 == 7 and UA <= NQ + n // 8 < OUT:
                            u_tile(it, NQ + n // 8)
                    if sc is not None and q == 0:
                        pool.wait_ge(*g_eg(it, 0))
                        pool.wait_ge(*s_f(it, sc - 1))
                        nc.gpsimd.tensor_tensor(sdec[:], st[:], bc(eg[:, 1, sc]), ALU.mult).then_inc(sdec_f.sem, 1)
                    if norm is not None and step_ == 1:
                        pool.wait_ge(*o_n(it, norm))
                        nc.gpsimd.tensor_tensor(on[:], on0[:], mhalf[:, 0:H], ALU.pow).then_inc(o_rt.sem, 1)
                    if slot == FRONT and not last:
                        front_rx(pool, it)
                    if last and slot == SAMPLE_SLOT["root"]:
                        pool.wait_ge(*silu(it, NQ - 1))
                        nc.gpsimd.memset(spw[:], -0.5).then_inc(*step("pool", "half"))
                        pool.wait_ge(*done("dve", "sst1"))
                        pool.wait_ge(*done("pool", "half"))
                        nc.gpsimd.tensor_tensor(rk[:, 1].rearrange("p h s -> p (h s)"), sst[:, 0:4].rearrange("p h s -> p (h s)"),
                                                spw[:], ALU.pow).then_inc(*step("pool", "rk"))
                    if last and slot == SAMPLE_SLOT["mean"]:
                        pool.wait_ge(*done("dve", "ms2"))
                        nc.gpsimd.tensor_tensor(rk[:, 1].rearrange("p h s -> p (h s)"), rk[:, 0].rearrange("p h s -> p (h s)"),
                                                spw[:], ALU.pow).then_inc(*step("pool", "rstd"))
                for m in range(1, 7 if last else 8):
                    split_lo(it, OUT + m)
                if not last:
                    split_lo(it, NW)
                pool.wait_ge(*ry_0(it, 0))
                pool.wait_ge(*yr_f(it, -1))
                nc.gpsimd.tensor_tensor(ry[:], ry0[:], mhalf[:, 0:4], ALU.pow).then_inc(ry_f.sem, 1)
                pool.wait_ge(*win_f(it, NG - 1))
                held(pool)
                nc.gpsimd.memset(ftab[:], 1.0).then_inc(ftab_f.sem, 1)


            with pool.Fori(0, NB - 1) as it:
                block_of(it)
            block_of(LAST, last=True)
            pool.wait_ge(*done("act", "y_sq"))
            nc.gpsimd.tensor_scalar(s8[:, 5:6], s8[:, 4:5], 1.0 / DM, EPS, ALU.mult, ALU.add).then_inc(*step("pool", "ry0"))
            pool.wait_ge(*done("pool", "ry0"))
            nc.gpsimd.tensor_tensor(s8[:, 6:7], s8[:, 5:6], mhalf[0:NS, 0:1], ALU.pow).then_inc(*step("pool", "ry"))

        def front_pe(pe, it, m):
            bank_free(pe, it, "xf", m, (xn, 3))
            for t in range(4):
                last = nc.tensor.transpose(bank("xf", m)[:, t * P:(t + 1) * P], xb[:, t, m * P:(m + 1) * P], ident[:])
            last.then_inc(job["xf"].sem, 1)

        @block.tensor
        def _(pe):
            for ev in [proj, outp] + [e for k, e in job.items() if k != "xf"]:
                pe.nop().then_inc(ev.sem, ev.per)
            pe.wait_ge(s_const, 64)
            pe.wait_ge(s_pre, 1)
            pe.wait_ge(s_cact, 1)
            def turn_rows(j, dst, col):
                pe.wait_ge(s_rows, j + 1)
                for i in range(4):
                    last = nc.tensor.transpose(dst[:, col + 9 * i:col + 9 * (i + 1)], rows9[j][:, i * P:(i + 1) * P],
                                               ident[0:1 + NS, 0:1 + NS])
                return last

            for j in range(6):
                pe.wait_ge(ada_in[j], 16)
                if j >= 2:
                    pe.wait_ge(s_rows, j - 1)
                for k in range(KT):
                    last = nc.tensor.matmul(acc[j % 2][0:1 + NS, :], cin[:, k, :], wada[j][:, k], start=(k == 0),
                                            stop=(k == KT - 1))
                last.then_inc(s_mod, 1)
                if 1 <= j <= 3:
                    turn_rows(j - 1, spare[0], (j - 1) * 36)
                if j == 2:
                    for m in range(3):
                        front_pe(pe, PROLOGUE, m)
                if j == 3:
                    turn_rows(3, spare[0], 108).then_inc(s_tr, 1)
                    pe.wait_ge(*done("dve", "xn"))
                    for k in range(KT):
                        last = nc.tensor.transpose(spare[2][:, k * NS:(k + 1) * NS], xrow[:, k * P:(k + 1) * P], ident[0:NS, 0:NS])
                    last.then_inc(*step("pe", "hs"))
                    for m in range(3, 5):
                        front_pe(pe, PROLOGUE, m)
                if j == 4:
                    for m in range(5, 8):
                        front_pe(pe, PROLOGUE, m)
            turn_rows(4, spare[1], 0)
            turn_rows(5, spare[1], 36).then_inc(s_tr, 1)
            pe.wait_ge(s_pre, 2)
            pe.wait_ge(*done("dve", "h"))
            for m in range(2):
                pe.wait_ge(s_trc, 2 * m + 2)
                nc.tensor.matmul((spare[2], spare[0])[m][:], ones[0:1, :], grow[0:1, m * 512:(m + 1) * 512], start=True,
                                 stop=True).then_inc(s_row, 1)
            pe.wait_ge(s_rowc, 2)
            pe.wait_ge(*done("dve", "h"))
            for t in range(2):
                pe.wait_ge(*w_in[t](0, 0))
                for k in range(KT):
                    last = nc.tensor.matmul(acc[0][:, t * NS:(t + 1) * NS], wraw[:, t, k], hs[:, k], start=(k == 0),
                                            stop=(k == KT - 1))
                last.then_inc(*step("pe", f"sp{t}"))
            pe.wait_ge(*done("dve", "pj01"))

            def tile(it, t, part=None):
                hi, lo = hhi, hlo
                ks = range(KT) if part is None else range(part, part + 1)
                for k in ks:
                    if k == 0:
                        pe.wait_ge(*w_lo(it, t))
                        tile_reader(pe, it, t)
                    if t == 0:
                        pe.wait_ge(*h_lo(it, k - 8))
                    nc.tensor.matmul(acc[t % 2][:], whi[:, t % 2, k], hi[:, k], start=(k == 0), stop=False)
                    nc.tensor.matmul(acc[t % 2][:], whi[:, t % 2, k], lo[:, k], start=False, stop=False)
                    last = nc.tensor.matmul(acc[t % 2][:], wlo[:, t % 2, k], hi[:, k], start=False, stop=(k == KT - 1))
                if ks[-1] == KT - 1:
                    last.then_inc(proj.sem, 1)

            def out_tile(it, m):
                hf, kp = divmod(m, 4)
                t = OUT + m
                pe.wait_ge(*w_lo(it, t))
                for j in range(2):
                    k = 2 * kp + j
                    if hf == 0:
                        pe.wait_ge(*ylo_f(it, k if k < 4 else 5))
                    w_hi_k, w_lo_k = (w[:, t % 2].rearrange("p k c -> p (k c)")[:, j * BT:(j + 1) * BT] for w in (whi, wlo))
                    for tt in range(4):
                        cols = slice(tt * P, (tt + 1) * P)
                        if k == 0:
                            if tt >= 2:
                                bank_free(pe, it, "out", 2 * hf + tt - 2)
                            elif hf:
                                pe.wait_ge(*ytok_f(it, tt))
                            else:
                                tile_reader(pe, it, t + tt)
                        o = out_bank(hf, tt)[:]
                        nc.tensor.matmul(o, yhi[:, k, cols], w_hi_k, start=(k == 0), stop=False)
                        nc.tensor.matmul(o, ylo[:, k, cols], w_hi_k, start=False, stop=False)
                        last = nc.tensor.matmul(o, yhi[:, k, cols], w_lo_k, start=False, stop=(k == KT - 1))
                        if k == KT - 1 and tt < 3:
                            last.then_inc(outp.sem, 1)
                last.then_inc(proj.sem, 1)

            def four(it, kind, i, left, right, *needs, n=C, rows=slice(0, P)):
                bank_free(pe, it, kind, i, *needs)
                if rows != slice(0, P):
                    pe.nop().then_inc(pe_held, 1)
                for h in range(H):
                    last = nc.tensor.matmul(bank(kind, i)[rows, h * n:(h + 1) * n], left(h), right(h), start=True, stop=True)
                last.then_inc(job[kind].sem, 1)

            def turn(it, kind, n, what, *needs):
                bank_free(pe, it, kind, n, *needs)
                for h in range(H):
                    last = nc.tensor.transpose(bank(kind, n)[:, h * C:(h + 1) * C], what(h), ident[:])
                last.then_inc(job[kind].sem, 1)

            def sample_tile(it, t):
                pe.wait_ge(*w_lo(it, t))
                bank_free(pe, it, "sp", t)
                for k in range(KT):
                    last = nc.tensor.matmul(bank("sp", t)[:, 0:NS], wraw[:, t % 2, k], hs[:, k], start=(k == 0), stop=(k == KT - 1))
                last.then_inc(*step("pe", f"sp{t}"))

            def sample_out(it, m):
                hf, kp = divmod(m, 4)
                t = OUT + m
                pe.wait_ge(*w_lo(it, t))
                pe.wait_ge(*done("dve", "yma"))
                pe.wait_ge(*done("dve", "ymb"))
                if kp == 0:
                    bank_free(pe, it, "so", hf)
                for j in range(2):
                    k = 2 * kp + j
                    last = nc.tensor.matmul(bank("so", hf)[0:NS, :], ym[:, k],
                                            wraw[:, t % 2].rearrange("p k c -> p (k c)")[:, j * BT:(j + 1) * BT],
                                            start=(k == 0), stop=(k == KT - 1))
                last.then_inc(*step("pe", f"sp{t}"))

            def sample_slot(it, slot):
                if slot == SAMPLE_SLOT["square"]:
                    bank_free(pe, it, "s2")
                    pe.wait_ge(*done("dve", "sq1"))
                    nc.tensor.matmul(bank("s2")[:, 0:96], ones[:], sqs[:].rearrange("p t s -> p (t s)"), start=True,
                                     stop=True).then_inc(*step("pe", "s20"))
                    bank_free(pe, it, "kv")
                    pe.wait_ge(*done("dve", "kq1"))
                    pe.wait_ge(sm_ssm, 16)
                    for s in range(NS):
                        for h in range(H):
                            col = 2 * (s * H + h)
                            last = nc.tensor.matmul(bank("kv")[:, col:col + 2], ssm[:, s, h], kq[:, s, h], start=True, stop=True)
                    last.then_inc(*step("pe", "kv0"))
                if slot == SAMPLE_SLOT["rows"]:
                    bank_free(pe, it, "dt")
                    pe.wait_ge(*done("dve", "d5"))
                    nc.tensor.transpose(bank("dt")[0:32, 0:P], kq[:, :, :, 0].rearrange("p s h -> p (s h)"), ident[:])
                    nc.tensor.transpose(bank("dt")[0:32, P:2 * P], dl[:, 2].rearrange("p h s -> p (h s)"), ident[:]
                                        ).then_inc(*step("pe", "dt0"))
                    bank_free(pe, it, "son")
                    pe.wait_ge(*done("dve", "o2"))
                    nc.tensor.matmul(bank("son")[:, 0:32], ones[:], dl[:, 3].rearrange("p h s -> p (h s)"), start=True,
                                     stop=True).then_inc(*step("pe", "son0"))
                if slot == SAMPLE_SLOT["pooled"]:
                    bank_free(pe, it, "spl")
                    pe.wait_ge(*done("dve", "pl8"))
                    for g in range(NG):
                        last = nc.tensor.matmul(bank("spl")[:, g * NS:(g + 1) * NS], poolw[:, g], pls[:, g], start=True, stop=True)
                    last.then_inc(*step("pe", "spl0"))

            def sample_state(it, m):
                bank_free(pe, it, "sop", m)
                pe.wait_ge(*done("dve", "krow"))
                for h in range(H):
                    last = nc.tensor.matmul(bank("sop", m)[:, h * P:(h + 1) * P], krow[:, m * H + h], drow[:, 1], start=True,
                                            stop=True)
                last.then_inc(*step("pe", f"sop{m}"))

            def sample_rows(it, kind, what):
                for m in range(8):
                    if m % 4 == 0:
                        bank_free(pe, it, kind, m // 4)
                    last = nc.tensor.transpose(bank(kind, m // 4)[0:NS, (m % 4) * P:(m % 4 + 1) * P], what(m), ident[:])
                    if m % 4 == 3:
                        last.then_inc(*step("pe", f"{kind}{m // 4}"))

            def block_of(it, last=False):
                for t in range(NQ):
                    if last and t >= 2:
                        sample_tile(it, t)
                    tile(it, t)
                    if t == GATES:
                        bank_free(pe, it, "gates")
                        for k in range(KT):
                            nc.tensor.matmul(bank("gates")[0:8, :], wgh[:, k], hhi[:, k], start=(k == 0), stop=False)
                            nc.tensor.matmul(bank("gates")[0:8, :], wgh[:, k], hlo[:, k], start=False, stop=False)
                            mm = nc.tensor.matmul(bank("gates")[0:8, :], wgl[:, k], hhi[:, k], start=False,
                                                    stop=(k == KT - 1))
                        mm.then_inc(job["gates"].sem, 1)
                    if t == GATES + 1:
                        bank_free(pe, it, "gt", 0, (g_c, 0))
                        pe.nop().then_inc(pe_held, 1)
                        for c in range(NC):
                            mm = nc.tensor.transpose(bank("gt")[:, c * 8:(c + 1) * 8], gsb[:, c * C:(c + 1) * C], ident[0:8, 0:8])
                        mm.then_inc(job["gt"].sem, 1)
                    if t == GATES + 5:
                        bank_free(pe, it, "gc", 0, (g_g, 0))
                        g16 = gg[:].rearrange("p c h -> p (c h)")
                        nc.tensor.matmul(bank("gc")[:, 0:16], upper[:], g16, start=True, stop=True)
                        nc.tensor.matmul(bank("gc")[:, 16:32], ones[:], g16, start=True, stop=True).then_inc(job["gc"].sem, 1)
                    if SUMS <= t < SUMS + 8:
                        bank_free(pe, it, "ss", t - SUMS, (sq, t - SUMS))
                        for c in range(NC):
                            mm = nc.tensor.matmul(bank("ss", t - SUMS)[:, c:c + 1], tmpa[:, (t - SUMS) % 2, c * C:(c + 1) * C],
                                                    ones[:, 0:1], start=True, stop=True)
                        mm.then_inc(job["ss"].sem, 1)
                    if last and t == 6:
                        bank_free(pe, it, "sg")
                        for k in range(KT):
                            mm = nc.tensor.matmul(bank("sg")[0:NS, 0:8], hs[:, k], wgr[:, k], start=(k == 0), stop=(k == KT - 1))
                        mm.then_inc(*step("pe", "sg0"))
                if last:
                    bank_free(pe, it, "sb")
                    pe.wait_ge(*done("dve", "g_d1"))
                    nc.tensor.matmul(bank("sb")[:, 0:64], ones[0:NS, :], gdg[:].rearrange("p s e -> p (s e)"), start=True,
                                     stop=True).then_inc(*step("pe", "sb0"))
                for slot, (c, p, sc, q, parts) in enumerate(PLAN):
                    norm, step_ = norm_step(slot)
                    for n in parts:
                        if last and n < PARTS and n % 8 == 0:
                            sample_tile(it, NQ + n // 8)
                        if n < PARTS:
                            tile(it, NQ + n // 8, n % 8)
                        g = pool_after(n)
                        if g is not None:
                            bank_free(pe, it, "pool", g, (pooled_f, g))
                            nc.tensor.matmul(bank("pool", g)[:], poolw[:, g], pooled[:, g % 2], start=True,
                                             stop=True).then_inc(job["pool"].sem, 1)
                    if c is not None:
                        s = slice(c * C, (c + 1) * C)
                        if p == 0:
                            turn(it, "kt", c, lambda h: cq[:, h, s], (silu, 3))
                            turn(it, "vt", c, lambda h: cq[:, 8 + h, s], (silu, NQ - 1))
                            four(it, "gb", c, lambda h: gb4[:, h], lambda h: upper[:], (gb_in, c))
                        elif p == 1:
                            four(it, "kk", c, lambda h: cq[:, h, s], lambda h: cq[:, h, s])
                            four(it, "qk", c, lambda h: cq[:, h, s], lambda h: cq[:, 4 + h, s])
                        elif p == 2:
                            turn(it, "xt", c, lambda h: yv[:, c % 2, h], (y_1, c))
                        elif p % 2:
                            i = c * NL + (p - 3) // 2
                            x_ready = (x_0, c) if p == 3 else (x_l, c * (NL - 1) + (p - 3) // 2 - 1)
                            sz = LEVELS[(p - 3) // 2]
                            if sz < C // 2:
                                four(it, "w", i, lambda h: lt[:, h], lambda h: head_blocks(xv[:, h], sz, 0), x_ready, n=C // 2)
                            else:
                                four(it, "w", i, lambda h: lt[0:sz, h, sz:], lambda h: xv[0:sz, h, 0:sz], x_ready, n=sz,
                                     rows=slice(sz, P))
                        else:
                            lv = (p - 4) // 2
                            sz = LEVELS[lv]
                            i = c * NL + lv
                            ready = [(w_f, i)] + ([(y_l, i - 1)] if lv else [])
                            if lv < NL - 1:
                                four(it, "xx", c * (NL - 1) + lv, lambda h: yv[:, c % 2, h],
                                     lambda h: head_blocks(wb[:, h], sz, 0), *ready, n=C // 2)
                            if sz < C // 2:
                                four(it, "yy", i, lambda h: wb[:, h], lambda h: head_blocks(yv[:, c % 2, h], sz, 1), *ready,
                                     n=C // 2)
                            else:
                                four(it, "yy", i, lambda h: wb[sz:, h, 0:sz], lambda h: yv[sz:, c % 2, h, sz:], *ready, n=sz,
                                     rows=slice(0, sz))
                    if sc is not None:
                        s = slice(sc * C, (sc + 1) * C)
                        if q == 0:
                            four(it, "ks", sc, lambda h: cq[:, h, s], lambda h: st[:, h], (s_f, sc - 1))
                            four(it, "qs", sc, lambda h: cq[:, 4 + h, s], lambda h: st[:, h])
                        elif q == 1:
                            four(it, "u", sc, lambda h: yv[:, sc % 2, h], lambda h: rv[:, sc % 2, h],
                                 (r_f, sc), (y_l, sc * NL + NL - 1))
                        elif q == 2:
                            four(it, "mv", sc, lambda h: mtb[:, sc % 2, h], lambda h: ub[:, h], (u_c, sc), (mt_f, sc))
                            four(it, "su", sc, lambda h: ktok[:, sc % 2, h], lambda h: ve[:, h], (ve_f, sc), (kt_f, sc))
                            if sc == NC - 1:
                                if last:
                                    sample_out(it, 0)
                                out_tile(it, 0)
                        else:
                            turn(it, "ot", sc, lambda h: ao[:, h], (o_s, sc))
                            if sc == NC - 1:
                                if last:
                                    sample_out(it, 1)
                                out_tile(it, 1)
                    if last:
                        sample_slot(it, slot)
                for m in range(8):
                    if not last:
                        front_pe(pe, it, m)
                    if last and m >= 2:
                        sample_out(it, m)
                    if m >= 2:
                        out_tile(it, m)
                    if last:
                        sample_state(it, m)
                if last:
                    sample_rows(it, "sgt", lambda e: mod[:, 16 + e, 1:1 + NS])

            with pe.Fori(0, NB - 1) as it:
                block_of(it)
            block_of(LAST, last=True)


def layouts(i):
    import numpy as np

    f = lambda n: np.asarray(i[n])

    def tiles(w):
        return w.reshape(KT, P, -1, P).transpose(2, 1, 0, 3)

    w_in = f("w_in")[0]
    u, za, q, k, v, zb = (w_in[:, s:s + 512] for s in range(0, 3072, 512))
    w_out = f("w_out")[0].reshape(4, 2, P, 2, BT).transpose(3, 0, 2, 1, 4).reshape(8, P, KT, P)
    x = f("x_prompt")[0].reshape(NB, 4, P, DM).transpose(0, 2, 1, 3)
    perm = lambda w: np.concatenate([w[..., 512:1024], w[..., 0:512], w[..., 1024:1536]], -1)
    j = np.arange(P)
    lm = []
    for s in (1,) + LEVELS:
        lm.append((j[:, None] // (2 * s) == j[None, :] // (2 * s)) & (j[:, None] // s < j[None, :] // s))
    lm[1:] = [m.T for m in lm[1:]]
    cnt = np.minimum(np.arange(16)[None] + 1, 2 << np.arange(NG)[:, None])
    ftab = (2 << np.arange(NG))[:, None] / cnt
    return {
        "x": x,
        "c_all": np.concatenate([f("c_prompt"), f("c_sample")]).T.reshape(KT, P, 1 + NS).transpose(1, 0, 2),
        "w": np.concatenate([tiles(np.concatenate([k, q, v, zb, za, u], 1)), w_out]),
        "w_gate": w_in[:, 3072:].reshape(KT, P, 8).transpose(1, 0, 2),
        "w_ada": f("w_ada")[0].reshape(KT, P, 6, BT).transpose(2, 1, 0, 3),
        "b_ada": f("b_ada")[0].reshape(24, P).T,
        "b_gate": f("b_ada")[:, 2 * DM:],
        "pre_w": f("pre_norm_w")[0].reshape(KT, P).T,
        "post_w": f("post_norm_w"),
        "conv_w": perm(f("conv_w")[0]).reshape(CK, NQ, P).transpose(2, 1, 0),
        "pool_w": f("pool_w")[0].transpose(1, 0, 2),
        "pool_scale": f("pool_scale")[0].reshape(NG, P).T,
        "a_log": f("a_log"), "dt_bias": f("dt_bias"),
        "o_norm": f("o_norm_w")[0].reshape(P, 1),
        "ident": np.eye(P, dtype=np.float32),
        "upper": (j[:, None] <= j[None, :]).astype(np.float32),
        "dmask": np.where(j[:, None] <= j[None, :], 0.0, -30000.0).astype(np.float32),
        "lmask": np.stack(lm, 1).astype(np.float32),
        "ftab": np.broadcast_to(ftab.astype(np.float32), (P, NG, 16)),
        "xs": f("x_sample").reshape(NS, DM),
        "s_conv": perm(f("state_conv")[0]).reshape(NS, CK - 1, NQ, P).transpose(3, 1, 2, 0),
        "s_pool": f("state_pool")[0].reshape(NS, PB, NG, P).transpose(3, 1, 2, 0),
        "s_ssm": f("state_ssm")[0].transpose(2, 0, 1, 3),
    }


OUTS = {"y": (NB, 4, P, DM), "o_pool": (P, NG, PB), "o_conv": (P, NQ, CK - 1), "o_ssm": (P, H, P),
        "ys": (NS, DM), "o_spool": (PB, P, NG, NS), "o_sconv": (CK - 1, P, NQ, NS), "o_sssm": (P, NS, H, P)}


def gather(r):
    import numpy as np

    def unperm(h):
        return np.concatenate([h[4:8], h[0:4], h[8:12]])

    return (
        r["y"].transpose(0, 1, 2, 3).reshape(1, SEQ, DM),
        r["ys"].reshape(NS, 1, DM),
        r["o_pool"].transpose(2, 1, 0).reshape(1, 1, PB, NG * P),
        unperm(r["o_conv"].transpose(1, 2, 0)).transpose(1, 0, 2).reshape(1, 1, CK - 1, NQ * P),
        r["o_ssm"].transpose(1, 0, 2)[None, None],
        r["o_spool"].transpose(3, 0, 2, 1).reshape(1, NS, PB, NG * P),
        unperm(r["o_sconv"].transpose(2, 3, 0, 1)).transpose(1, 2, 0, 3).reshape(1, NS, CK - 1, NQ * P),
        r["o_sssm"].transpose(1, 2, 0, 3)[None],
    )


def kernel(**inputs):
    import numpy as _np
    import concourse.bacc as _bacc
    from concourse.bass_utils import run_bass_kernel_spmd as _run

    nc = _bacc.Bacc("TRN2", target_bir_lowering=False, num_devices=1)
    arrays, aps = {}, {}
    for name, value in layouts(inputs).items():
        arrays[f"in_{name}"] = _np.ascontiguousarray(value)
        aps[name] = nc.dram_tensor(f"in_{name}", value.shape, F32, kind="ExternalInput").ap()
    for name, shape in OUTS.items():
        aps[name] = nc.dram_tensor(f"out_{name}", shape, F32, kind="ExternalOutput").ap()
    layer_kernel(nc, aps)
    r = _run(nc, [arrays], core_ids=[0]).results[0]
    return gather({name: r[f"out_{name}"] for name in OUTS})
```
